# Optimizing a Trainium2 kernel written in Bass

```python
import jax, jax.numpy as jnp
from jax import lax
import numpy as np

"""One inference step (prompt group + sample group, shared weights) of a 2-layer hybrid decoder.

Each layer: x += W_o( sig(gA) * RetentionBranch(h) + sig(gB) * RGLRUBranch(h) ),  h = RMSNorm(x)
            x += SwiGLU(RMSNorm(x));  final RMSNorm after the last layer.
Both branches read ONE combined input projection of h whose columns are partitioned into
[q | k | v | retention swish gate | lru x-branch | lru gelu-branch | merge gate A | merge gate B].

Inputs:
  x_prompt   (BATCH, SEQ, D_MODEL)        positions 0..SEQ-1, empty initial state
  x_sample   (DEC_BATCH, DEC_SEQ, D_MODEL) positions PAST_LEN..PAST_LEN+DEC_SEQ-1
  state_ret  (DEPTH, DEC_BATCH, RET_HEADS, RET_DK, RET_DV)  retention recurrent matrix state
  state_lru  (DEPTH, DEC_BATCH, LRU_WIDTH)                  RG-LRU hidden state
  state_conv (DEPTH, DEC_BATCH, CONV_W-1, LRU_WIDTH)        last 3 pre-conv rows of the lru x-branch
  + weights.
Output tuple:
  (y_prompt (BATCH,SEQ,D_MODEL), y_sample (DEC_BATCH,DEC_SEQ,D_MODEL),
   new_ret_prompt (DEPTH,BATCH,H,DK,DV), new_lru_prompt (DEPTH,BATCH,LRU_WIDTH), new_conv_prompt (DEPTH,BATCH,CONV_W-1,LRU_WIDTH),
   new_ret_sample (DEPTH,DEC_BATCH,H,DK,DV), new_lru_sample (DEPTH,DEC_BATCH,LRU_WIDTH), new_conv_sample (DEPTH,DEC_BATCH,CONV_W-1,LRU_WIDTH))
"""

D_MODEL = 1024
BATCH = 1
SEQ = 512
DEPTH = 2
DEC_BATCH = 8
DEC_SEQ = 1
PAST_LEN = 4096
PAGE_SIZE = 128

RET_HEADS = 4
RET_DK = 256
RET_DV = 512
RET_QK = RET_HEADS * RET_DK
RET_V = RET_HEADS * RET_DV
RET_CHUNK = 128
ROPE_THETA = 10000.0
LRU_WIDTH = 1280
LRU_BLOCKS = 16
LRU_BLOCK = LRU_WIDTH // LRU_BLOCKS
LRU_C = 8.0
CONV_W = 4
D_FF = -(-8 * D_MODEL // (3 * 256)) * 256
EPS = 1e-6

IN_SIZES = (RET_QK, RET_QK, RET_V, RET_V, LRU_WIDTH, LRU_WIDTH, D_MODEL, D_MODEL)
IN_TOTAL = sum(IN_SIZES)
IN_SPLITS = tuple(int(s) for s in np.cumsum(IN_SIZES)[:-1])

kernel_name = "retention_rglru_gated_hybrid_step"

def rmsnorm(x, g):
    xf = x.astype(jnp.float32)
    y = xf * lax.rsqrt(jnp.mean(xf * xf, axis=-1, keepdims=True) + EPS)
    return (y * g.astype(jnp.float32)).astype(x.dtype)

def rope(x, pos):
    half = x.shape[-1] // 2
    freqs = ROPE_THETA ** (-jnp.arange(half, dtype=jnp.float32) / half)
    ang = pos[:, None] * freqs[None, :]
    cos = jnp.cos(ang)[None, :, None, :]
    sin = jnp.sin(ang)[None, :, None, :]
    x1, x2 = x[..., :half], x[..., half:]
    return jnp.concatenate([x1 * cos - x2 * sin, x1 * sin + x2 * cos], axis=-1)

def retention(q, k, v, S0):
    B, L, H, _ = q.shape
    C = RET_CHUNK if L % RET_CHUNK == 0 else L
    N = L // C
    log_g = jnp.log(1.0 - 2.0 ** (-5.0 - jnp.arange(H, dtype=jnp.float32)))
    idx = jnp.arange(C, dtype=jnp.float32)
    diff = idx[:, None] - idx[None, :]
    decay = jnp.where(diff >= 0, jnp.exp(log_g[:, None, None] * jnp.maximum(diff, 0.0)), 0.0)
    q_dec = jnp.exp(log_g[:, None] * (idx[None, :] + 1.0))
    k_dec = jnp.exp(log_g[:, None] * (C - 1.0 - idx[None, :]))
    chunk_dec = jnp.exp(log_g * C)

    def to_chunks(t):
        return t.reshape(B, N, C, H, t.shape[-1]).transpose(1, 0, 3, 2, 4)

    def step(S, inp):
        qc, kc, vc = inp
        scores = jnp.einsum('bhid,bhjd->bhij', qc, kc) * decay[None]
        inner = jnp.einsum('bhij,bhje->bhie', scores, vc)
        cross = jnp.einsum('bhid,bhde->bhie', qc, S) * q_dec[None, :, :, None]
        S_new = S * chunk_dec[None, :, None, None] + jnp.einsum(
            'bhjd,bhje->bhde', kc * k_dec[None, :, :, None], vc)
        return S_new, inner + cross

    S, o = lax.scan(step, S0, (to_chunks(q), to_chunks(k), to_chunks(v)))
    o = o.transpose(1, 0, 3, 2, 4).reshape(B, L, H, v.shape[-1])
    return o, S

def causal_conv(x, buf, w, b):
    L = x.shape[1]
    xx = jnp.concatenate([buf.astype(x.dtype), x], axis=1)
    y = b[None, None, :]
    for j in range(CONV_W):
        y = y + xx[:, j:j + L] * w[j][None, None, :]
    return y, xx[:, -(CONV_W - 1):]

def rg_lru(xc, w_a, b_a, w_x, b_x, lam, h0):
    B, L, W = xc.shape
    xf = xc.astype(jnp.float32)
    xb = xf.reshape(B, L, LRU_BLOCKS, LRU_BLOCK)
    r = jax.nn.sigmoid(jnp.einsum('blnc,ncd->blnd', xb, w_a.astype(jnp.float32)).reshape(B, L, W) + b_a)
    i = jax.nn.sigmoid(jnp.einsum('blnc,ncd->blnd', xb, w_x.astype(jnp.float32)).reshape(B, L, W) + b_x)
    log_a = -LRU_C * r * jax.nn.softplus(-lam.astype(jnp.float32))
    a = jnp.exp(log_a)
    u = jnp.sqrt(-jnp.expm1(2.0 * log_a)) * (i * xf)
    u = u.at[:, 0].add(a[:, 0] * h0.astype(jnp.float32))

    def comb(l, rr):
        return (l[0] * rr[0], rr[0] * l[1] + rr[1])

    _, h = lax.associative_scan(comb, (a, u), axis=1)
    return h, h[:, -1]

def layer(x, pos, S_ret, h_lru, conv_buf, w_in, norm_mix, gn_gain, w_ret_out, conv_w, conv_b,
          lru_wa, lru_ba, lru_wx, lru_bx, lru_lambda, w_lru_out, b_gate, w_o, norm_ffn,
          w_gate_up, w_down):
    B, L, _ = x.shape
    h = rmsnorm(x, norm_mix)
    proj = h @ w_in
    q, k, v, g_ret, x_lru, y_lru, g_a, g_b = jnp.split(proj, IN_SPLITS, axis=-1)
    qf = rope(q.reshape(B, L, RET_HEADS, RET_DK).astype(jnp.float32), pos)
    kf = rope(k.reshape(B, L, RET_HEADS, RET_DK).astype(jnp.float32), pos) * (RET_DK ** -0.5)
    vf = v.reshape(B, L, RET_HEADS, RET_DV).astype(jnp.float32)
    o, S_new = retention(qf, kf, vf, S_ret.astype(jnp.float32))
    mu = jnp.mean(o, axis=-1, keepdims=True)
    var = jnp.mean(jnp.square(o - mu), axis=-1, keepdims=True)
    o = ((o - mu) * lax.rsqrt(var + EPS)).reshape(B, L, RET_V) * gn_gain.astype(jnp.float32)
    ret_branch = (jax.nn.silu(g_ret) * o.astype(x.dtype)) @ w_ret_out
    xc, new_buf = causal_conv(x_lru, conv_buf, conv_w, conv_b)
    hl, h_last = rg_lru(xc, lru_wa, lru_ba, lru_wx, lru_bx, lru_lambda, h_lru)
    lru_branch = (jax.nn.gelu(y_lru) * hl.astype(x.dtype)) @ w_lru_out
    merged = jax.nn.sigmoid(g_a + b_gate[0]) * ret_branch + jax.nn.sigmoid(g_b + b_gate[1]) * lru_branch
    x = x + merged @ w_o
    h2 = rmsnorm(x, norm_ffn)
    gu = h2 @ w_gate_up
    gt, up = gu[..., :D_FF], gu[..., D_FF:]
    x = x + (jax.nn.silu(gt) * up) @ w_down
    return x, S_new, h_last, new_buf

def trunk(x, pos, S_rets, h_lrus, conv_bufs, w_in, norm_mix, gn_gain, w_ret_out, conv_w, conv_b,
          lru_wa, lru_ba, lru_wx, lru_bx, lru_lambda, w_lru_out, b_gate, w_o, norm_ffn,
          w_gate_up, w_down, norm_final):
    new_S, new_h, new_c = [], [], []
    for l in range(DEPTH):
        x, S, hh, cb = layer(x, pos, S_rets[l], h_lrus[l], conv_bufs[l], w_in[l], norm_mix[l], gn_gain[l],
                             w_ret_out[l], conv_w[l], conv_b[l], lru_wa[l], lru_ba[l], lru_wx[l], lru_bx[l],
                             lru_lambda[l], w_lru_out[l], b_gate[l], w_o[l], norm_ffn[l], w_gate_up[l], w_down[l])
        new_S.append(S)
        new_h.append(hh)
        new_c.append(cb)
    return rmsnorm(x, norm_final), jnp.stack(new_S, 0), jnp.stack(new_h, 0), jnp.stack(new_c, 0)

def setup_inputs(seed: int = 0) -> dict:
    key = jax.random.key(seed)
    ks = jax.random.split(key, 24)
    f32 = jnp.float32

    def nrm(k, shape, s):
        return jax.random.normal(k, shape, f32) * s

    u = jax.random.uniform(ks[15], (DEPTH, LRU_WIDTH), f32, minval=0.9, maxval=0.999)
    a0 = u ** (1.0 / LRU_C)
    lam = jnp.log(a0) - jnp.log1p(-a0)
    return {
        "x_prompt": nrm(ks[0], (BATCH, SEQ, D_MODEL), 1.0),
        "x_sample": nrm(ks[1], (DEC_BATCH, DEC_SEQ, D_MODEL), 1.0),
        "state_ret": nrm(ks[2], (DEPTH, DEC_BATCH, RET_HEADS, RET_DK, RET_DV), 0.5),
        "state_lru": nrm(ks[3], (DEPTH, DEC_BATCH, LRU_WIDTH), 0.5),
        "state_conv": nrm(ks[4], (DEPTH, DEC_BATCH, CONV_W - 1, LRU_WIDTH), 1.0),
        "w_in": nrm(ks[5], (DEPTH, D_MODEL, IN_TOTAL), D_MODEL ** -0.5),
        "norm_mix": 1.0 + nrm(ks[6], (DEPTH, D_MODEL), 0.02),
        "gn_gain": 1.0 + nrm(ks[7], (DEPTH, RET_V), 0.02),
        "w_ret_out": nrm(ks[8], (DEPTH, RET_V, D_MODEL), RET_V ** -0.5),
        "conv_w": nrm(ks[9], (DEPTH, CONV_W, LRU_WIDTH), CONV_W ** -0.5),
        "conv_b": nrm(ks[10], (DEPTH, LRU_WIDTH), 0.02),
        "lru_wa": nrm(ks[11], (DEPTH, LRU_BLOCKS, LRU_BLOCK, LRU_BLOCK), LRU_BLOCK ** -0.5),
        "lru_ba": nrm(ks[12], (DEPTH, LRU_WIDTH), 0.02),
        "lru_wx": nrm(ks[13], (DEPTH, LRU_BLOCKS, LRU_BLOCK, LRU_BLOCK), LRU_BLOCK ** -0.5),
        "lru_bx": nrm(ks[14], (DEPTH, LRU_WIDTH), 0.02),
        "lru_lambda": lam,
        "w_lru_out": nrm(ks[16], (DEPTH, LRU_WIDTH, D_MODEL), LRU_WIDTH ** -0.5),
        "b_gate": nrm(ks[17], (DEPTH, 2, D_MODEL), 0.02),
        "w_o": nrm(ks[18], (DEPTH, D_MODEL, D_MODEL), D_MODEL ** -0.5),
        "norm_ffn": 1.0 + nrm(ks[19], (DEPTH, D_MODEL), 0.02),
        "w_gate_up": nrm(ks[20], (DEPTH, D_MODEL, 2 * D_FF), D_MODEL ** -0.5),
        "w_down": nrm(ks[21], (DEPTH, D_FF, D_MODEL), D_FF ** -0.5),
        "norm_final": 1.0 + nrm(ks[22], (D_MODEL,), 0.02),
    }

def reference(x_prompt, x_sample, state_ret, state_lru, state_conv, w_in, norm_mix, gn_gain, w_ret_out,
              conv_w, conv_b, lru_wa, lru_ba, lru_wx, lru_bx, lru_lambda, w_lru_out, b_gate, w_o,
              norm_ffn, w_gate_up, w_down, norm_final):
    Bp, Lp, _ = x_prompt.shape
    Bs, Ls, _ = x_sample.shape
    pos_p = jnp.arange(Lp, dtype=jnp.float32)
    S0 = jnp.zeros((DEPTH, Bp, RET_HEADS, RET_DK, RET_DV), jnp.float32)
    h0 = jnp.zeros((DEPTH, Bp, LRU_WIDTH), jnp.float32)
    c0 = jnp.zeros((DEPTH, Bp, CONV_W - 1, LRU_WIDTH), x_prompt.dtype)
    y_prompt, ret_p, lru_p, conv_p = trunk(
        x_prompt, pos_p, S0, h0, c0, w_in, norm_mix, gn_gain, w_ret_out, conv_w, conv_b,
        lru_wa, lru_ba, lru_wx, lru_bx, lru_lambda, w_lru_out, b_gate, w_o, norm_ffn,
        w_gate_up, w_down, norm_final)
    pos_s = PAST_LEN + jnp.arange(Ls, dtype=jnp.float32)
    y_sample, ret_s, lru_s, conv_s = trunk(
        x_sample, pos_s, state_ret, state_lru, state_conv, w_in, norm_mix, gn_gain, w_ret_out, conv_w,
        conv_b, lru_wa, lru_ba, lru_wx, lru_bx, lru_lambda, w_lru_out, b_gate, w_o, norm_ffn,
        w_gate_up, w_down, norm_final)
    return (y_prompt, y_sample, ret_p, lru_p, conv_p, ret_s, lru_s, conv_s)


_drawn_inputs = setup_inputs


def setup_inputs(seed=0):
    import zlib

    import numpy as np

    out = dict(_drawn_inputs(seed))
    spreads = {}
    factors = {'gn_gain': 5.757,
     'lru_ba': 8.0,
     'lru_bx': 7.574,
     'b_gate': 8.0,
     'norm_ffn': 2.772,
     'norm_final': 2.784}
    for name, (base, spread) in spreads.items():
        noise = np.random.default_rng([zlib.crc32(name.encode()), seed]).standard_normal(out[name].shape)
        drawn = base * np.exp(spread * noise) if base else spread * noise
        out[name] = __import__('jax').numpy.asarray(drawn.astype(out[name].dtype))
    for name, factor in factors.items():
        out[name] = (out[name] * factor).astype(out[name].dtype)
    return out
```

```python
from contextlib import ExitStack

import concourse.bass as bass
from concourse import mybir

F32 = mybir.dt.float32
F32R = mybir.dt.float32r
ACT = mybir.ActivationFunctionType
ALU = mybir.AluOpType
AX = mybir.AxisListType

P = 128
DEPTH, DM, SEQ, NS = 2, 1024, 512, 8
TOK = SEQ + NS
HALF = TOK // 2
MT = DM // P
HEADS, DK, DV = 4, 256, 512
KT, VT = DK // P, DV // P
TT = SEQ // P
LW, CW, NBLK = 1280, 4, 16
LT = LW // P
GROUPS = 2
GT = LT // GROUPS
DFF = 2816
FH = 2
FT = DFF // P // FH
EPS = 1e-6
UW = 8 * P

BLK = LW // NBLK
BAND = [sorted({(b * BLK + e) // P for b in range(t * P // BLK, (t * P + P - 1) // BLK + 1)
                for e in (0, BLK - 1)}) for t in range(GT)]

U_HEAD = 2 * KT + 2 * VT + MT // 2
U_LRU = 3 * GT + MT
U_RET, U_LRUS, U_MERGE, U_WO = HEADS * U_HEAD, GROUPS * U_LRU, 2 * MT, MT
U_FFN = 2 * FT + 2 * MT
B_LRU = U_RET
B_MERGE = B_LRU + U_LRUS
B_WO = B_MERGE + U_MERGE
B_FFN = B_WO + U_WO
UNITS = B_FFN + FH * U_FFN
K_DOWN = (6, FT - 6)

T_HEAD = 2 * KT + 2 * VT + 2 + MT
T_LRU = 4 * GT + MT
C_LRU = HEADS * T_HEAD
C_MERGE = C_LRU + GROUPS * T_LRU
C_WO = C_MERGE + 2 * MT
C_NORM1 = C_WO + MT
C_FFN = C_NORM1 + 1
T_FFN = 2 * FT + MT
C_NORM2 = C_FFN + FH * T_FFN
TILES = C_NORM2 + 1
TILE0 = 2
TG = [2 * KT + VT, 2 * KT + VT + 1, 2 * KT + VT + 2, 2 * KT + VT + 4]
T_MEAN, T_VAR, T_OUT = 2 * KT + VT + 3, 2 * KT + VT + 5, 2 * KT + VT + 6
assert UNITS % 2 == TILES % 2 == U_HEAD % 2 == T_HEAD % 2 == T_LRU % 2 == 0

N_SC, N_TK, N_TV, N_VS, N_AT, N_ST = 0, 4, 6, 10, 11, 15
AUX_USES = 17
BANK = [0, 1, 2, 3, 0, 1, 2, 3, 0, 1, 2, 0, 1, 2, 0, 1, 2]
BANK_SO = 3
PREV = [max([m for m in range(n) if BANK[m] == BANK[n]], default=None) for n in range(AUX_USES)]

ST_OFF = [sum(SEQ - P * i for i in range(j)) for j in range(TT + 1)]
SRING, VRING = 3, 2
SUSES = [len(range(r, NS, SRING)) for r in range(SRING)]

PC_GN, PC_CW, PC_CB, PC_BA, PC_BX, PC_BG, PC_SP = 0, 16, 56, 66, 76, 86, 102
PCOLS = 112


def build(nc, wstream, xt, params, norms, tables, dec, kdt, slru, sconv, sret, ident,
          yt, ret_p, ret_s, lru_o, conv_p, conv_s, vscr):
    ctx = ExitStack()
    with ctx:
        def sb(name, shape, dt=F32):
            return ctx.enter_context(nc.sbuf_tensor(name, shape, dt))

        def sem(name):
            return ctx.enter_context(nc.semaphore(name))

        X = sb("residual", [P, MT, TOK])
        XH = sb("x_high", [P, MT, TOK], F32R)
        XL = sb("x_low", [P, MT, TOK], F32R)
        WR = sb("w_raw", [P, 2, UW])
        WH = sb("w_high", [P, 2, UW], F32R)
        WL = sb("w_low", [P, 2, UW], F32R)
        ACC = sb("ret_acc", [P, MT, TOK])
        COS = sb("cos_r", [P, TOK])
        SIN = sb("sin_r", [P, TOK])
        DEC = sb("decay", [P, SEQ])
        RINV = sb("rinv", [P, TOK])
        ONES = sb("ones", [P, P])
        ID = sb("ident_sb", [P, P])
        PAR = sb("params_all", [P, DEPTH, PCOLS])
        CUR = sb("params_cur", [P, PCOLS])
        NRM = sb("norms_all", [P, 2 * DEPTH + 1, MT])
        GAIN = sb("gain_cur", [P, MT])
        GAIN2 = GAIN[:, :].rearrange("p (n two) -> p two n", two=2)
        KDT = sb("kd_all", [P, HEADS, TT + 1])
        KDC = sb("kd_cur", [P, TT + 1])
        GNC = sb("gn_cur", [P, VT])
        SLR = sb("state_lru_sb", [P, LT, NS])
        SCV = sb("state_conv_sb", [P, LT, CW - 1, NS])
        LRO = sb("lru_out_sb", [P, LT, NS + 1])
        CVP = sb("conv_p_sb", [P, LT, CW - 1])
        CVS = sb("conv_s_sb", [P, LT, CW - 1, NS])
        EPST = sb("eps", [P, 1])
        TOUCH = sb("touch", [P, 1])
        KSC = sb("k_sample", [P, KT, NS])

        R_HEAD = 4 * KT * TOK + 2 * TT * DV + 2 * TT * DK + 2 * ST_OFF[TT]
        R = sb("split_scratch", [P, max(R_HEAD + 2 * VT * NS, 2 * FT * TOK)], F32R)

        def rview(off, a, b):
            return R[:, off:off + a * b].rearrange("p (a b) -> p a b", a=a)

        QH, QL, KH, KL = (rview(i * KT * TOK, KT, TOK) for i in range(4))
        o = 4 * KT * TOK
        VH, VL = rview(o, TT, DV), rview(o + TT * DV, TT, DV)
        OGH, OGL = rview(o, VT, TOK), rview(o + VT * TOK, VT, TOK)
        o += 2 * VT * TOK
        KDH, KDL = rview(o, TT, DK), rview(o + TT * DK, TT, DK)
        o += 2 * TT * DK
        STH, STL = R[:, o:o + ST_OFF[TT]], R[:, o + ST_OFF[TT]:o + 2 * ST_OFF[TT]]
        XCH, XCL, GLH, GLL = (rview(i * GT * TOK, GT, TOK) for i in range(4))
        MH, ML = rview(0, MT, TOK), rview(MT * TOK, MT, TOK)
        AH, AL = rview(0, FT, TOK), rview(FT * TOK, FT, TOK)

        sizes = [("qk", 2 * KT * TOK), ("vo", VT * TOK), ("sg", VT * TOK), ("rt", 2 * TOK),
                 ("s", SRING * KT * DV), ("t", KT * DV), ("vb", VRING * DV), ("stat", 3 * TOK)]
        FA = sb("scratch", [P, sum(n for _, n in sizes)])
        at, pos = {}, 0
        for name, n in sizes:
            at[name] = pos
            pos += n

        def fview(off, a, b):
            return FA[:, off:off + a * b].rearrange("p (a b) -> p a b", a=a)

        QF, KF = fview(at["qk"], KT, TOK), fview(at["qk"] + KT * TOK, KT, TOK)
        SQ4 = fview(at["qk"], VT, TOK)
        VF = OF = fview(at["vo"], VT, TOK)
        SG = fview(at["sg"], VT, TOK)
        STF = FA[:, at["sg"]:at["sg"] + ST_OFF[TT]]
        RT = fview(at["rt"], 2, TOK)
        SF = fview(at["rt"], KT, DV)
        SS = FA[:, at["s"]:at["s"] + SRING * KT * DV].rearrange("p (r a b) -> p r a b", r=SRING, a=KT)
        TS = fview(at["t"], KT, DV)
        VB = fview(at["vb"], VRING, DV)
        VS = FA[0:NS, at["t"]:at["t"] + DV]
        SUM, RSTD, SSQ = (FA[:, at["stat"] + i * TOK:at["stat"] + (i + 1) * TOK] for i in range(3))
        SQT = fview(at["rt"], 2, TOK)
        ACCL = fview(0, MT, TOK)
        o = MT * TOK
        XCF = fview(o, GT, TOK)
        o += GT * TOK
        LA, IX, YF, AF = (fview(o + 2 * i * TOK, 2, TOK) for i in range(4))
        o += 8 * TOK
        DF, HF, XR = (FA[:, o + i * TOK:o + (i + 1) * TOK] for i in range(3))
        assert o + 3 * TOK <= pos
        ZM = fview(MT * TOK, 2, TOK)
        MG = FA[:, MT * TOK + 2 * TOK:MT * TOK + 3 * TOK]
        FG = fview(0, 2, TOK)
        FF = FA[:, 2 * TOK:3 * TOK]

        PP = ctx.enter_context(nc.psum_tensor("proj", [P, 2, 2, 512], F32))
        AUX = ctx.enter_context(nc.psum_tensor("aux", [P, 4, 512], F32))

        names = ("go_pool go_pe setup_ld x_ld boot w_split w_used p_done t_free "
                 "rope_done qk_high qk_low st_high st_low aux_mm aux_free kv_high kv_low "
                 "vs_st dec_ld trig_ld silu_g t_mul s_new so_done gn_sum gn_sq gn_sd og_full og_high "
                 "og_low sfin_st state_ld xc_full xc_high xc_low gate_r gate_i th_full d_full "
                 "w_sqrt y_gelu gl_full gl_high gl_low small_rd small_st sg_m mg_full mg_high mg_low "
                 "x_full x_sq x_high_s x_low_s x_sd f_silu f_full f_high f_low sp_e ones_ok y_full y_st").split()
        s = {n: sem(n) for n in names}
        w_ld = [sem(f"w_loaded{j}") for j in range(2)]
        s_ld = [sem(f"s_loaded{j}") for j in range(SRING)]
        s_st = [sem(f"s_stored{j}") for j in range(SRING)]
        v_ld = [sem(f"vb_loaded{j}") for j in range(VRING)]

        def halves(ap):
            return ap.rearrange("p (t b) -> p t b", t=2)

        def pair_row(t, i, j):
            return t[:, :, :].rearrange("p (n two) t -> p two n t", two=2)[:, j, bass.ds(i, 1), :].rearrange(
                "p a t -> p (a t)")

        def slot(idx):
            return (TILE0 + idx) % 2

        def pp(idx):
            return PP[:, slot(idx), :, 0:HALF]

        block = ctx.enter_context(nc.Block())

        @block.sync
        def _(sp):
            for j in range(2):
                sp.dma_start(WR[:, j, :], wstream[j]).then_inc(w_ld[j], 16)
            pairs = wstream.rearrange("(n two) p c -> two n p c", two=2)
            with sp.Fori(1, DEPTH * UNITS // 2) as i:
                for j in range(2):
                    sp.wait_ge(s["w_split"], 2 * i + (j - 1))
                    sp.dma_start(WR[:, j, :], pairs[j, bass.ds(i, 1)].rearrange("a p n -> (a p) n")
                                 ).then_inc(w_ld[j], 16)

        @block.gpsimd
        def _(pool):
            pool.memset(ONES[:], 1.0).then_inc(s["ones_ok"], 1)

            def split(j):
                pool.tensor_scalar(WH[:, j, :], WR[:, j, :], 1.0, 0.0, ALU.mult, ALU.add)
                pool.drain()
                pool.tensor_tensor(WL[:, j, :], WR[:, j, :], WH[:, j, :].bitcast(F32),
                                   ALU.subtract).then_inc(s["w_split"], 1)

            for j in range(2):
                pool.wait_ge(w_ld[j], 16)
                split(j)
            with pool.Fori(1, DEPTH * UNITS // 2) as i:
                for j in range(2):
                    pool.wait_ge(s["w_used"], 2 * i + j)
                    pool.wait_ge(w_ld[j], 16 * (i + 1))
                    pool.sem_inc(s["go_pool"], 1)
                    split(j)

        @block.tensor
        def _(pe):
            def product(outs, w, blk, xs, first, last):
                started = blk
                for n, (wt, xi) in enumerate(((WH, 0), (WH, 1), (WL, 0))):
                    for out, x in zip(outs, xs):
                        m = pe.matmul(out, wt[:, w, blk * P:(blk + 1) * P], x[xi],
                                      start=first and n == 0, stop=last and n == 2)
                        if not started:
                            m.then_inc(s["w_used"], 1)
                            started = True
                return m

            def tile_begin(tb, idx):
                pe.wait_ge(s["t_free"], tb + (idx - 1))

            def unit_begin(ub, u):
                pe.wait_ge(s["w_split"], ub + (u + 1))

            def pairs(hi, lo, k):
                return [(hi[:, k, c * HALF:(c + 1) * HALF], lo[:, k, c * HALF:(c + 1) * HALF])
                        for c in range(2)]

            def whole(ub, u, tb, idx, hi, lo):
                unit_begin(ub, u)
                tile_begin(tb, idx)
                outs = [PP[:, slot(idx), c, 0:HALF] for c in range(2)]
                for k in range(MT):
                    m = product(outs, u % 2, k, pairs(hi, lo, k), k == 0, k == MT - 1)
                m.then_inc(s["p_done"], 1)

            def column_sums(tb, idx, src):
                tile_begin(tb, idx)
                for c in range(2):
                    m = pe.matmul(PP[:, slot(idx), c, 0:HALF], ONES[:], src[:, c * HALF:(c + 1) * HALF],
                                  start=True, stop=True)
                m.then_inc(s["p_done"], 1)

            pe.sem_inc(s["p_done"], 1)
            pe.wait_ge(s["ones_ok"], 1)
            pe.wait_ge(s["setup_ld"], 16 * 4)
            pe.wait_ge(s["x_low_s"], MT)
            for c in range(2):
                m = pe.matmul(PP[:, 1, c, 0:HALF], ONES[:], SSQ[:, c * HALF:(c + 1) * HALF],
                              start=True, stop=True)
            m.then_inc(s["p_done"], 1)

            with pe.Fori(0, DEPTH) as layer:
                ub0, tb0 = layer * UNITS, layer * TILES + TILE0

                with pe.Fori(0, HEADS) as head:
                    ub, tb = ub0 + head * U_HEAD, tb0 + head * T_HEAD
                    hh = layer * HEADS + head
                    for i in range(2 * KT + VT):
                        whole(ub, i, tb, i, XH, XL)
                    pe.wait_ge(s["qk_low"], hh * 2 + 2)

                    def aux_begin(n):
                        if PREV[n] is not None:
                            pe.wait_ge(s["aux_free"], hh * AUX_USES + (PREV[n] + 1))

                    for j in range(TT):
                        aux_begin(N_SC + j)
                        for d in range(KT):
                            for n, (a, b) in enumerate(((KH, QH), (KH, QL), (KL, QH))):
                                m = pe.matmul(AUX[:, BANK[N_SC + j], 0:SEQ - j * P],
                                              a[:, d, j * P:(j + 1) * P], b[:, d, j * P:SEQ],
                                              start=d == n == 0, stop=d == KT - 1 and n == 2)
                        m.then_inc(s["aux_mm"], 1)
                    for i in range(TT // 2):
                        aux_begin(N_TK + i)
                        for j in range(2):
                            for d in range(KT):
                                m = pe.transpose(
                                    AUX[:, BANK[N_TK + i], (j * KT + d) * P:(j * KT + d + 1) * P],
                                    KF[:, d, (2 * i + j) * P:(2 * i + j + 1) * P], ID[:])
                        m.then_inc(s["aux_mm"], 1)
                    pe.wait_ge(s["t_free"], tb + 2 * KT + VT)
                    for j in range(TT):
                        aux_begin(N_TV + j)
                        for e in range(VT):
                            m = pe.transpose(AUX[:, BANK[N_TV + j], e * P:(e + 1) * P],
                                             VF[:, e, j * P:(j + 1) * P], ID[:])
                        m.then_inc(s["aux_mm"], 1)
                    aux_begin(N_VS)
                    for e in range(VT):
                        m = pe.transpose(AUX[0:NS, BANK[N_VS], e * P:(e + 1) * P],
                                         VF[:, e, SEQ:TOK], ID[:])
                    m.then_inc(s["aux_mm"], 1)

                    def gate(e):
                        whole(ub, 2 * KT + VT + e, tb, TG[e], XH, XL)

                    def attend(e):
                        aux_begin(N_AT + e)
                        for j in range(TT):
                            for n, (a, b) in enumerate(((VH, STH), (VH, STL), (VL, STH))):
                                m = pe.matmul(AUX[:, BANK[N_AT + e], j * P:SEQ],
                                              a[:, j, e * P:(e + 1) * P],
                                              b[:, ST_OFF[j]:ST_OFF[j + 1]],
                                              start=j == n == 0, stop=j == TT - 1 and n == 2)
                        m.then_inc(s["aux_mm"], 1)

                    def final_state(d):
                        aux_begin(N_ST + d)
                        for j in range(TT):
                            for n, (a, b) in enumerate(((KDH, VH), (KDH, VL), (KDL, VH))):
                                m = pe.matmul(AUX[:, BANK[N_ST + d], :], a[:, j, d * P:(d + 1) * P],
                                              b[:, j, :], start=j == n == 0,
                                              stop=j == TT - 1 and n == 2)
                        m.then_inc(s["aux_mm"], 1)

                    def sample_out(b):
                        pe.wait_ge(s["s_new"], hh * NS + (b + 1))
                        for e in range(VT):
                            for d in range(KT):
                                m = pe.matmul(AUX[:, BANK_SO, e * NS + b:e * NS + b + 1],
                                              SS[:, b % SRING, d, e * P:(e + 1) * P],
                                              QF[:, d, SEQ + b:SEQ + b + 1],
                                              start=b == e == d == 0, stop=d == KT - 1,
                                              skip_group_check=True)
                        m.then_inc(s["so_done"], 1)

                    gate(0)
                    gate(1)
                    pe.wait_ge(s["kv_low"], hh * (2 * TT) + 2 * TT)
                    pe.wait_ge(s["st_low"], hh * TT + TT)
                    sample_out(0)
                    for e in range(VT):
                        attend(e)
                        sample_out(1 + e)
                    for d in range(KT):
                        final_state(d)
                        sample_out(1 + VT + d)
                    gate(2)
                    sample_out(NS - 1)
                    pe.wait_ge(s["gn_sum"], hh * 2 + 1)
                    column_sums(tb, T_MEAN, SUM)
                    gate(3)
                    pe.wait_ge(s["gn_sum"], hh * 2 + 2)
                    column_sums(tb, T_VAR, SUM)
                    for m_ in range(MT):
                        u = 2 * KT + 2 * VT + m_ // 2
                        if m_ % 2 == 0:
                            unit_begin(ub, u)
                        tile_begin(tb, T_OUT + m_)
                        outs = [PP[:, slot(T_OUT + m_), c, 0:HALF] for c in range(2)]
                        for k in range(VT):
                            if m_ == 0:
                                pe.wait_ge(s["og_low"], hh * VT + (k + 1))
                            m = product(outs, u % 2, (m_ % 2) * VT + k, pairs(OGH, OGL, k),
                                        k == 0, k == VT - 1)
                        m.then_inc(s["p_done"], 1)

                for g in range(GROUPS):
                    bu, tb = B_LRU + g * U_LRU, tb0 + (C_LRU + g * T_LRU)
                    cb = layer * LT + g * GT
                    for t in range(GT):
                        whole(ub0, bu + t, tb, t, XH, XL)
                    for t in range(GT):
                        whole(ub0, bu + GT + 2 * t, tb, GT + 3 * t, XH, XL)
                        u = bu + GT + 2 * t + 1
                        unit_begin(ub0, u)
                        pe.wait_ge(s["xc_low"], cb + (BAND[t][-1] + 1))
                        for w in range(2):
                            idx = GT + 3 * t + 1 + w
                            tile_begin(tb, idx)
                            outs = [PP[:, slot(idx), c, 0:HALF] for c in range(2)]
                            for n, k in enumerate(BAND[t]):
                                m = product(outs, u % 2, w * len(BAND[t]) + n, pairs(XCH, XCL, k),
                                            n == 0, n == len(BAND[t]) - 1)
                            m.then_inc(s["p_done"], 1)
                    pe.wait_ge(s["gl_low"], cb + GT)
                    pe.sem_inc(s["go_pe"], 1)
                    with pe.Fori(0, MT // 2) as mm:
                        for j in range(2):
                            u, idx = bu + 3 * GT + j, 4 * GT + j
                            pe.wait_ge(s["w_split"], ub0 + (u + 1) + 2 * mm)
                            pe.wait_ge(s["t_free"], tb + (idx - 1) + 2 * mm)
                            outs = [PP[:, slot(idx), c, 0:HALF] for c in range(2)]
                            for k in range(GT):
                                m = product(outs, u % 2, k, pairs(GLH, GLL, k), k == 0, k == GT - 1)
                            m.then_inc(s["p_done"], 1)

                with pe.Fori(0, MT) as i:
                    for j in range(2):
                        whole(ub0 + 2 * i, B_MERGE + j, tb0 + 2 * i, C_MERGE + j, XH, XL)

                pe.wait_ge(s["mg_low"], layer * MT + MT)
                pe.sem_inc(s["go_pe"], 1)
                with pe.Fori(0, MT // 2) as i:
                    for j in range(2):
                        whole(ub0 + 2 * i, B_WO + j, tb0 + 2 * i, C_WO + j, MH, ML)
                pe.wait_ge(s["x_low_s"], layer * (2 * MT) + 2 * MT)
                column_sums(tb0, C_NORM1, SSQ)

                for f in range(FH):
                    bu, bt = B_FFN + f * U_FFN, C_FFN + f * T_FFN
                    with pe.Fori(0, FT) as i:
                        for j in range(2):
                            whole(ub0 + 2 * i, bu + j, tb0 + 2 * i, bt + j, XH, XL)
                    pe.wait_ge(s["f_low"], layer * (FH * FT) + (f + 1) * FT)
                    pe.sem_inc(s["go_pe"], 1)
                    with pe.Fori(0, MT // 2) as i:
                        for j in range(2):
                            idx = bt + 2 * FT + j
                            pe.wait_ge(s["t_free"], tb0 + (idx - 1) + 2 * i)
                            outs = [PP[:, slot(idx), c, 0:HALF] for c in range(2)]
                            k = 0
                            for v in range(2):
                                u = bu + 2 * FT + 2 * j + v
                                pe.wait_ge(s["w_split"], ub0 + (u + 1) + 4 * i)
                                for b in range(K_DOWN[v]):
                                    m = product(outs, u % 2, b, pairs(AH, AL, k), k == 0, k == FT - 1)
                                    k += 1
                            m.then_inc(s["p_done"], 1)
                pe.wait_ge(s["x_low_s"], layer * (2 * MT) + 3 * MT)
                column_sums(tb0, C_NORM2, SSQ)

        @block.vector
        def _(dve):
            tt, ts, stt = dve.tensor_tensor, dve.tensor_scalar, dve.scalar_tensor_tensor

            def done(tb, idx):
                dve.wait_ge(s["p_done"], tb + (idx + 1))

            def norm_low(x, xh, xl, gain, j, first):
                if first:
                    ts(SSQ, SQT[:, j, :], 1.0, None, ALU.mult)
                else:
                    tt(SSQ, SSQ, SQT[:, j, :], ALU.add)
                return stt(xl, x, gain, xh.bitcast(F32), ALU.mult, ALU.subtract)

            def root_inverse(dst):
                return dve.reciprocal(dst, dst)

            NL = DEPTH * LT
            lam = RT[:, 0, 0:NL].rearrange("p (d c) -> p d c", d=DEPTH)
            e_, z_, z2, acc = (RT[:, 0, NL * i:NL * (i + 1)] for i in range(1, 5))
            dve.sem_inc(s["t_free"], 1)
            dve.memset(EPST[:], EPS).then_inc(s["boot"], 1)
            dve.wait_ge(s["setup_ld"], 16 * 4)
            dve.tensor_copy(lam, PAR[:, :, PC_SP:PC_SP + LT]).then_inc(s["sp_e"], 1)
            dve.wait_ge(s["sp_e"], 3)
            ts(z_, e_, 2.0, None, ALU.add)
            dve.drain()
            dve.reciprocal(z_, z_)
            dve.drain()
            tt(z_, z_, e_, ALU.mult)
            dve.drain()
            tt(z2, z_, z_, ALU.mult)
            dve.memset(acc, 1.0 / 19)
            dve.drain()
            for n in range(17, 0, -2):
                tt(acc, acc, z2, ALU.mult)
                dve.drain()
                ts(acc, acc, 1.0 / n, None, ALU.add)
                dve.drain()
            tt(acc, acc, z_, ALU.mult)
            ts(e_, RT[:, 0, 0:NL], -8.0, 0.0, ALU.mult, ALU.max)
            dve.drain()
            stt(PAR[:, :, PC_SP:PC_SP + LT], acc.rearrange("p (d c) -> p d c", d=DEPTH), 16.0,
                e_.rearrange("p (d c) -> p d c", d=DEPTH), ALU.mult, ALU.add)
            dve.tensor_copy(GAIN[:], NRM[:, 0, :])
            dve.drain().then_inc(s["boot"], 1)
            dve.wait_ge(s["x_ld"], 16)
            for m in range(MT):
                dve.wait_ge(s["x_high_s"], m + 1)
                norm_low(X[:, m, :], XH[:, m, :], XL[:, m, :], GAIN[:, m:m + 1], m % 2, m == 0
                         ).then_inc(s["x_low_s"], 1)
                dve.drain()
            dve.wait_ge(s["x_sd"], 1)
            dve.drain()
            root_inverse(RINV[:]).then_inc(s["t_free"], 1)

            with dve.Fori(0, DEPTH) as layer:
                tb0 = layer * TILES + TILE0
                nb = layer * (2 * MT)
                dve.drain()
                dve.tensor_copy(CUR[:], PAR[:, bass.ds(layer, 1), :].rearrange("p a n -> p (a n)"))
                dve.memset(ACC[:], 0.0)
                dve.wait_ge(s["trig_ld"], layer * 32 + 32)
                tt(COS[:], COS[:], RINV[:], ALU.mult)
                tt(SIN[:], SIN[:], RINV[:], ALU.mult)

                with dve.Fori(0, HEADS) as head:
                    tb = tb0 + head * T_HEAD
                    hh = layer * HEADS + head
                    dve.drain()
                    dve.tensor_copy(KDC[:], KDT[:, bass.ds(head, 1), :].rearrange("p a n -> p (a n)"))
                    dve.tensor_copy(GNC[:], CUR[:, bass.ds(head * VT + PC_GN, VT)])
                    dve.wait_ge(s["sfin_st"], hh * 16 + 16)

                    def rotate(n, dst):
                        done(tb, n)
                        tt(halves(dst[:, 0, :]), pp(n), halves(COS[:]), ALU.mult)
                        tt(halves(dst[:, 1, :]), pp(n), halves(SIN[:]), ALU.mult).then_inc(s["t_free"], 1)
                        if n:
                            low(QL, QF, QH, 1.0, 1)
                        done(tb, n + 1)
                        tt(halves(RT[:, 0, :]), pp(n + 1), halves(SIN[:]), ALU.mult)
                        tt(halves(RT[:, 1, :]), pp(n + 1), halves(COS[:]), ALU.mult).then_inc(s["t_free"], 1)
                        dve.drain()
                        tt(dst[:, 0, :], dst[:, 0, :], RT[:, 0, :], ALU.subtract)
                        tt(dst[:, 1, :], dst[:, 1, :], RT[:, 1, :], ALU.add).then_inc(s["rope_done"], 1)
                        dve.drain()

                    def low(dst, src, hi, scale, n):
                        dve.wait_ge(s["qk_high"], hh * 2 + n)
                        stt(dst, src, scale, hi.bitcast(F32), ALU.mult, ALU.subtract
                            ).then_inc(s["qk_low"], 1)

                    rotate(0, QF)
                    rotate(2, KF)
                    ts(KSC[:], KF[:, :, SEQ:TOK], DK ** -0.5, None, ALU.mult)
                    for e in range(VT):
                        done(tb, 2 * KT + e)
                        tt(halves(VF[:, e, :]), pp(2 * KT + e), halves(RINV[:]), ALU.mult
                           ).then_inc(s["t_free"], 1)
                        if e == 0:
                            low(KL, KF, KH, DK ** -0.5, 2)

                    def aux(n):
                        dve.wait_ge(s["aux_mm"], hh * AUX_USES + (n + 1))

                    dve.wait_ge(s["dec_ld"], hh * 16 + 16)
                    for j in range(TT):
                        aux(N_SC + j)
                        tt(STF[:, ST_OFF[j]:ST_OFF[j + 1]], AUX[:, BANK[N_SC + j], 0:SEQ - j * P],
                           DEC[:, 0:SEQ - j * P], ALU.mult).then_inc(s["aux_free"], 1)
                    for j in range(TT):
                        dve.wait_ge(s["st_high"], hh * TT + (j + 1))
                        w = slice(ST_OFF[j], ST_OFF[j + 1])
                        tt(STL[:, w], STF[:, w], STH[:, w].bitcast(F32), ALU.subtract
                           ).then_inc(s["st_low"], 1)
                    for j in range(TT):
                        dve.wait_ge(s["kv_high"], hh * 2 * TT + (j + 1))
                        m = stt(KDL[:, j, :], AUX[:, BANK[N_TK + j // 2], (j % 2) * DK:(j % 2 + 1) * DK],
                                KDC[:, j:j + 1], KDH[:, j, :].bitcast(F32), ALU.mult, ALU.subtract)
                        m.then_inc(s["kv_low"], 1)
                        if j % 2:
                            dve.drain().then_inc(s["aux_free"], 1)
                    for j in range(TT):
                        dve.wait_ge(s["kv_high"], hh * 2 * TT + (TT + j + 1))
                        tt(VL[:, j, :], AUX[:, BANK[N_TV + j], :], VH[:, j, :].bitcast(F32), ALU.subtract
                           ).then_inc(s["kv_low"], 1)
                        dve.drain().then_inc(s["aux_free"], 1)
                    aux(N_VS)
                    ts(VS, AUX[0:NS, BANK[N_VS], :], 1.0, None, ALU.mult).then_inc(s["aux_free"], 1)

                    def gate(e):
                        done(tb, TG[e])
                        tt(halves(SG[:, e, :]), pp(TG[e]), halves(RINV[:]), ALU.mult
                           ).then_inc(s["t_free"], 1)

                    def new_state(b):
                        r = b % SRING
                        dve.wait_ge(s_ld[r], hh * (16 * SUSES[r]) + 16 * (b // SRING + 1))
                        dve.wait_ge(s["t_mul"], hh * NS + (b + 1))
                        stt(SS[:, r], SS[:, r], KDC[:, TT:TT + 1], TS, ALU.mult, ALU.add
                            ).then_inc(s["s_new"], 1)

                    gate(0)
                    gate(1)
                    new_state(0)
                    for e in range(VT):
                        new_state(1 + e)
                        aux(N_AT + e)
                        ts(OF[:, e, 0:SEQ], AUX[:, BANK[N_AT + e], :], 1.0, None, ALU.mult
                           ).then_inc(s["aux_free"], 1)
                    for d in range(KT):
                        new_state(1 + VT + d)
                        aux(N_ST + d)
                        ts(SF[:, d, :], AUX[:, BANK[N_ST + d], :], 1.0, None, ALU.mult
                           ).then_inc(s["aux_free"], 1)
                    gate(2)
                    new_state(NS - 1)
                    dve.wait_ge(s["so_done"], hh * NS + NS)
                    ts(OF[:, :, SEQ:TOK], AUX[:, BANK_SO, 0:VT * NS].rearrange("p (e b) -> p e b", e=VT),
                       1.0, None, ALU.mult)
                    dve.drain()
                    dve.tensor_reduce(SUM, OF.rearrange("p e t -> p t e"), AX.X, ALU.add
                                      ).then_inc(s["gn_sum"], 1)
                    done(tb, T_MEAN)
                    for e in range(VT):
                        m = stt(halves(OF[:, e, :]), pp(T_MEAN), -1.0 / DV, halves(OF[:, e, :]),
                                ALU.mult, ALU.add)
                    m.then_inc(s["t_free"], 1)
                    gate(3)
                    dve.wait_ge(s["gn_sq"], hh + 1)
                    dve.tensor_reduce(SUM, SQ4.rearrange("p e t -> p t e"), AX.X, ALU.add
                                      ).then_inc(s["gn_sum"], 1)
                    dve.wait_ge(s["silu_g"], hh * VT + VT)
                    tt(SG, SG, OF, ALU.mult)
                    dve.drain()
                    dve.wait_ge(s["gn_sd"], hh + 1)
                    root_inverse(RSTD).then_inc(s["t_free"], 1)
                    dve.drain()
                    for e in range(VT):
                        tt(SG[:, e, :], SG[:, e, :], RSTD, ALU.mult).then_inc(s["og_full"], 1)
                    dve.drain()
                    for e in range(VT):
                        dve.wait_ge(s["og_high"], hh * VT + (e + 1))
                        stt(OGL[:, e, :], SG[:, e, :], GNC[:, e:e + 1], OGH[:, e, :].bitcast(F32),
                            ALU.mult, ALU.subtract).then_inc(s["og_low"], 1)
                    for m_ in range(MT):
                        done(tb, T_OUT + m_)
                        tt(halves(ACC[:, m_, :]), pp(T_OUT + m_), halves(ACC[:, m_, :]), ALU.add
                           ).then_inc(s["t_free"], 1)

                dve.drain()
                dve.wait_ge(s["sfin_st"], (layer + 1) * (16 * HEADS) + 16)
                for r in range(SRING):
                    dve.wait_ge(s_st[r], (layer + 1) * (16 * SUSES[r] * HEADS) + 16)
                dve.wait_ge(s["state_ld"], layer * 32 + 32)
                dve.wait_ge(s["small_st"], layer * 48 + 16)
                for g in range(GROUPS):
                    tb = tb0 + (C_LRU + g * T_LRU)
                    cb = layer * LT + g * GT

                    if g:
                        dve.drain()

                    def low_xc(t):
                        dve.wait_ge(s["xc_high"], cb + (t + 1))
                        tt(XCL[:, t, :], XCF[:, t, :], XCH[:, t, :].bitcast(F32), ALU.subtract
                           ).then_inc(s["xc_low"], 1)

                    for t in range(GT):
                        c = g * GT + t

                        def cw(j):
                            return CUR[:, PC_CW + c * CW + j:PC_CW + c * CW + j + 1]

                        done(tb, t)
                        tt(halves(XR), pp(t), halves(RINV[:]), ALU.mult).then_inc(s["t_free"], 1)
                        dve.drain()
                        ts(XCF[:, t, :], XR, cw(CW - 1), CUR[:, PC_CB + c:PC_CB + c + 1],
                           ALU.mult, ALU.add)
                        dve.tensor_copy(CVP[:, c, :], XR[:, SEQ - CW + 1:SEQ])
                        dve.tensor_copy(CVS[:, c, 0:CW - 2, :], SCV[:, c, 1:CW - 1, :])
                        dve.tensor_copy(CVS[:, c, CW - 2, :], XR[:, SEQ:TOK])
                        for j in range(CW - 1):
                            d = CW - 1 - j
                            dve.drain()
                            stt(XCF[:, t, d:SEQ], XR[:, 0:SEQ - d], cw(j), XCF[:, t, d:SEQ],
                                ALU.mult, ALU.add)
                            m = stt(XCF[:, t, SEQ:TOK], SCV[:, c, j, :], cw(j), XCF[:, t, SEQ:TOK],
                                    ALU.mult, ALU.add)
                        m.then_inc(s["xc_full"], 1)
                        dve.drain()
                        if t:
                            low_xc(t - 1)
                    low_xc(GT - 1)

                    def stage_a(t):
                        b, c = t % 2, g * GT + t
                        dve.drain()
                        done(tb, GT + 3 * t)
                        tt(halves(YF[:, b, :]), pp(GT + 3 * t), halves(RINV[:]), ALU.mult
                           ).then_inc(s["t_free"], 1)
                        dve.wait_ge(s["gate_r"], cb + (t + 1))
                        ts(LA[:, b, :], LA[:, b, :], CUR[:, PC_SP + c:PC_SP + c + 1], None, ALU.mult
                           ).then_inc(s["t_free"], 1)
                        dve.wait_ge(s["gate_i"], cb + (t + 1))
                        tt(IX[:, b, :], IX[:, b, :], XCF[:, t, :], ALU.mult).then_inc(s["t_free"], 1)

                    def stage_b(t):
                        b, c = t % 2, g * GT + t
                        dve.wait_ge(s["th_full"], cb + (t + 1))
                        ts(DF, LA[:, b, :], 1.0, None, ALU.add)
                        dve.drain()
                        dve.reciprocal(DF, DF)
                        dve.drain()
                        stt(DF, LA[:, b, :], 2.0, DF, ALU.mult, ALU.mult).then_inc(s["d_full"], 1)
                        dve.wait_ge(s["w_sqrt"], cb + (t + 1))
                        tt(IX[:, b, :], IX[:, b, :], DF, ALU.mult)
                        tt(HF[:, SEQ:TOK], AF[:, b, SEQ:TOK], SLR[:, c, :], ALU.mult)
                        dve.drain()
                        dve.tensor_tensor_scan(HF[:, 0:SEQ], AF[:, b, 0:SEQ], IX[:, b, 0:SEQ], 0.0,
                                               ALU.mult, ALU.add)
                        tt(HF[:, SEQ:TOK], HF[:, SEQ:TOK], IX[:, b, SEQ:TOK], ALU.add)
                        dve.drain()
                        dve.tensor_copy(LRO[:, c, :], HF[:, SEQ - 1:TOK])
                        dve.wait_ge(s["y_gelu"], cb + (t + 1))
                        tt(YF[:, b, :], YF[:, b, :], HF, ALU.mult).then_inc(s["gl_full"], 1)
                        dve.wait_ge(s["gl_high"], cb + (t + 1))
                        tt(GLL[:, t, :], YF[:, b, :], GLH[:, t, :].bitcast(F32), ALU.subtract
                           ).then_inc(s["gl_low"], 1)

                    for t in range(GT + 1):
                        if t < GT:
                            stage_a(t)
                        if t:
                            stage_b(t - 1)
                    if g == GROUPS - 1:
                        dve.drain().then_inc(s["small_rd"], 1)
                    with dve.Fori(0, MT // 2) as mm:
                        for j in range(2):
                            idx = 4 * GT + j
                            dve.wait_ge(s["p_done"], tb + (idx + 1) + 2 * mm)
                            dst = halves(pair_row(ACCL, mm, j))
                            if g == 0:
                                ts(dst, pp(idx), 1.0, None, ALU.mult).then_inc(s["t_free"], 1)
                            else:
                                tt(dst, pp(idx), dst, ALU.add).then_inc(s["t_free"], 1)

                with dve.Fori(0, MT) as mm:
                    dve.drain()
                    for j in range(2):
                        idx = C_MERGE + j
                        dve.wait_ge(s["p_done"], tb0 + (idx + 1) + 2 * mm)
                        tt(halves(ZM[:, j, :]), pp(idx), halves(RINV[:]), ALU.mult).then_inc(s["t_free"], 1)
                    dve.wait_ge(s["sg_m"], layer * (2 * MT) + 2 + 2 * mm)
                    tt(ZM[:, 0, :], ZM[:, 0, :], ACC[:, bass.ds(mm, 1), :].rearrange("p a t -> p (a t)"), ALU.mult)
                    tt(ZM[:, 1, :], ZM[:, 1, :], ACCL[:, bass.ds(mm, 1), :].rearrange("p a t -> p (a t)"), ALU.mult)
                    dve.drain()
                    tt(MG, ZM[:, 0, :], ZM[:, 1, :], ALU.add).then_inc(s["mg_full"], 1)
                    dve.wait_ge(s["mg_high"], layer * MT + 1 + mm)
                    tt(ML[:, bass.ds(mm, 1), :].rearrange("p a t -> p (a t)"), MG,
                       MH[:, bass.ds(mm, 1), :].rearrange("p a t -> p (a t)").bitcast(F32),
                       ALU.subtract).then_inc(s["mg_low"], 1)

                def residual(tbi, idx, i, j, count, normed):
                    dve.wait_ge(s["p_done"], tbi + (idx + 1) + 2 * i)
                    xr = halves(pair_row(X, i, j))
                    m = tt(xr, pp(idx), xr, ALU.add)
                    m.then_inc(s["t_free"], 1)
                    if normed:
                        dve.drain().then_inc(s["x_full"], 1)
                        dve.wait_ge(s["x_high_s"], count + 2 * i)
                        x1, h1, l1 = (pair_row(v, i, j) for v in (X, XH, XL))
                        tt(SSQ, SSQ, SQT[:, j, :], ALU.add)
                        stt(l1, x1, GAIN2[:, j, bass.ds(i, 1)], h1.bitcast(F32), ALU.mult,
                            ALU.subtract).then_inc(s["x_low_s"], 1)
                        dve.drain()

                def next_norm(idx, n):
                    dve.drain()
                    dve.memset(SSQ, 0.0)
                    dve.tensor_copy(GAIN[:], NRM[:, bass.ds(layer * 2 + n, 1), :].rearrange("p a n -> p (a n)"))
                    dve.drain()

                next_norm(0, 1)
                with dve.Fori(0, MT // 2) as i:
                    for j in range(2):
                        residual(tb0, C_WO + j, i, j, nb + MT + j + 1, True)
                dve.wait_ge(s["x_sd"], layer * 2 + 2)
                root_inverse(RINV[:]).then_inc(s["t_free"], 1)

                for f in range(FH):
                    bt = C_FFN + f * T_FFN
                    fb = layer * (FH * FT) + f * FT
                    dve.drain()
                    with dve.Fori(0, FT) as i:
                        for j in range(2):
                            idx = bt + j
                            dve.wait_ge(s["p_done"], tb0 + (idx + 1) + 2 * i)
                            tt(halves(FG[:, j, :]), pp(idx), halves(RINV[:]), ALU.mult
                               ).then_inc(s["t_free"], 1)
                        dve.drain()
                        dve.wait_ge(s["f_silu"], fb + 1 + i)
                        tt(FF, FG[:, 0, :], FG[:, 1, :], ALU.mult).then_inc(s["f_full"], 1)
                        dve.wait_ge(s["f_high"], fb + 1 + i)
                        tt(AL[:, bass.ds(i, 1), :].rearrange("p a t -> p (a t)"), FF,
                           AH[:, bass.ds(i, 1), :].rearrange("p a t -> p (a t)").bitcast(F32),
                           ALU.subtract).then_inc(s["f_low"], 1)
                    if f == FH - 1:
                        next_norm(1, 2)
                    with dve.Fori(0, MT // 2) as i:
                        for j in range(2):
                            residual(tb0, bt + 2 * FT + j, i, j, nb + 2 * MT + j + 1, f == FH - 1)
                dve.wait_ge(s["x_sd"], layer * 2 + 3)
                root_inverse(RINV[:]).then_inc(s["t_free"], 1)

            dve.drain()
            for m in range(MT):
                stt(ACC[:, m, :], X[:, m, :], GAIN[:, m:m + 1], RINV[:], ALU.mult, ALU.mult
                    ).then_inc(s["y_full"], 1)

        @block.scalar
        def _(act):
            copy, A = ACT.Copy, act.activation

            def apart():
                act.wait_ge(s["boot"], 1)

            for st in (*s_st, s["sfin_st"], s["small_st"]):
                act.sem_inc(st, 16)
            act.dma_start(PAR[:], params).then_inc(s["setup_ld"], 16)
            act.dma_start(NRM[:], norms).then_inc(s["setup_ld"], 16)
            act.dma_start(KDT[:], kdt).then_inc(s["setup_ld"], 16)
            act.dma_start(ID[:], ident).then_inc(s["setup_ld"], 16)
            act.dma_start(X[:], xt).then_inc(s["x_ld"], 16)
            NL = DEPTH * LT
            act.wait_ge(s["sp_e"], 1)
            A(RT[:, 0, NL:2 * NL], RT[:, 0, 0:NL], ACT.Abs).then_inc(s["sp_e"], 1)
            act.wait_ge(s["sp_e"], 2)
            A(RT[:, 0, NL:2 * NL], RT[:, 0, NL:2 * NL], ACT.Exp, scale=-1.0).then_inc(s["sp_e"], 1)

            act.wait_ge(s["x_ld"], 16)
            act.wait_ge(s["boot"], 2)
            for m in range(MT):
                if m >= 2:
                    act.wait_ge(s["x_low_s"], m - 1)
                A(SQT[:, m % 2, :], X[:, m, :], ACT.Square)
                A(XH[:, m, :], X[:, m, :], copy, scale=GAIN[:, m:m + 1]).then_inc(s["x_high_s"], 1)
                act.drain()
            act.wait_ge(s["p_done"], TILE0)
            A(halves(RINV[:]), PP[:, 1, :, 0:HALF], ACT.Sqrt, bias=EPST[:], scale=1.0 / DM
              ).then_inc(s["x_sd"], 1)

            with act.Fori(0, DEPTH) as layer:
                tb0 = layer * TILES + TILE0
                nb = layer * (2 * MT)
                act.dma_start(COS[:], tables[0]).then_inc(s["trig_ld"], 16)
                act.dma_start(SIN[:], tables[1]).then_inc(s["trig_ld"], 16)
                act.dma_start(SLR[:], slru[bass.ds(layer, 1)].rearrange("a p c b -> (a p) c b")
                              ).then_inc(s["state_ld"], 16)
                act.dma_start(SCV[:], sconv[bass.ds(layer, 1)].rearrange("a p c j b -> (a p) c j b")
                              ).then_inc(s["state_ld"], 16)

                with act.Fori(0, HEADS) as head:
                    tb = tb0 + head * T_HEAD
                    hh = layer * HEADS + head

                    def state(dram, b):
                        return dram[bass.ds(layer, 1), b, bass.ds(head, 1)].rearrange(
                            "l h (d p) e -> p (l h d) e", p=P)

                    def load_state(b):
                        act.dma_start(SS[:, b % SRING], state(sret, b)).then_inc(s_ld[b % SRING], 16)

                    def load_vb(b):
                        act.dma_start(VB[:, b % VRING, :],
                                      vscr[b:b + 1, :].broadcast_to([P, DV])
                                      ).then_inc(v_ld[b % VRING], 16)

                    act.dma_start(DEC[:], dec[bass.ds(head, 1)].rearrange("a p n -> (a p) n")
                                  ).then_inc(s["dec_ld"], 16)
                    for r in range(SRING):
                        act.wait_ge(s_st[r], hh * (16 * SUSES[r]) + 16)
                        load_state(r)
                    for n, (hi, full, scale) in enumerate(((QH, QF, 1.0), (KH, KF, DK ** -0.5))):
                        act.wait_ge(s["rope_done"], hh * 2 + (n + 1))
                        A(hi, full, copy, scale=scale).then_inc(s["qk_high"], 1)
                    for j in range(TT):
                        act.wait_ge(s["aux_free"], hh * AUX_USES + (N_SC + j + 1))
                        w = slice(ST_OFF[j], ST_OFF[j + 1])
                        A(STH[:, w], STF[:, w], copy).then_inc(s["st_high"], 1)
                    for j in range(TT):
                        act.wait_ge(s["aux_mm"], hh * AUX_USES + (N_TK + j // 2 + 1))
                        A(KDH[:, j, :], AUX[:, BANK[N_TK + j // 2], (j % 2) * DK:(j % 2 + 1) * DK], copy,
                          scale=KDC[:, j:j + 1]).then_inc(s["kv_high"], 1)
                        if j % 2 == 0:
                            act.wait_ge(s["kv_low"], hh * (2 * TT) + (j + 1))
                    for j in range(TT):
                        act.wait_ge(s["aux_mm"], hh * AUX_USES + (N_TV + j + 1))
                        A(VH[:, j, :], AUX[:, BANK[N_TV + j], :], copy).then_inc(s["kv_high"], 1)
                    act.wait_ge(s["aux_free"], hh * AUX_USES + (N_VS + 1))
                    act.dma_start(vscr[:, :], VS).then_inc(s["vs_st"], 16)
                    act.wait_ge(s["vs_st"], hh * 16 + 16)
                    for b in range(VRING):
                        load_vb(b)

                    def silu(e):
                        act.wait_ge(s["t_free"], tb + (TG[e] + 1))
                        A(SG[:, e, :], SG[:, e, :], ACT.Silu).then_inc(s["silu_g"], 1)

                    silu(0)
                    silu(1)
                    for b in range(NS):
                        act.wait_ge(v_ld[b % VRING], hh * (16 * NS // VRING) + 16 * (b // VRING + 1))
                        if b:
                            act.wait_ge(s["s_new"], hh * NS + b)
                        A(TS[:, 0, :], VB[:, b % VRING, :], copy, scale=KSC[:, 0, b:b + 1])
                        A(TS[:, 1, :], VB[:, b % VRING, :], copy, scale=KSC[:, 1, b:b + 1]
                          ).then_inc(s["t_mul"], 1)
                        if b:
                            act.dma_start(state(ret_s, b - 1), SS[:, (b - 1) % SRING]
                                          ).then_inc(s_st[(b - 1) % SRING], 16)
                        if b >= 2 and b + 1 < NS:
                            r = (b - 2) % SRING
                            act.wait_ge(s_st[r], hh * (16 * SUSES[r]) + 16 * ((b - 2) // SRING + 2))
                            act.wait_ge(s["so_done"], hh * NS + (b - 1))
                            load_state(b + 1)
                        if b + VRING < NS:
                            act.wait_ge(s["t_mul"], hh * NS + (b + 1))
                            load_vb(b + VRING)
                        if b == 6:
                            act.wait_ge(s["aux_free"], hh * AUX_USES + (N_ST + KT))
                            act.dma_start(ret_p[bass.ds(layer, 1), bass.ds(head, 1)].rearrange(
                                "l h (d p) e -> p (l h d) e", p=P), SF).then_inc(s["sfin_st"], 16)
                    act.wait_ge(s["s_new"], hh * NS + NS)
                    act.dma_start(state(ret_s, NS - 1), SS[:, (NS - 1) % SRING]
                                  ).then_inc(s_st[(NS - 1) % SRING], 16)
                    silu(2)
                    act.wait_ge(s["t_free"], tb + (T_MEAN + 1))
                    A(SQ4, OF, ACT.Square).then_inc(s["gn_sq"], 1)
                    silu(3)
                    act.wait_ge(s["p_done"], tb + (T_VAR + 1))
                    A(halves(RSTD), pp(T_VAR), ACT.Sqrt, bias=EPST[:], scale=1.0 / DV
                      ).then_inc(s["gn_sd"], 1)
                    for e in range(VT):
                        act.wait_ge(s["og_full"], hh * VT + (e + 1))
                        A(OGH[:, e, :], SG[:, e, :], copy, scale=GNC[:, e:e + 1]).then_inc(s["og_high"], 1)

                for g in range(GROUPS):
                    tb = tb0 + (C_LRU + g * T_LRU)
                    cb = layer * LT + g * GT
                    for t in range(GT):
                        act.wait_ge(s["xc_full"], cb + (t + 1))
                        A(XCH[:, t, :], XCF[:, t, :], copy).then_inc(s["xc_high"], 1)

                    def stage_a(t):
                        b, c = t % 2, g * GT + t
                        act.wait_ge(s["p_done"], tb + (GT + 3 * t + 2))
                        A(halves(LA[:, b, :]), pp(GT + 3 * t + 1), ACT.Sigmoid,
                          bias=CUR[:, PC_BA + c:PC_BA + c + 1]).then_inc(s["gate_r"], 1)
                        act.wait_ge(s["p_done"], tb + (GT + 3 * t + 3))
                        A(halves(IX[:, b, :]), pp(GT + 3 * t + 2), ACT.Sigmoid,
                          bias=CUR[:, PC_BX + c:PC_BX + c + 1]).then_inc(s["gate_i"], 1)
                        act.wait_ge(s["t_free"], tb + (GT + 3 * t + 2))
                        A(AF[:, b, :], LA[:, b, :], ACT.Exp, scale=-1.0)
                        act.drain()
                        A(LA[:, b, :], LA[:, b, :], ACT.Tanh).then_inc(s["th_full"], 1)
                        A(YF[:, b, :], YF[:, b, :], ACT.Gelu_apprx_tanh).then_inc(s["y_gelu"], 1)

                    def stage_b(t):
                        b = t % 2
                        act.wait_ge(s["d_full"], cb + (t + 1))
                        A(DF, DF, ACT.Sqrt).then_inc(s["w_sqrt"], 1)
                        act.wait_ge(s["gl_full"], cb + (t + 1))
                        A(GLH[:, t, :], YF[:, b, :], copy).then_inc(s["gl_high"], 1)

                    for t in range(GT + 1):
                        if t < GT:
                            stage_a(t)
                        if t:
                            stage_b(t - 1)
                act.wait_ge(s["small_rd"], layer + 1)
                for dram, src in ((lru_o, LRO), (conv_p, CVP)):
                    act.dma_start(dram[bass.ds(layer, 1)].rearrange("a p c b -> (a p) c b"), src[:]
                                  ).then_inc(s["small_st"], 16)
                act.dma_start(conv_s[bass.ds(layer, 1)].rearrange("a p c j b -> (a p) c j b"), CVS[:]
                              ).then_inc(s["small_st"], 16)

                A(TOUCH[:], EPST[:], ACT.Sigmoid)
                with act.Fori(0, MT) as mm:
                    for j in range(2):
                        act.wait_ge(s["t_free"], tb0 + (C_MERGE + j + 1) + 2 * mm)
                        apart()
                        A(ZM[:, j, :], ZM[:, j, :], ACT.Sigmoid, bias=CUR[:, bass.ds(mm + (PC_BG + j * MT), 1)]
                          ).then_inc(s["sg_m"], 1)
                    act.wait_ge(s["mg_full"], layer * MT + 1 + mm)
                    apart()
                    A(MH[:, bass.ds(mm, 1), :].rearrange("p a t -> p (a t)"), MG, copy
                      ).then_inc(s["mg_high"], 1)

                def normed(full, high, i, j):
                    act.wait_ge(s["x_full"], full + 2 * i)
                    act.wait_ge(s["x_low_s"], high - 2 + 2 * i)
                    apart()
                    x1, h1 = pair_row(X, i, j), pair_row(XH, i, j)
                    A(SQT[:, j, :], x1, ACT.Square)
                    A(h1, x1, copy, scale=GAIN2[:, j, bass.ds(i, 1)]).then_inc(s["x_high_s"], 1)
                    act.drain()

                with act.Fori(0, MT // 2) as i:
                    for j in range(2):
                        normed(nb + j + 1, nb + MT + j + 1, i, j)
                act.wait_ge(s["p_done"], tb0 + (C_NORM1 + 1))
                A(halves(RINV[:]), pp(C_NORM1), ACT.Sqrt, bias=EPST[:], scale=1.0 / DM
                  ).then_inc(s["x_sd"], 1)

                A(TOUCH[:], EPST[:], ACT.Silu)
                for f in range(FH):
                    bt = C_FFN + f * T_FFN
                    fb = layer * (FH * FT) + f * FT
                    with act.Fori(0, FT) as i:
                        act.wait_ge(s["t_free"], tb0 + (bt + 1) + 2 * i)
                        A(FG[:, 0, :], FG[:, 0, :], ACT.Silu).then_inc(s["f_silu"], 1)
                        act.wait_ge(s["f_full"], fb + 1 + i)
                        apart()
                        A(AH[:, bass.ds(i, 1), :].rearrange("p a t -> p (a t)"), FF, copy
                          ).then_inc(s["f_high"], 1)
                with act.Fori(0, MT // 2) as i:
                    for j in range(2):
                        normed(nb + MT + j + 1, nb + 2 * MT + j + 1, i, j)
                act.wait_ge(s["p_done"], tb0 + (C_NORM2 + 1))
                A(halves(RINV[:]), pp(C_NORM2), ACT.Sqrt, bias=EPST[:], scale=1.0 / DM
                  ).then_inc(s["x_sd"], 1)

            for m in range(MT):
                act.wait_ge(s["y_full"], m + 1)
                act.dma_start(yt[:, m, :], ACC[:, m, :]).then_inc(s["y_st"], 16)
            act.wait_ge(s["y_st"], 16 * MT)
            act.wait_ge(s["small_st"], 48 * DEPTH + 16)
            act.wait_ge(s["sfin_st"], 16 * DEPTH * HEADS + 16)
            act.wait_ge(s["vs_st"], 16 * DEPTH * HEADS)
            for r in range(SRING):
                act.wait_ge(s_st[r], 16 * SUSES[r] * DEPTH * HEADS + 16)


def weight_units(np, w_in, w_ret_out, wa, wx, w_lru_out, w_o, w_gate_up, w_down):
    off = np.cumsum([0, HEADS * DK, HEADS * DK, HEADS * DV, HEADS * DV, LW, LW, DM])
    out = np.zeros((DEPTH * UNITS, P, UW), np.float32)
    n = 0

    def tile(w, col, rows, put=0):
        for i, r in enumerate(rows):
            out[n, :, (put + i) * P:(put + i + 1) * P] = w[r * P:(r + 1) * P, col:col + P]

    for l in range(DEPTH):
        for h in range(HEADS):
            cols = [off[0] + h * DK + i * P for i in range(KT)] + [off[1] + h * DK + i * P for i in range(KT)]
            cols += [off[2] + h * DV + i * P for i in range(VT)] + [off[3] + h * DV + i * P for i in range(VT)]
            for c in cols:
                tile(w_in[l], c, range(MT))
                n += 1
            for m in range(0, MT, 2):
                for j in range(2):
                    tile(w_ret_out[l], (m + j) * P, range(h * VT, (h + 1) * VT), j * VT)
                n += 1
        for g in range(GROUPS):
            wide = GT * P
            gates = []
            for w in (wa, wx):
                full = np.zeros((wide, wide), np.float32)
                for b in range(NBLK // GROUPS):
                    full[b * BLK:(b + 1) * BLK, b * BLK:(b + 1) * BLK] = w[l, g * (NBLK // GROUPS) + b]
                gates.append(full)
            for t in range(GT):
                tile(w_in[l], off[4] + g * wide + t * P, range(MT))
                n += 1
            for t in range(GT):
                tile(w_in[l], off[5] + g * wide + t * P, range(MT))
                n += 1
                for i, full in enumerate(gates):
                    tile(full, t * P, BAND[t], i * len(BAND[t]))
                n += 1
            for m in range(MT):
                tile(w_lru_out[l], m * P, range(g * GT, (g + 1) * GT))
                n += 1
        for m in range(MT):
            for j in range(2):
                tile(w_in[l], off[6 + j] + m * P, range(MT))
                n += 1
        for m in range(MT):
            tile(w_o[l], m * P, range(MT))
            n += 1
        for f in range(FH):
            for t in range(FT):
                for j in range(2):
                    tile(w_gate_up[l], j * DFF + (f * FT + t) * P, range(MT))
                    n += 1
            for m in range(MT):
                tile(w_down[l], m * P, range(f * FT, f * FT + K_DOWN[0]))
                n += 1
                tile(w_down[l], m * P, range(f * FT + K_DOWN[0], (f + 1) * FT))
                n += 1
    assert n == DEPTH * UNITS
    return out


def constants(np, past):
    f4 = np.float32
    half = DK // 2
    freqs = np.power(10000.0, -(np.arange(half, dtype=f4) / f4(half)).astype(np.float64)).astype(f4)
    pos = np.concatenate([np.arange(SEQ, dtype=f4), np.full(NS, past, f4)])
    ang = (freqs[:, None] * pos[None, :]).astype(f4).astype(np.float64)
    trig = np.stack([np.cos(ang), np.sin(ang)]).astype(f4)
    lg = np.log(1.0 - 2.0 ** (-5.0 - np.arange(HEADS)))
    diff = np.arange(SEQ)[None, :] - np.arange(P)[:, None]
    dec = np.where(diff >= 0, np.exp(lg[:, None, None] * np.maximum(diff, 0)), 0.0).astype(f4)
    kd = np.zeros((P, HEADS, TT + 1), f4)
    for h in range(HEADS):
        for j in range(TT):
            kd[:, h, j] = np.exp(lg[h] * (SEQ - 1 - j * P - np.arange(P))) * DK ** -0.5
        kd[:, h, TT] = np.exp(lg[h])
    return trig, dec, kd, np.eye(P, dtype=f4)


def kernel(x_prompt, x_sample, state_ret, state_lru, state_conv, w_in, norm_mix, gn_gain, w_ret_out,
           conv_w, conv_b, lru_wa, lru_ba, lru_wx, lru_bx, lru_lambda, w_lru_out, b_gate, w_o,
           norm_ffn, w_gate_up, w_down, norm_final):
    import numpy as np
    import concourse.bacc as bacc
    from concourse.bass_utils import run_bass_kernel_spmd

    arr = lambda a: np.asarray(a)
    x = np.concatenate([arr(x_prompt)[0], arr(x_sample)[:, 0]], 0)
    xt = np.ascontiguousarray(x.T.reshape(MT, P, TOK).transpose(1, 0, 2))

    def chan(a):
        a = arr(a)
        return np.moveaxis(a.reshape(a.shape[:-1] + (-1, P)), -1, -2)

    cw = chan(conv_w)
    params = np.concatenate([
        chan(gn_gain), cw.transpose(0, 2, 3, 1).reshape(DEPTH, P, LT * CW), chan(conv_b), chan(lru_ba),
        chan(lru_bx), chan(b_gate).transpose(0, 2, 1, 3).reshape(DEPTH, P, 2 * MT), chan(lru_lambda)], 2)
    params = np.ascontiguousarray(params.transpose(1, 0, 2))
    nm, nf = chan(norm_mix), chan(norm_ffn)
    norms = np.stack([nm[0], nf[0], nm[1], nf[1], chan(norm_final)], 1)
    slru = chan(state_lru).transpose(0, 2, 3, 1)
    sconv = chan(state_conv).transpose(0, 3, 4, 2, 1)
    trig, dec, kdt, ident = constants(np, 4096)
    ins = dict(
        wstream=weight_units(np, *(arr(a) for a in (w_in, w_ret_out, lru_wa, lru_wx, w_lru_out, w_o,
                                                    w_gate_up, w_down))),
        xt=xt, params=params, norms=norms, tables=trig, dec=dec, kdt=kdt, slru=slru, sconv=sconv,
        sret=arr(state_ret), ident=ident)
    outs = dict(yt=(P, MT, TOK), ret_p=(DEPTH, HEADS, DK, DV), ret_s=(DEPTH, NS, HEADS, DK, DV),
                lru_o=(DEPTH, P, LT, NS + 1), conv_p=(DEPTH, P, LT, CW - 1),
                conv_s=(DEPTH, P, LT, CW - 1, NS))

    nc = bacc.Bacc("TRN2", target_bir_lowering=False, num_devices=1)
    arrays, aps = {}, {}
    for name, a in ins.items():
        a = np.ascontiguousarray(a)
        arrays["in_" + name] = a
        aps[name] = nc.dram_tensor("in_" + name, a.shape, F32, kind="ExternalInput").ap()
    for name, shape in outs.items():
        aps[name] = nc.dram_tensor("out_" + name, shape, F32, kind="ExternalOutput").ap()
    aps["vscr"] = nc.dram_tensor("v_rows", (NS, DV), F32, kind="Internal").ap()
    build(nc, **aps)
    got = run_bass_kernel_spmd(nc, [arrays], core_ids=[0]).results[0]
    got = {name: got["out_" + name] for name in outs}

    y = got["yt"].transpose(1, 0, 2).reshape(DM, TOK).T
    lru = got["lru_o"].transpose(0, 3, 2, 1).reshape(DEPTH, NS + 1, LW)
    return (
        np.ascontiguousarray(y[:SEQ])[None], np.ascontiguousarray(y[SEQ:])[:, None],
        got["ret_p"][:, None], np.ascontiguousarray(lru[:, :1]),
        np.ascontiguousarray(got["conv_p"].transpose(0, 3, 2, 1).reshape(DEPTH, 1, CW - 1, LW)),
        got["ret_s"], np.ascontiguousarray(lru[:, 1:]),
        np.ascontiguousarray(got["conv_s"].transpose(0, 4, 3, 2, 1).reshape(DEPTH, NS, CW - 1, LW)),
    )
```

```python
from contextlib import ExitStack

import concourse.bass as bass
from concourse import mybir

F32 = mybir.dt.float32
F32R = mybir.dt.float32r
ACT = mybir.ActivationFunctionType
ALU = mybir.AluOpType
AX = mybir.AxisListType

P = 128
DEPTH, DM, SEQ, NS = 2, 1024, 512, 8
TOK = SEQ + NS
HALF = TOK // 2
MT = DM // P
HEADS, DK, DV = 4, 256, 512
KT, VT = DK // P, DV // P
TT = SEQ // P
LW, CW, NBLK = 1280, 4, 16
LT = LW // P
GROUPS = 2
GT = LT // GROUPS
DFF = 2816
FH = 2
FT = DFF // P // FH
EPS = 1e-6
UW = 8 * P

BLK = LW // NBLK
BAND = [sorted({(b * BLK + e) // P for b in range(t * P // BLK, (t * P + P - 1) // BLK + 1)
                for e in (0, BLK - 1)}) for t in range(GT)]

QK, GATES = 2 * KT, VT
LRU_GATES = [n for t in range(GT) for n in (MT, 2 * len(BAND[t]))]
K_DOWN = (6, FT - 6)
U_HEAD = QK + VT + GATES + MT // 2
RUNS = ([(HEADS * U_HEAD, (MT,))]
        + [(1, (MT,) * GT + tuple(LRU_GATES)), (MT, (GT,))] * GROUPS
        + [(3 * MT, (MT,))] + [(2 * FT, (MT,)), (MT, K_DOWN)] * FH)
U_LRU = 3 * GT + MT
B_LRU = HEADS * U_HEAD
B_MERGE = B_LRU + GROUPS * U_LRU
B_WO = B_MERGE + 2 * MT
B_FFN = B_WO + MT
U_FFN = 2 * FT + 2 * MT
UNITS = B_FFN + FH * U_FFN
assert UNITS == sum(n * len(w) for n, w in RUNS)

T_HEAD = QK + VT + GATES + 2 + MT
T_LRU = 4 * GT + MT
C_LRU = HEADS * T_HEAD
C_MERGE = C_LRU + GROUPS * T_LRU
C_WO = C_MERGE + 2 * MT
C_NORM1 = C_WO + MT
C_FFN = C_NORM1 + 1
T_FFN = 2 * FT + MT
C_NORM2 = C_FFN + FH * T_FFN
TILES = C_NORM2 + 1
TILE0 = 2
TG = [0, 1, 4, 2]
T_MEAN, T_VAR = 3, 5
UG = [0, 1, 3, 2]
assert UNITS % 2 == TILES % 2 == U_HEAD % 2 == T_HEAD % 2 == T_LRU % 2 == MT // 2 % 2 == 0

N_SC, N_TK, N_VS, N_TV, N_AT, N_ST = 0, 4, 6, 7, 11, 15
AUX_USES = 17
BANK = [0, 1, 2, 3, 0, 1, 2, 3, 0, 1, 2, 0, 1, 2, 0, 1, 2]
BANK_SO = 3
PREV = [max([m for m in range(n) if BANK[m] == BANK[n]], default=None) for n in range(AUX_USES)]

ST_OFF = [sum(SEQ - P * i for i in range(j)) for j in range(TT + 1)]
SRING, VRING = 3, 2
SUSES = [len(range(r, NS, SRING)) for r in range(SRING)]

PC_GN, PC_CW, PC_CB, PC_BA, PC_BX, PC_BG, PC_SP = 0, 16, 56, 66, 76, 86, 102
PCOLS = 112


def build(nc, wstream, xt, params, norms, tables, dec, kdt, slru, sconv, sret, ident,
          yt, ret_p, ret_s, lru_o, conv_p, conv_s, vscr):
    ctx = ExitStack()
    with ctx:
        def sb(name, shape, dt=F32):
            return ctx.enter_context(nc.sbuf_tensor(name, shape, dt))

        def sem(name):
            return ctx.enter_context(nc.semaphore(name))

        X = sb("residual", [P, MT, TOK])
        XH = sb("x_high", [P, MT, TOK], F32R)
        XL = sb("x_low", [P, MT, TOK], F32R)
        WR = sb("w_raw", [P, 2, UW])
        WH = sb("w_high", [P, 2, UW], F32R)
        WL = sb("w_low", [P, 2, UW], F32R)
        ACC = sb("ret_acc", [P, MT, TOK])
        COS = sb("cos_r", [P, TOK])
        SIN = sb("sin_r", [P, TOK])
        DEC = sb("decay", [P, SEQ])
        RINV = sb("rinv", [P, TOK])
        ONES = sb("ones", [P, P])
        ID = sb("ident_sb", [P, P])
        PAR = sb("params_all", [P, DEPTH, PCOLS])
        CUR = sb("params_cur", [P, PCOLS])
        NRM = sb("norms_all", [P, 2 * DEPTH + 1, MT])
        GAIN = sb("gain_cur", [P, MT])
        GAIN2 = GAIN[:, :].rearrange("p (n two) -> p two n", two=2)
        KDT = sb("kd_all", [P, HEADS, TT + 1])
        KDC = sb("kd_cur", [P, TT + 1])
        GNC = sb("gn_cur", [P, VT])
        SLR = sb("state_lru_sb", [P, LT, NS])
        SCV = sb("state_conv_sb", [P, LT, CW - 1, NS])
        LRO = sb("lru_out_sb", [P, LT, NS + 1])
        CVP = sb("conv_p_sb", [P, LT, CW - 1])
        CVS = sb("conv_s_sb", [P, LT, CW - 1, NS])
        EPST = sb("eps", [P, 1])
        TOUCH = sb("touch", [P, 1])
        KSC = sb("k_sample", [P, KT, NS])

        R_HEAD = 4 * KT * TOK + 2 * TT * DV + 2 * TT * DK + 2 * ST_OFF[TT]
        R = sb("split_scratch", [P, max(R_HEAD + 2 * VT * NS, 2 * FT * TOK)], F32R)

        def rview(off, a, b):
            return R[:, off:off + a * b].rearrange("p (a b) -> p a b", a=a)

        QH, QL, KH, KL = (rview(i * KT * TOK, KT, TOK) for i in range(4))
        o = 4 * KT * TOK
        VH, VL = rview(o, TT, DV), rview(o + TT * DV, TT, DV)
        OGH, OGL = rview(o, VT, TOK), rview(o + VT * TOK, VT, TOK)
        o += 2 * VT * TOK
        KDH, KDL = rview(o, TT, DK), rview(o + TT * DK, TT, DK)
        o += 2 * TT * DK
        STH, STL = R[:, o:o + ST_OFF[TT]], R[:, o + ST_OFF[TT]:o + 2 * ST_OFF[TT]]
        XCH, XCL, GLH, GLL = (rview(i * GT * TOK, GT, TOK) for i in range(4))
        MH, ML = rview(0, MT, TOK), rview(MT * TOK, MT, TOK)
        AH, AL = rview(0, FT, TOK), rview(FT * TOK, FT, TOK)

        sizes = [("qk", 2 * KT * TOK), ("vo", VT * TOK), ("sg", VT * TOK), ("rt", 2 * TOK),
                 ("s", SRING * KT * DV), ("t", KT * DV), ("vb", VT * TOK - KT * DV), ("stat", 3 * TOK)]
        FA = sb("scratch", [P, sum(n for _, n in sizes)])
        at, pos = {}, 0
        for name, n in sizes:
            at[name] = pos
            pos += n

        def fview(off, a, b):
            return FA[:, off:off + a * b].rearrange("p (a b) -> p a b", a=a)

        QF, KF = fview(at["qk"], KT, TOK), fview(at["qk"] + KT * TOK, KT, TOK)
        SQ4 = fview(at["t"], VT, TOK)
        VF = OF = fview(at["vo"], VT, TOK)
        SG = fview(at["sg"], VT, TOK)
        STF = FA[:, at["sg"]:at["sg"] + ST_OFF[TT]]
        RT = fview(at["rt"], 2, TOK)
        SF = fview(at["rt"], KT, DV)
        SS = FA[:, at["s"]:at["s"] + SRING * KT * DV].rearrange("p (r a b) -> p r a b", r=SRING, a=KT)
        TS = [fview(at["t"], KT, DV), fview(at["rt"], KT, DV)]
        VB = fview(at["vb"], VRING, DV)
        VS = FA[0:NS, at["t"]:at["t"] + DV]
        SUM, RSTD, SSQ = (FA[:, at["stat"] + i * TOK:at["stat"] + (i + 1) * TOK] for i in range(3))
        SQT = fview(at["rt"], 2, TOK)
        ACCL = fview(0, MT, TOK)
        o = MT * TOK
        XCF = fview(o, GT, TOK)
        o += GT * TOK
        LA, IX, YF, AF = (fview(o + 2 * i * TOK, 2, TOK) for i in range(4))
        o += 8 * TOK
        DF, HF, XR = (FA[:, o + i * TOK:o + (i + 1) * TOK] for i in range(3))
        assert o + 3 * TOK <= pos
        ZM = fview(MT * TOK, 2, TOK)
        MG = FA[:, MT * TOK + 2 * TOK:MT * TOK + 3 * TOK]
        FG = fview(0, 2, TOK)
        FF = FA[:, 2 * TOK:3 * TOK]

        PP = ctx.enter_context(nc.psum_tensor("proj", [P, 2, 2, 512], F32))
        AUX = ctx.enter_context(nc.psum_tensor("aux", [P, 4, 512], F32))

        names = ("go_pool go_pe setup_ld x_ld boot w_split w_used p_done t_free "
                 "rope_done qk_high qk_low st_high st_low aux_mm aux_free kv_high kv_low "
                 "vs_st dec_ld trig_ld silu_g t_mul s_new so_done gn_sum gn_sq gn_sd og_full og_high "
                 "og_low sfin_st state_ld xc_full xc_high xc_low gate_r gate_i th_full d_full "
                 "w_sqrt y_gelu gl_full gl_high gl_low small_rd small_st sg_m mg_full mg_high mg_low "
                 "x_full x_sq x_high_s x_low_s x_sd f_silu f_full f_high f_low sp_e ones_ok y_full y_st").split()
        s = {n: sem(n) for n in names}
        w_ld = [sem(f"w_loaded{j}") for j in range(2)]
        s_ld = [sem(f"s_loaded{j}") for j in range(SRING)]
        s_st = [sem(f"s_stored{j}") for j in range(SRING)]
        v_ld = [sem(f"vb_loaded{j}") for j in range(VRING)]

        def halves(ap):
            return ap.rearrange("p (t b) -> p t b", t=2)

        def pair_row(t, i, j):
            return t[:, :, :].rearrange("p (n two) t -> p two n t", two=2)[:, j, bass.ds(i, 1), :].rearrange(
                "p a t -> p (a t)")

        def slot(idx):
            return (TILE0 + idx) % 2

        def pp(idx):
            return PP[:, slot(idx), :, 0:HALF]

        def runs():
            base = 0
            for times, blocks in RUNS:
                if len(blocks) % 2 and times > 1:
                    times, blocks = times // 2, blocks * 2
                yield base, times, blocks
                base += times * len(blocks)

        block = ctx.enter_context(nc.Block())

        @block.sync
        def _(sp):
            with sp.Fori(0, DEPTH) as layer:
                for base, times, blocks in runs():
                    units = wstream[:, base:base + times * len(blocks)].rearrange(
                        "l (n k) p c -> l k n p c", k=len(blocks))
                    with sp.Fori(0, times) as i:
                        for k, n in enumerate(blocks):
                            u = base + k
                            sp.wait_ge(s["w_split"], layer * UNITS + (u + 1) + i * len(blocks))
                            sp.dma_start(WR[:, u % 2, 0:n * P],
                                         units[bass.ds(layer, 1), k, bass.ds(i, 1), :, 0:n * P].rearrange(
                                             "l a p c -> p (l a) c").rearrange("p a c -> p (a c)")
                                         ).then_inc(w_ld[u % 2], 16)

        @block.gpsimd
        def _(pool):
            pool.memset(ONES[:], 1.0).then_inc(s["ones_ok"], 1)

            pool.sem_inc(s["w_split"], 2)
            with pool.Fori(0, DEPTH) as layer:
                for base, times, blocks in runs():
                    with pool.Fori(0, times) as i:
                        for k, n in enumerate(blocks):
                            j, w = (base + k) % 2, slice(0, n * P)
                            u = layer * UNITS + base + k + i * len(blocks)
                            pool.wait_ge(s["w_used"], u + 2)
                            pool.wait_ge(w_ld[j], (layer * (UNITS // 2) + i * (len(blocks) // 2)) * 16
                                         + 16 * ((base + k) // 2 + 1))
                            pool.sem_inc(s["go_pool"], 1)
                            pool.tensor_scalar(WH[:, j, w], WR[:, j, w], 1.0, 0.0, ALU.mult, ALU.add)
                            pool.drain()
                            pool.tensor_tensor(WL[:, j, w], WR[:, j, w], WH[:, j, w].bitcast(F32),
                                               ALU.subtract).then_inc(s["w_split"], 1)

        @block.tensor
        def _(pe):
            def product(outs, w, blk, xs, first, last):
                started = blk
                for n, (wt, xi) in enumerate(((WH, 0), (WH, 1), (WL, 0))):
                    for out, x in zip(outs, xs):
                        m = pe.matmul(out, wt[:, w, blk * P:(blk + 1) * P], x[xi],
                                      start=first and n == 0, stop=last and n == 2)
                        if not started:
                            m.then_inc(s["w_used"], 1)
                            started = True
                return m

            def tile_begin(tb, idx):
                pe.wait_ge(s["t_free"], tb + (idx - 1))

            def unit_begin(ub, u):
                pe.wait_ge(s["w_split"], ub + (u + 3))

            def pairs(hi, lo, k):
                return [(hi[:, k, c * HALF:(c + 1) * HALF], lo[:, k, c * HALF:(c + 1) * HALF])
                        for c in range(2)]

            def whole(ub, u, tb, idx, hi, lo):
                unit_begin(ub, u)
                tile_begin(tb, idx)
                outs = [PP[:, slot(idx), c, 0:HALF] for c in range(2)]
                for k in range(MT):
                    m = product(outs, u % 2, k, pairs(hi, lo, k), k == 0, k == MT - 1)
                m.then_inc(s["p_done"], 1)

            def column_sums(tb, idx, src):
                tile_begin(tb, idx)
                for c in range(2):
                    m = pe.matmul(PP[:, slot(idx), c, 0:HALF], ONES[:], src[:, c * HALF:(c + 1) * HALF],
                                  start=True, stop=True)
                m.then_inc(s["p_done"], 1)

            pe.sem_inc(s["p_done"], 1)
            pe.sem_inc(s["w_used"], 2)
            pe.wait_ge(s["ones_ok"], 1)
            pe.wait_ge(s["setup_ld"], 16 * 4)
            pe.wait_ge(s["x_low_s"], MT)
            for c in range(2):
                m = pe.matmul(PP[:, 1, c, 0:HALF], ONES[:], SSQ[:, c * HALF:(c + 1) * HALF],
                              start=True, stop=True)
            m.then_inc(s["p_done"], 1)

            with pe.Fori(0, DEPTH) as layer:
                ub0, tb0 = layer * UNITS, layer * TILES + TILE0

                def ret_out(hh, ub, u0, tb, i0):
                    for m_ in range(MT):
                        if m_ % 2 == 0:
                            unit_begin(ub, u0 + m_ // 2)
                        tile_begin(tb, i0 + m_)
                        outs = [PP[:, slot(i0 + m_), c, 0:HALF] for c in range(2)]
                        for k in range(VT):
                            if m_ == 0:
                                pe.wait_ge(s["og_low"], hh * VT + (k + 1 - VT))
                            m = product(outs, (u0 + m_ // 2) % 2, (m_ % 2) * VT + k, pairs(OGH, OGL, k),
                                        k == 0, k == VT - 1)
                        m.then_inc(s["p_done"], 1)

                def one_head(head, first):
                    hh = layer * HEADS + head
                    if first:
                        ub, tb, uv, v0 = ub0, tb0, QK, QK
                    else:
                        ub, tb = ub0 - MT // 2 + head * U_HEAD, tb0 - MT + head * T_HEAD
                        uv, v0 = QK + MT // 2, QK + MT
                    for i in range(QK):
                        whole(ub, i, tb, i, XH, XL)
                    if not first:
                        ret_out(hh, ub, QK, tb, QK)
                    for i in range(VT):
                        whole(ub, uv + i, tb, v0 + i, XH, XL)
                    pe.wait_ge(s["qk_low"], hh * 2 + 2)

                    def aux_begin(n):
                        if PREV[n] is not None:
                            pe.wait_ge(s["aux_free"], hh * AUX_USES + (PREV[n] + 1))

                    for j in range(TT):
                        aux_begin(N_SC + j)
                        for d in range(KT):
                            for n, (a, b) in enumerate(((KH, QH), (KH, QL), (KL, QH))):
                                m = pe.matmul(AUX[:, BANK[N_SC + j], 0:SEQ - j * P],
                                              a[:, d, j * P:(j + 1) * P], b[:, d, j * P:SEQ],
                                              start=d == n == 0, stop=d == KT - 1 and n == 2)
                        m.then_inc(s["aux_mm"], 1)
                    for i in range(TT // 2):
                        aux_begin(N_TK + i)
                        for j in range(2):
                            for d in range(KT):
                                m = pe.transpose(
                                    AUX[:, BANK[N_TK + i], (j * KT + d) * P:(j * KT + d + 1) * P],
                                    KF[:, d, (2 * i + j) * P:(2 * i + j + 1) * P], ID[:])
                        m.then_inc(s["aux_mm"], 1)
                    pe.wait_ge(s["t_free"], tb + (v0 + VT))
                    aux_begin(N_VS)
                    for e in range(VT):
                        m = pe.transpose(AUX[0:NS, BANK[N_VS], e * P:(e + 1) * P],
                                         VF[:, e, SEQ:TOK], ID[:])
                    m.then_inc(s["aux_mm"], 1)

                    def v_by_token(j):
                        aux_begin(N_TV + j)
                        for e in range(VT):
                            m = pe.transpose(AUX[:, BANK[N_TV + j], e * P:(e + 1) * P],
                                             VF[:, e, j * P:(j + 1) * P], ID[:])
                        m.then_inc(s["aux_mm"], 1)

                    def gate(e):
                        whole(ub, uv + VT + UG[e], tb, v0 + VT + TG[e], XH, XL)

                    def attend(e):
                        aux_begin(N_AT + e)
                        for j in range(TT):
                            for n, (a, b) in enumerate(((VH, STH), (VH, STL), (VL, STH))):
                                m = pe.matmul(AUX[:, BANK[N_AT + e], j * P:SEQ],
                                              a[:, j, e * P:(e + 1) * P],
                                              b[:, ST_OFF[j]:ST_OFF[j + 1]],
                                              start=j == n == 0, stop=j == TT - 1 and n == 2)
                        m.then_inc(s["aux_mm"], 1)

                    def final_state(d):
                        aux_begin(N_ST + d)
                        for j in range(TT):
                            for n, (a, b) in enumerate(((KDH, VH), (KDH, VL), (KDL, VH))):
                                m = pe.matmul(AUX[:, BANK[N_ST + d], :], a[:, j, d * P:(d + 1) * P],
                                              b[:, j, :], start=j == n == 0,
                                              stop=j == TT - 1 and n == 2)
                        m.then_inc(s["aux_mm"], 1)

                    def sample_out(b):
                        pe.wait_ge(s["s_new"], hh * NS + (b + 1))
                        for e in range(VT):
                            for d in range(KT):
                                m = pe.matmul(AUX[:, BANK_SO, e * NS + b:e * NS + b + 1],
                                              SS[:, b % SRING, d, e * P:(e + 1) * P],
                                              QF[:, d, SEQ + b:SEQ + b + 1],
                                              start=b == e == d == 0, stop=d == KT - 1,
                                              skip_group_check=True)
                        m.then_inc(s["so_done"], 1)

                    v_by_token(0)
                    gate(0)
                    for j in range(1, TT):
                        v_by_token(j)
                    gate(1)
                    sample_out(0)
                    gate(3)
                    sample_out(1)
                    sample_out(2)
                    pe.wait_ge(s["kv_low"], hh * (2 * TT) + 2 * TT)
                    pe.wait_ge(s["st_low"], hh * TT + TT)
                    attend(0)
                    for e in range(1, VT):
                        attend(e)
                        sample_out(2 + e)
                    sample_out(NS - 2)
                    sample_out(NS - 1)
                    final_state(0)
                    pe.wait_ge(s["gn_sum"], hh * 2 + 1)
                    column_sums(tb, v0 + VT + T_MEAN, SUM)
                    gate(2)
                    final_state(1)
                    pe.wait_ge(s["gn_sum"], hh * 2 + 2)
                    column_sums(tb, v0 + VT + T_VAR, SUM)

                one_head(0, True)
                with pe.Fori(1, HEADS) as head:
                    one_head(head, False)
                ret_out((layer + 1) * HEADS, ub0, B_LRU - MT // 2, tb0, C_LRU - MT)

                for g in range(GROUPS):
                    bu, tb = B_LRU + g * U_LRU, tb0 + (C_LRU + g * T_LRU)
                    cb = layer * LT + g * GT
                    for t in range(GT):
                        whole(ub0, bu + t, tb, t, XH, XL)
                    for t in range(GT):
                        whole(ub0, bu + GT + 2 * t, tb, GT + 3 * t, XH, XL)
                        u = bu + GT + 2 * t + 1
                        unit_begin(ub0, u)
                        pe.wait_ge(s["xc_low"], cb + (BAND[t][-1] + 1))
                        for w in range(2):
                            idx = GT + 3 * t + 1 + w
                            tile_begin(tb, idx)
                            outs = [PP[:, slot(idx), c, 0:HALF] for c in range(2)]
                            for n, k in enumerate(BAND[t]):
                                m = product(outs, u % 2, w * len(BAND[t]) + n, pairs(XCH, XCL, k),
                                            n == 0, n == len(BAND[t]) - 1)
                            m.then_inc(s["p_done"], 1)
                    pe.wait_ge(s["gl_low"], cb + GT)
                    pe.sem_inc(s["go_pe"], 1)
                    with pe.Fori(0, MT // 2) as mm:
                        for j in range(2):
                            u, idx = bu + 3 * GT + j, 4 * GT + j
                            pe.wait_ge(s["w_split"], ub0 + (u + 3) + 2 * mm)
                            pe.wait_ge(s["t_free"], tb + (idx - 1) + 2 * mm)
                            outs = [PP[:, slot(idx), c, 0:HALF] for c in range(2)]
                            for k in range(GT):
                                m = product(outs, u % 2, k, pairs(GLH, GLL, k), k == 0, k == GT - 1)
                            m.then_inc(s["p_done"], 1)

                with pe.Fori(0, MT) as i:
                    for j in range(2):
                        whole(ub0 + 2 * i, B_MERGE + j, tb0 + 2 * i, C_MERGE + j, XH, XL)

                pe.wait_ge(s["mg_low"], layer * MT + MT)
                pe.sem_inc(s["go_pe"], 1)
                with pe.Fori(0, MT // 2) as i:
                    for j in range(2):
                        whole(ub0 + 2 * i, B_WO + j, tb0 + 2 * i, C_WO + j, MH, ML)
                pe.wait_ge(s["x_low_s"], layer * (2 * MT) + 2 * MT)
                column_sums(tb0, C_NORM1, SSQ)

                for f in range(FH):
                    bu, bt = B_FFN + f * U_FFN, C_FFN + f * T_FFN
                    with pe.Fori(0, FT) as i:
                        for j in range(2):
                            whole(ub0 + 2 * i, bu + j, tb0 + 2 * i, bt + j, XH, XL)
                    pe.wait_ge(s["f_low"], layer * (FH * FT) + (f + 1) * FT)
                    pe.sem_inc(s["go_pe"], 1)
                    with pe.Fori(0, MT // 2) as i:
                        for j in range(2):
                            idx = bt + 2 * FT + j
                            pe.wait_ge(s["t_free"], tb0 + (idx - 1) + 2 * i)
                            outs = [PP[:, slot(idx), c, 0:HALF] for c in range(2)]
                            k = 0
                            for v in range(2):
                                u = bu + 2 * FT + 2 * j + v
                                pe.wait_ge(s["w_split"], ub0 + (u + 3) + 4 * i)
                                for b in range(K_DOWN[v]):
                                    m = product(outs, u % 2, b, pairs(AH, AL, k), k == 0, k == FT - 1)
                                    k += 1
                            m.then_inc(s["p_done"], 1)
                pe.wait_ge(s["x_low_s"], layer * (2 * MT) + 3 * MT)
                column_sums(tb0, C_NORM2, SSQ)

        @block.vector
        def _(dve):
            tt, ts, stt = dve.tensor_tensor, dve.tensor_scalar, dve.scalar_tensor_tensor

            def done(tb, idx):
                dve.wait_ge(s["p_done"], tb + (idx + 1))

            def norm_low(x, xh, xl, gain, j, first):
                if first:
                    ts(SSQ, SQT[:, j, :], 1.0, None, ALU.mult)
                else:
                    tt(SSQ, SSQ, SQT[:, j, :], ALU.add)
                return stt(xl, x, gain, xh.bitcast(F32), ALU.mult, ALU.subtract)

            def root_inverse(dst):
                return dve.reciprocal(dst, dst)

            NL = DEPTH * LT
            lam = RT[:, 0, 0:NL].rearrange("p (d c) -> p d c", d=DEPTH)
            e_, z_, z2, acc = (RT[:, 0, NL * i:NL * (i + 1)] for i in range(1, 5))
            dve.sem_inc(s["t_free"], 1)
            dve.memset(EPST[:], EPS).then_inc(s["boot"], 1)
            dve.wait_ge(s["setup_ld"], 16 * 4)
            dve.tensor_copy(lam, PAR[:, :, PC_SP:PC_SP + LT]).then_inc(s["sp_e"], 1)
            dve.wait_ge(s["sp_e"], 3)
            ts(z_, e_, 2.0, None, ALU.add)
            dve.drain()
            dve.reciprocal(z_, z_)
            dve.drain()
            tt(z_, z_, e_, ALU.mult)
            dve.drain()
            tt(z2, z_, z_, ALU.mult)
            dve.memset(acc, 1.0 / 19)
            dve.drain()
            for n in range(17, 0, -2):
                tt(acc, acc, z2, ALU.mult)
                dve.drain()
                ts(acc, acc, 1.0 / n, None, ALU.add)
                dve.drain()
            tt(acc, acc, z_, ALU.mult)
            ts(e_, RT[:, 0, 0:NL], -8.0, 0.0, ALU.mult, ALU.max)
            dve.drain()
            stt(PAR[:, :, PC_SP:PC_SP + LT], acc.rearrange("p (d c) -> p d c", d=DEPTH), 16.0,
                e_.rearrange("p (d c) -> p d c", d=DEPTH), ALU.mult, ALU.add)
            dve.tensor_copy(GAIN[:], NRM[:, 0, :])
            dve.drain().then_inc(s["boot"], 1)
            dve.wait_ge(s["x_ld"], 16)
            for m in range(MT):
                dve.wait_ge(s["x_high_s"], m + 1)
                norm_low(X[:, m, :], XH[:, m, :], XL[:, m, :], GAIN[:, m:m + 1], m % 2, m == 0
                         ).then_inc(s["x_low_s"], 1)
                dve.drain()
            dve.wait_ge(s["x_sd"], 1)
            dve.drain()
            root_inverse(RINV[:]).then_inc(s["t_free"], 1)

            with dve.Fori(0, DEPTH) as layer:
                tb0 = layer * TILES + TILE0
                nb = layer * (2 * MT)
                dve.drain()
                dve.tensor_copy(CUR[:], PAR[:, bass.ds(layer, 1), :].rearrange("p a n -> p (a n)"))
                dve.memset(ACC[:], 0.0)
                dve.wait_ge(s["trig_ld"], layer * 32 + 32)
                tt(COS[:], COS[:], RINV[:], ALU.mult)
                tt(SIN[:], SIN[:], RINV[:], ALU.mult)

                def ret_tail(hh):
                    dve.wait_ge(s["gn_sd"], hh)
                    root_inverse(RSTD).then_inc(s["t_free"], 1)
                    dve.drain()
                    for e in range(VT):
                        tt(SG[:, e, :], SG[:, e, :], RSTD, ALU.mult).then_inc(s["og_full"], 1)
                    dve.drain()

                def og_split(hh):
                    for e in range(VT):
                        dve.wait_ge(s["og_high"], hh * VT + (e + 1 - VT))
                        stt(OGL[:, e, :], SG[:, e, :], GNC[:, e:e + 1], OGH[:, e, :].bitcast(F32),
                            ALU.mult, ALU.subtract).then_inc(s["og_low"], 1)

                def ret_add(tb, i0, m_):
                    done(tb, i0 + m_)
                    tt(halves(ACC[:, m_, :]), pp(i0 + m_), halves(ACC[:, m_, :]), ALU.add
                       ).then_inc(s["t_free"], 1)

                def one_head(head, first):
                    hh = layer * HEADS + head
                    tb, v0 = (tb0, QK) if first else (tb0 - MT + head * T_HEAD, QK + MT)
                    g0 = v0 + VT
                    dve.drain()
                    dve.tensor_copy(KDC[:], KDT[:, bass.ds(head, 1), :].rearrange("p a n -> p (a n)"))
                    if not first:
                        ret_tail(hh)
                    dve.wait_ge(s["sfin_st"], hh * 16 + 16)

                    def low(dst, src, hi, scale, n):
                        dve.wait_ge(s["qk_high"], hh * 2 + n)
                        stt(dst, src, scale, hi.bitcast(F32), ALU.mult, ALU.subtract
                            ).then_inc(s["qk_low"], 1)

                    def rotate(n, dst, meanwhile):
                        done(tb, n)
                        tt(halves(dst[:, 0, :]), pp(n), halves(COS[:]), ALU.mult)
                        tt(halves(dst[:, 1, :]), pp(n), halves(SIN[:]), ALU.mult).then_inc(s["t_free"], 1)
                        meanwhile()
                        done(tb, n + 1)
                        tt(halves(RT[:, 0, :]), pp(n + 1), halves(SIN[:]), ALU.mult)
                        tt(halves(RT[:, 1, :]), pp(n + 1), halves(COS[:]), ALU.mult).then_inc(s["t_free"], 1)
                        dve.drain()
                        tt(dst[:, 0, :], dst[:, 0, :], RT[:, 0, :], ALU.subtract)
                        tt(dst[:, 1, :], dst[:, 1, :], RT[:, 1, :], ALU.add).then_inc(s["rope_done"], 1)
                        dve.drain()

                    def new_gain():
                        if not first:
                            og_split(hh)
                            dve.drain()
                        dve.tensor_copy(GNC[:], CUR[:, bass.ds(head * VT + PC_GN, VT)])

                    rotate(0, QF, new_gain)
                    rotate(KT, KF, lambda: low(QL, QF, QH, 1.0, 1))
                    ts(KSC[:], KF[:, :, SEQ:TOK], DK ** -0.5, None, ALU.mult)
                    if not first:
                        for m_ in range(MT):
                            ret_add(tb, QK, m_)
                            if m_ == 0:
                                low(KL, KF, KH, DK ** -0.5, 2)
                    for e in range(VT):
                        done(tb, v0 + e)
                        tt(halves(VF[:, e, :]), pp(v0 + e), halves(RINV[:]), ALU.mult
                           ).then_inc(s["t_free"], 1)
                        if first and e == 0:
                            low(KL, KF, KH, DK ** -0.5, 2)

                    def aux(n):
                        dve.wait_ge(s["aux_mm"], hh * AUX_USES + (n + 1))

                    dve.wait_ge(s["dec_ld"], hh * 16 + 16)
                    for j in range(TT):
                        aux(N_SC + j)
                        tt(STF[:, ST_OFF[j]:ST_OFF[j + 1]], AUX[:, BANK[N_SC + j], 0:SEQ - j * P],
                           DEC[:, 0:SEQ - j * P], ALU.mult).then_inc(s["aux_free"], 1)
                    for i in range(TT // 2):
                        dve.wait_ge(s["kv_high"], hh * 2 * TT + 2 * (i + 1))
                        for j in range(2 * i, 2 * i + 2):
                            stt(KDL[:, j, :], AUX[:, BANK[N_TK + i], (j % 2) * DK:(j % 2 + 1) * DK],
                                KDC[:, j:j + 1], KDH[:, j, :].bitcast(F32), ALU.mult, ALU.subtract
                                ).then_inc(s["kv_low"], 1)
                        dve.drain().then_inc(s["aux_free"], 1)
                    aux(N_VS)
                    ts(VS, AUX[0:NS, BANK[N_VS], :], 1.0, None, ALU.mult).then_inc(s["aux_free"], 1)

                    def v_low(j):
                        dve.wait_ge(s["kv_high"], hh * 2 * TT + (TT + j + 1))
                        tt(VL[:, j, :], AUX[:, BANK[N_TV + j], :], VH[:, j, :].bitcast(F32), ALU.subtract
                           ).then_inc(s["kv_low"], 1)
                        dve.drain().then_inc(s["aux_free"], 1)

                    v_low(0)
                    for j in range(TT):
                        dve.wait_ge(s["st_high"], hh * TT + (j + 1))
                        w = slice(ST_OFF[j], ST_OFF[j + 1])
                        tt(STL[:, w], STF[:, w], STH[:, w].bitcast(F32), ALU.subtract
                           ).then_inc(s["st_low"], 1)
                    for j in range(1, TT):
                        v_low(j)

                    def gate(e):
                        done(tb, g0 + TG[e])
                        tt(halves(SG[:, e, :]), pp(g0 + TG[e]), halves(RINV[:]), ALU.mult
                           ).then_inc(s["t_free"], 1)

                    def new_state(b):
                        r = b % SRING
                        dve.wait_ge(s_ld[r], hh * (16 * SUSES[r]) + 16 * (b // SRING + 1))
                        dve.wait_ge(s["t_mul"], hh * NS + (b + 1))
                        stt(SS[:, r], SS[:, r], KDC[:, TT:TT + 1], TS[b % 2], ALU.mult, ALU.add
                            ).then_inc(s["s_new"], 1)

                    def attended(e):
                        aux(N_AT + e)
                        ts(OF[:, e, 0:SEQ], AUX[:, BANK[N_AT + e], :], 1.0, None, ALU.mult
                           ).then_inc(s["aux_free"], 1)

                    def final_state(d):
                        aux(N_ST + d)
                        ts(SF[:, d, :], AUX[:, BANK[N_ST + d], :], 1.0, None, ALU.mult
                           ).then_inc(s["aux_free"], 1)

                    gate(0)
                    new_state(0)
                    gate(1)
                    new_state(1)
                    new_state(2)
                    gate(3)
                    new_state(3)
                    for e in range(VT):
                        attended(e)
                        new_state(VT + e)
                    dve.wait_ge(s["so_done"], hh * NS + NS)
                    ts(OF[:, :, SEQ:TOK], AUX[:, BANK_SO, 0:VT * NS].rearrange("p (e b) -> p e b", e=VT),
                       1.0, None, ALU.mult)
                    dve.drain()
                    dve.tensor_reduce(SUM, OF.rearrange("p e t -> p t e"), AX.X, ALU.add
                                      ).then_inc(s["gn_sum"], 1)
                    final_state(0)
                    done(tb, g0 + T_MEAN)
                    for e in range(VT):
                        m = stt(halves(OF[:, e, :]), pp(g0 + T_MEAN), -1.0 / DV, halves(OF[:, e, :]),
                                ALU.mult, ALU.add)
                    m.then_inc(s["t_free"], 1)
                    dve.wait_ge(s["gn_sq"], hh + 1)
                    dve.tensor_reduce(SUM, SQ4.rearrange("p e t -> p t e"), AX.X, ALU.add
                                      ).then_inc(s["gn_sum"], 1)
                    gate(2)
                    final_state(1)
                    dve.wait_ge(s["silu_g"], hh * VT + VT)
                    tt(SG, SG, OF, ALU.mult)

                one_head(0, True)
                with dve.Fori(1, HEADS) as head:
                    one_head(head, False)
                dve.drain()
                ret_tail((layer + 1) * HEADS)
                og_split((layer + 1) * HEADS)
                for m_ in range(MT):
                    ret_add(tb0, C_LRU - MT, m_)

                dve.drain()
                dve.wait_ge(s["sfin_st"], (layer + 1) * (16 * HEADS) + 16)
                for r in range(SRING):
                    dve.wait_ge(s_st[r], (layer + 1) * (16 * SUSES[r] * HEADS) + 16)
                dve.wait_ge(s["state_ld"], layer * 32 + 32)
                dve.wait_ge(s["small_st"], layer * 48 + 16)
                for g in range(GROUPS):
                    tb = tb0 + (C_LRU + g * T_LRU)
                    cb = layer * LT + g * GT

                    if g:
                        dve.drain()

                    def low_xc(t):
                        dve.wait_ge(s["xc_high"], cb + (t + 1))
                        tt(XCL[:, t, :], XCF[:, t, :], XCH[:, t, :].bitcast(F32), ALU.subtract
                           ).then_inc(s["xc_low"], 1)

                    for t in range(GT):
                        c = g * GT + t

                        def cw(j):
                            return CUR[:, PC_CW + c * CW + j:PC_CW + c * CW + j + 1]

                        done(tb, t)
                        tt(halves(XR), pp(t), halves(RINV[:]), ALU.mult).then_inc(s["t_free"], 1)
                        dve.drain()
                        ts(XCF[:, t, :], XR, cw(CW - 1), CUR[:, PC_CB + c:PC_CB + c + 1],
                           ALU.mult, ALU.add)
                        dve.tensor_copy(CVP[:, c, :], XR[:, SEQ - CW + 1:SEQ])
                        dve.tensor_copy(CVS[:, c, 0:CW - 2, :], SCV[:, c, 1:CW - 1, :])
                        dve.tensor_copy(CVS[:, c, CW - 2, :], XR[:, SEQ:TOK])
                        for j in range(CW - 1):
                            d = CW - 1 - j
                            dve.drain()
                            stt(XCF[:, t, d:SEQ], XR[:, 0:SEQ - d], cw(j), XCF[:, t, d:SEQ],
                                ALU.mult, ALU.add)
                            m = stt(XCF[:, t, SEQ:TOK], SCV[:, c, j, :], cw(j), XCF[:, t, SEQ:TOK],
                                    ALU.mult, ALU.add)
                        m.then_inc(s["xc_full"], 1)
                        dve.drain()
                        if t:
                            low_xc(t - 1)
                    low_xc(GT - 1)

                    def stage_a(t):
                        b, c = t % 2, g * GT + t
                        dve.drain()
                        done(tb, GT + 3 * t)
                        tt(halves(YF[:, b, :]), pp(GT + 3 * t), halves(RINV[:]), ALU.mult
                           ).then_inc(s["t_free"], 1)
                        dve.wait_ge(s["gate_r"], cb + (t + 1))
                        ts(LA[:, b, :], LA[:, b, :], CUR[:, PC_SP + c:PC_SP + c + 1], None, ALU.mult
                           ).then_inc(s["t_free"], 1)
                        dve.wait_ge(s["gate_i"], cb + (t + 1))
                        tt(IX[:, b, :], IX[:, b, :], XCF[:, t, :], ALU.mult).then_inc(s["t_free"], 1)

                    def stage_b(t):
                        b, c = t % 2, g * GT + t
                        dve.wait_ge(s["th_full"], cb + (t + 1))
                        ts(DF, LA[:, b, :], 1.0, None, ALU.add)
                        dve.drain()
                        dve.reciprocal(DF, DF)
                        dve.drain()
                        stt(DF, LA[:, b, :], 2.0, DF, ALU.mult, ALU.mult).then_inc(s["d_full"], 1)
                        dve.wait_ge(s["w_sqrt"], cb + (t + 1))
                        tt(IX[:, b, :], IX[:, b, :], DF, ALU.mult)
                        tt(HF[:, SEQ:TOK], AF[:, b, SEQ:TOK], SLR[:, c, :], ALU.mult)
                        dve.drain()
                        dve.tensor_tensor_scan(HF[:, 0:SEQ], AF[:, b, 0:SEQ], IX[:, b, 0:SEQ], 0.0,
                                               ALU.mult, ALU.add)
                        tt(HF[:, SEQ:TOK], HF[:, SEQ:TOK], IX[:, b, SEQ:TOK], ALU.add)
                        dve.drain()
                        dve.tensor_copy(LRO[:, c, :], HF[:, SEQ - 1:TOK])
                        dve.wait_ge(s["y_gelu"], cb + (t + 1))
                        tt(YF[:, b, :], YF[:, b, :], HF, ALU.mult).then_inc(s["gl_full"], 1)
                        dve.wait_ge(s["gl_high"], cb + (t + 1))
                        tt(GLL[:, t, :], YF[:, b, :], GLH[:, t, :].bitcast(F32), ALU.subtract
                           ).then_inc(s["gl_low"], 1)

                    for t in range(GT + 1):
                        if t < GT:
                            stage_a(t)
                        if t:
                            stage_b(t - 1)
                    if g == GROUPS - 1:
                        dve.drain().then_inc(s["small_rd"], 1)
                    with dve.Fori(0, MT // 2) as mm:
                        for j in range(2):
                            idx = 4 * GT + j
                            dve.wait_ge(s["p_done"], tb + (idx + 1) + 2 * mm)
                            dst = halves(pair_row(ACCL, mm, j))
                            if g == 0:
                                ts(dst, pp(idx), 1.0, None, ALU.mult).then_inc(s["t_free"], 1)
                            else:
                                tt(dst, pp(idx), dst, ALU.add).then_inc(s["t_free"], 1)

                with dve.Fori(0, MT) as mm:
                    dve.drain()
                    for j in range(2):
                        idx = C_MERGE + j
                        dve.wait_ge(s["p_done"], tb0 + (idx + 1) + 2 * mm)
                        tt(halves(ZM[:, j, :]), pp(idx), halves(RINV[:]), ALU.mult).then_inc(s["t_free"], 1)
                    dve.wait_ge(s["sg_m"], layer * (2 * MT) + 2 + 2 * mm)
                    tt(ZM[:, 0, :], ZM[:, 0, :], ACC[:, bass.ds(mm, 1), :].rearrange("p a t -> p (a t)"), ALU.mult)
                    tt(ZM[:, 1, :], ZM[:, 1, :], ACCL[:, bass.ds(mm, 1), :].rearrange("p a t -> p (a t)"), ALU.mult)
                    dve.drain()
                    tt(MG, ZM[:, 0, :], ZM[:, 1, :], ALU.add).then_inc(s["mg_full"], 1)
                    dve.wait_ge(s["mg_high"], layer * MT + 1 + mm)
                    tt(ML[:, bass.ds(mm, 1), :].rearrange("p a t -> p (a t)"), MG,
                       MH[:, bass.ds(mm, 1), :].rearrange("p a t -> p (a t)").bitcast(F32),
                       ALU.subtract).then_inc(s["mg_low"], 1)

                def residual(tbi, idx, i, j, count, normed):
                    dve.wait_ge(s["p_done"], tbi + (idx + 1) + 2 * i)
                    xr = halves(pair_row(X, i, j))
                    m = tt(xr, pp(idx), xr, ALU.add)
                    m.then_inc(s["t_free"], 1)
                    if normed:
                        dve.drain().then_inc(s["x_full"], 1)
                        dve.wait_ge(s["x_high_s"], count + 2 * i)
                        x1, h1, l1 = (pair_row(v, i, j) for v in (X, XH, XL))
                        tt(SSQ, SSQ, SQT[:, j, :], ALU.add)
                        stt(l1, x1, GAIN2[:, j, bass.ds(i, 1)], h1.bitcast(F32), ALU.mult,
                            ALU.subtract).then_inc(s["x_low_s"], 1)
                        dve.drain()

                def next_norm(idx, n):
                    dve.drain()
                    dve.memset(SSQ, 0.0)
                    dve.tensor_copy(GAIN[:], NRM[:, bass.ds(layer * 2 + n, 1), :].rearrange("p a n -> p (a n)"))
                    dve.drain()

                next_norm(0, 1)
                with dve.Fori(0, MT // 2) as i:
                    for j in range(2):
                        residual(tb0, C_WO + j, i, j, nb + MT + j + 1, True)
                dve.wait_ge(s["x_sd"], layer * 2 + 2)
                root_inverse(RINV[:]).then_inc(s["t_free"], 1)

                for f in range(FH):
                    bt = C_FFN + f * T_FFN
                    fb = layer * (FH * FT) + f * FT
                    dve.drain()
                    with dve.Fori(0, FT) as i:
                        for j in range(2):
                            idx = bt + j
                            dve.wait_ge(s["p_done"], tb0 + (idx + 1) + 2 * i)
                            tt(halves(FG[:, j, :]), pp(idx), halves(RINV[:]), ALU.mult
                               ).then_inc(s["t_free"], 1)
                        dve.drain()
                        dve.wait_ge(s["f_silu"], fb + 1 + i)
                        tt(FF, FG[:, 0, :], FG[:, 1, :], ALU.mult).then_inc(s["f_full"], 1)
                        dve.wait_ge(s["f_high"], fb + 1 + i)
                        tt(AL[:, bass.ds(i, 1), :].rearrange("p a t -> p (a t)"), FF,
                           AH[:, bass.ds(i, 1), :].rearrange("p a t -> p (a t)").bitcast(F32),
                           ALU.subtract).then_inc(s["f_low"], 1)
                    if f == FH - 1:
                        next_norm(1, 2)
                    with dve.Fori(0, MT // 2) as i:
                        for j in range(2):
                            residual(tb0, bt + 2 * FT + j, i, j, nb + 2 * MT + j + 1, f == FH - 1)
                dve.wait_ge(s["x_sd"], layer * 2 + 3)
                root_inverse(RINV[:]).then_inc(s["t_free"], 1)

            dve.drain()
            for m in range(MT):
                stt(ACC[:, m, :], X[:, m, :], GAIN[:, m:m + 1], RINV[:], ALU.mult, ALU.mult
                    ).then_inc(s["y_full"], 1)

        @block.scalar
        def _(act):
            copy, A = ACT.Copy, act.activation

            def apart():
                act.wait_ge(s["boot"], 1)

            for st in (*s_st, s["sfin_st"], s["small_st"]):
                act.sem_inc(st, 16)
            act.dma_start(PAR[:], params).then_inc(s["setup_ld"], 16)
            act.dma_start(NRM[:], norms).then_inc(s["setup_ld"], 16)
            act.dma_start(KDT[:], kdt).then_inc(s["setup_ld"], 16)
            act.dma_start(ID[:], ident).then_inc(s["setup_ld"], 16)
            act.dma_start(X[:], xt).then_inc(s["x_ld"], 16)
            NL = DEPTH * LT
            act.wait_ge(s["sp_e"], 1)
            A(RT[:, 0, NL:2 * NL], RT[:, 0, 0:NL], ACT.Abs).then_inc(s["sp_e"], 1)
            act.wait_ge(s["sp_e"], 2)
            A(RT[:, 0, NL:2 * NL], RT[:, 0, NL:2 * NL], ACT.Exp, scale=-1.0).then_inc(s["sp_e"], 1)

            act.wait_ge(s["x_ld"], 16)
            act.wait_ge(s["boot"], 2)
            for m in range(MT):
                if m >= 2:
                    act.wait_ge(s["x_low_s"], m - 1)
                A(SQT[:, m % 2, :], X[:, m, :], ACT.Square)
                A(XH[:, m, :], X[:, m, :], copy, scale=GAIN[:, m:m + 1]).then_inc(s["x_high_s"], 1)
                act.drain()
            act.wait_ge(s["p_done"], TILE0)
            A(halves(RINV[:]), PP[:, 1, :, 0:HALF], ACT.Sqrt, bias=EPST[:], scale=1.0 / DM
              ).then_inc(s["x_sd"], 1)

            with act.Fori(0, DEPTH) as layer:
                tb0 = layer * TILES + TILE0
                nb = layer * (2 * MT)
                act.dma_start(COS[:], tables[0]).then_inc(s["trig_ld"], 16)
                act.dma_start(SIN[:], tables[1]).then_inc(s["trig_ld"], 16)
                act.dma_start(SLR[:], slru[bass.ds(layer, 1)].rearrange("a p c b -> (a p) c b")
                              ).then_inc(s["state_ld"], 16)
                act.dma_start(SCV[:], sconv[bass.ds(layer, 1)].rearrange("a p c j b -> (a p) c j b")
                              ).then_inc(s["state_ld"], 16)

                def ret_tail(hh, tb, var):
                    act.wait_ge(s["p_done"], tb + (var + 1))
                    A(halves(RSTD), pp(var), ACT.Sqrt, bias=EPST[:], scale=1.0 / DV
                      ).then_inc(s["gn_sd"], 1)
                    for e in range(VT):
                        act.wait_ge(s["og_full"], hh * VT + (e + 1 - VT))
                        A(OGH[:, e, :], SG[:, e, :], copy, scale=GNC[:, e:e + 1]).then_inc(s["og_high"], 1)

                def one_head(head, first):
                    hh = layer * HEADS + head
                    tb, v0 = (tb0, QK) if first else (tb0 - MT + head * T_HEAD, QK + MT)
                    g0 = v0 + VT

                    def state(dram, b):
                        return dram[bass.ds(layer, 1), b, bass.ds(head, 1)].rearrange(
                            "l h (d p) e -> p (l h d) e", p=P)

                    def load_state(b):
                        act.dma_start(SS[:, b % SRING], state(sret, b)).then_inc(s_ld[b % SRING], 16)

                    def load_vb(b):
                        act.dma_start(VB[:, b % VRING, :],
                                      vscr[b:b + 1, :].broadcast_to([P, DV])
                                      ).then_inc(v_ld[b % VRING], 16)

                    act.dma_start(DEC[:], dec[bass.ds(head, 1)].rearrange("a p n -> (a p) n")
                                  ).then_inc(s["dec_ld"], 16)
                    if not first:
                        ret_tail(hh, tb, -1)
                    for r in range(SRING):
                        act.wait_ge(s_st[r], hh * (16 * SUSES[r]) + 16)
                        load_state(r)
                    for n, (hi, full, scale) in enumerate(((QH, QF, 1.0), (KH, KF, DK ** -0.5))):
                        act.wait_ge(s["rope_done"], hh * 2 + (n + 1))
                        A(hi, full, copy, scale=scale).then_inc(s["qk_high"], 1)
                    for i in range(TT // 2):
                        act.wait_ge(s["aux_mm"], hh * AUX_USES + (N_TK + i + 1))
                        for j in range(2 * i, 2 * i + 2):
                            A(KDH[:, j, :], AUX[:, BANK[N_TK + i], (j % 2) * DK:(j % 2 + 1) * DK], copy,
                              scale=KDC[:, j:j + 1]).then_inc(s["kv_high"], 1)
                    act.wait_ge(s["aux_free"], hh * AUX_USES + (N_VS + 1))
                    act.dma_start(vscr[:, :], VS).then_inc(s["vs_st"], 16)

                    def v_high(j):
                        act.wait_ge(s["aux_mm"], hh * AUX_USES + (N_TV + j + 1))
                        A(VH[:, j, :], AUX[:, BANK[N_TV + j], :], copy).then_inc(s["kv_high"], 1)

                    v_high(0)
                    for j in range(TT):
                        w = slice(ST_OFF[j], ST_OFF[j + 1])
                        A(STH[:, w], STF[:, w], copy).then_inc(s["st_high"], 1)
                    act.wait_ge(s["vs_st"], hh * 16 + 16)
                    for b in range(VRING):
                        load_vb(b)
                    for j in range(1, TT):
                        v_high(j)

                    def silu(e):
                        act.wait_ge(s["t_free"], tb + (g0 + TG[e] + 1))
                        A(SG[:, e, :], SG[:, e, :], ACT.Silu).then_inc(s["silu_g"], 1)

                    for b in range(NS):
                        act.wait_ge(v_ld[b % VRING], hh * (16 * NS // VRING) + 16 * (b // VRING + 1))
                        if b >= 2:
                            act.wait_ge(s["s_new"], hh * NS + (b - 1))
                        A(TS[b % 2][:, 0, :], VB[:, b % VRING, :], copy, scale=KSC[:, 0, b:b + 1])
                        A(TS[b % 2][:, 1, :], VB[:, b % VRING, :], copy, scale=KSC[:, 1, b:b + 1]
                          ).then_inc(s["t_mul"], 1)
                        if b + VRING < NS:
                            act.wait_ge(s["t_mul"], hh * NS + (b + 1))
                            load_vb(b + VRING)
                        if b:
                            act.wait_ge(s["s_new"], hh * NS + b)
                            act.dma_start(state(ret_s, b - 1), SS[:, (b - 1) % SRING]
                                          ).then_inc(s_st[(b - 1) % SRING], 16)
                        if b in (1, 2, 3):
                            silu((0, 1, 3)[b - 1])
                        if b >= 2 and b + 1 < NS:
                            r = (b - 2) % SRING
                            act.wait_ge(s_st[r], hh * (16 * SUSES[r]) + 16 * ((b - 2) // SRING + 2))
                            act.wait_ge(s["so_done"], hh * NS + (b - 1))
                            load_state(b + 1)
                    act.wait_ge(s["s_new"], hh * NS + NS)
                    act.dma_start(state(ret_s, NS - 1), SS[:, (NS - 1) % SRING]
                                  ).then_inc(s_st[(NS - 1) % SRING], 16)
                    act.wait_ge(s["t_free"], tb + (g0 + T_MEAN + 1))
                    A(SQ4, OF, ACT.Square).then_inc(s["gn_sq"], 1)
                    silu(2)
                    act.wait_ge(s["aux_free"], hh * AUX_USES + (N_ST + KT))
                    act.dma_start(ret_p[bass.ds(layer, 1), bass.ds(head, 1)].rearrange(
                        "l h (d p) e -> p (l h d) e", p=P), SF).then_inc(s["sfin_st"], 16)

                one_head(0, True)
                with act.Fori(1, HEADS) as head:
                    one_head(head, False)
                ret_tail((layer + 1) * HEADS, tb0, C_LRU - MT - 1)

                for g in range(GROUPS):
                    tb = tb0 + (C_LRU + g * T_LRU)
                    cb = layer * LT + g * GT
                    for t in range(GT):
                        act.wait_ge(s["xc_full"], cb + (t + 1))
                        A(XCH[:, t, :], XCF[:, t, :], copy).then_inc(s["xc_high"], 1)

                    def stage_a(t):
                        b, c = t % 2, g * GT + t
                        act.wait_ge(s["p_done"], tb + (GT + 3 * t + 2))
                        A(halves(LA[:, b, :]), pp(GT + 3 * t + 1), ACT.Sigmoid,
                          bias=CUR[:, PC_BA + c:PC_BA + c + 1]).then_inc(s["gate_r"], 1)
                        act.wait_ge(s["p_done"], tb + (GT + 3 * t + 3))
                        A(halves(IX[:, b, :]), pp(GT + 3 * t + 2), ACT.Sigmoid,
                          bias=CUR[:, PC_BX + c:PC_BX + c + 1]).then_inc(s["gate_i"], 1)
                        act.wait_ge(s["t_free"], tb + (GT + 3 * t + 2))
                        A(AF[:, b, :], LA[:, b, :], ACT.Exp, scale=-1.0)
                        act.drain()
                        A(LA[:, b, :], LA[:, b, :], ACT.Tanh).then_inc(s["th_full"], 1)
                        A(YF[:, b, :], YF[:, b, :], ACT.Gelu_apprx_tanh).then_inc(s["y_gelu"], 1)

                    def stage_b(t):
                        b = t % 2
                        act.wait_ge(s["d_full"], cb + (t + 1))
                        A(DF, DF, ACT.Sqrt).then_inc(s["w_sqrt"], 1)
                        act.wait_ge(s["gl_full"], cb + (t + 1))
                        A(GLH[:, t, :], YF[:, b, :], copy).then_inc(s["gl_high"], 1)

                    for t in range(GT + 1):
                        if t < GT:
                            stage_a(t)
                        if t:
                            stage_b(t - 1)
                act.wait_ge(s["small_rd"], layer + 1)
                for dram, src in ((lru_o, LRO), (conv_p, CVP)):
                    act.dma_start(dram[bass.ds(layer, 1)].rearrange("a p c b -> (a p) c b"), src[:]
                                  ).then_inc(s["small_st"], 16)
                act.dma_start(conv_s[bass.ds(layer, 1)].rearrange("a p c j b -> (a p) c j b"), CVS[:]
                              ).then_inc(s["small_st"], 16)

                A(TOUCH[:], EPST[:], ACT.Sigmoid)
                with act.Fori(0, MT) as mm:
                    for j in range(2):
                        act.wait_ge(s["t_free"], tb0 + (C_MERGE + j + 1) + 2 * mm)
                        apart()
                        A(ZM[:, j, :], ZM[:, j, :], ACT.Sigmoid, bias=CUR[:, bass.ds(mm + (PC_BG + j * MT), 1)]
                          ).then_inc(s["sg_m"], 1)
                    act.wait_ge(s["mg_full"], layer * MT + 1 + mm)
                    apart()
                    A(MH[:, bass.ds(mm, 1), :].rearrange("p a t -> p (a t)"), MG, copy
                      ).then_inc(s["mg_high"], 1)

                def normed(full, high, i, j):
                    act.wait_ge(s["x_full"], full + 2 * i)
                    act.wait_ge(s["x_low_s"], high - 2 + 2 * i)
                    apart()
                    x1, h1 = pair_row(X, i, j), pair_row(XH, i, j)
                    A(SQT[:, j, :], x1, ACT.Square)
                    A(h1, x1, copy, scale=GAIN2[:, j, bass.ds(i, 1)]).then_inc(s["x_high_s"], 1)
                    act.drain()

                with act.Fori(0, MT // 2) as i:
                    for j in range(2):
                        normed(nb + j + 1, nb + MT + j + 1, i, j)
                act.wait_ge(s["p_done"], tb0 + (C_NORM1 + 1))
                A(halves(RINV[:]), pp(C_NORM1), ACT.Sqrt, bias=EPST[:], scale=1.0 / DM
                  ).then_inc(s["x_sd"], 1)

                A(TOUCH[:], EPST[:], ACT.Silu)
                for f in range(FH):
                    bt = C_FFN + f * T_FFN
                    fb = layer * (FH * FT) + f * FT
                    with act.Fori(0, FT) as i:
                        act.wait_ge(s["t_free"], tb0 + (bt + 1) + 2 * i)
                        A(FG[:, 0, :], FG[:, 0, :], ACT.Silu).then_inc(s["f_silu"], 1)
                        act.wait_ge(s["f_full"], fb + 1 + i)
                        apart()
                        A(AH[:, bass.ds(i, 1), :].rearrange("p a t -> p (a t)"), FF, copy
                          ).then_inc(s["f_high"], 1)
                with act.Fori(0, MT // 2) as i:
                    for j in range(2):
                        normed(nb + MT + j + 1, nb + 2 * MT + j + 1, i, j)
                act.wait_ge(s["p_done"], tb0 + (C_NORM2 + 1))
                A(halves(RINV[:]), pp(C_NORM2), ACT.Sqrt, bias=EPST[:], scale=1.0 / DM
                  ).then_inc(s["x_sd"], 1)

            for m in range(MT):
                act.wait_ge(s["y_full"], m + 1)
                act.dma_start(yt[:, m, :], ACC[:, m, :]).then_inc(s["y_st"], 16)
            act.wait_ge(s["y_st"], 16 * MT)
            act.wait_ge(s["small_st"], 48 * DEPTH + 16)
            act.wait_ge(s["sfin_st"], 16 * DEPTH * HEADS + 16)
            act.wait_ge(s["vs_st"], 16 * DEPTH * HEADS)
            for r in range(SRING):
                act.wait_ge(s_st[r], 16 * SUSES[r] * DEPTH * HEADS + 16)


def weight_units(np, w_in, w_ret_out, wa, wx, w_lru_out, w_o, w_gate_up, w_down):
    off = np.cumsum([0, HEADS * DK, HEADS * DK, HEADS * DV, HEADS * DV, LW, LW, DM])
    out = np.zeros((DEPTH * UNITS, P, UW), np.float32)
    n = 0

    def tile(w, col, rows, put=0):
        for i, r in enumerate(rows):
            out[n, :, (put + i) * P:(put + i + 1) * P] = w[r * P:(r + 1) * P, col:col + P]

    for l in range(DEPTH):
        def ret_out(h):
            nonlocal n
            for m in range(0, MT, 2):
                for j in range(2):
                    tile(w_ret_out[l], (m + j) * P, range(h * VT, (h + 1) * VT), j * VT)
                n += 1

        for h in range(HEADS):
            for part in range(3):
                if part == 0:
                    cols = [off[i] + h * DK + j * P for i in range(2) for j in range(KT)]
                elif part == 1:
                    cols = [off[2] + h * DV + j * P for j in range(VT)]
                    if h:
                        ret_out(h - 1)
                else:
                    cols = [off[3] + h * DV + UG.index(j) * P for j in range(VT)]
                for c in cols:
                    tile(w_in[l], c, range(MT))
                    n += 1
        ret_out(HEADS - 1)
        for g in range(GROUPS):
            wide = GT * P
            gates = []
            for w in (wa, wx):
                full = np.zeros((wide, wide), np.float32)
                for b in range(NBLK // GROUPS):
                    full[b * BLK:(b + 1) * BLK, b * BLK:(b + 1) * BLK] = w[l, g * (NBLK // GROUPS) + b]
                gates.append(full)
            for t in range(GT):
                tile(w_in[l], off[4] + g * wide + t * P, range(MT))
                n += 1
            for t in range(GT):
                tile(w_in[l], off[5] + g * wide + t * P, range(MT))
                n += 1
                for i, full in enumerate(gates):
                    tile(full, t * P, BAND[t], i * len(BAND[t]))
                n += 1
            for m in range(MT):
                tile(w_lru_out[l], m * P, range(g * GT, (g + 1) * GT))
                n += 1
        for m in range(MT):
            for j in range(2):
                tile(w_in[l], off[6 + j] + m * P, range(MT))
                n += 1
        for m in range(MT):
            tile(w_o[l], m * P, range(MT))
            n += 1
        for f in range(FH):
            for t in range(FT):
                for j in range(2):
                    tile(w_gate_up[l], j * DFF + (f * FT + t) * P, range(MT))
                    n += 1
            for m in range(MT):
                tile(w_down[l], m * P, range(f * FT, f * FT + K_DOWN[0]))
                n += 1
                tile(w_down[l], m * P, range(f * FT + K_DOWN[0], (f + 1) * FT))
                n += 1
    assert n == DEPTH * UNITS
    return out.reshape(DEPTH, UNITS, P, UW)


def constants(np, past):
    f4 = np.float32
    half = DK // 2
    freqs = np.power(10000.0, -(np.arange(half, dtype=f4) / f4(half)).astype(np.float64)).astype(f4)
    pos = np.concatenate([np.arange(SEQ, dtype=f4), np.full(NS, past, f4)])
    ang = (freqs[:, None] * pos[None, :]).astype(f4).astype(np.float64)
    trig = np.stack([np.cos(ang), np.sin(ang)]).astype(f4)
    lg = np.log(1.0 - 2.0 ** (-5.0 - np.arange(HEADS)))
    diff = np.arange(SEQ)[None, :] - np.arange(P)[:, None]
    dec = np.where(diff >= 0, np.exp(lg[:, None, None] * np.maximum(diff, 0)), 0.0).astype(f4)
    kd = np.zeros((P, HEADS, TT + 1), f4)
    for h in range(HEADS):
        for j in range(TT):
            kd[:, h, j] = np.exp(lg[h] * (SEQ - 1 - j * P - np.arange(P))) * DK ** -0.5
        kd[:, h, TT] = np.exp(lg[h])
    return trig, dec, kd, np.eye(P, dtype=f4)


def kernel(x_prompt, x_sample, state_ret, state_lru, state_conv, w_in, norm_mix, gn_gain, w_ret_out,
           conv_w, conv_b, lru_wa, lru_ba, lru_wx, lru_bx, lru_lambda, w_lru_out, b_gate, w_o,
           norm_ffn, w_gate_up, w_down, norm_final):
    import numpy as np
    import concourse.bacc as bacc
    from concourse.bass_utils import run_bass_kernel_spmd

    arr = lambda a: np.asarray(a)
    x = np.concatenate([arr(x_prompt)[0], arr(x_sample)[:, 0]], 0)
    xt = np.ascontiguousarray(x.T.reshape(MT, P, TOK).transpose(1, 0, 2))

    def chan(a):
        a = arr(a)
        return np.moveaxis(a.reshape(a.shape[:-1] + (-1, P)), -1, -2)

    cw = chan(conv_w)
    params = np.concatenate([
        chan(gn_gain), cw.transpose(0, 2, 3, 1).reshape(DEPTH, P, LT * CW), chan(conv_b), chan(lru_ba),
        chan(lru_bx), chan(b_gate).transpose(0, 2, 1, 3).reshape(DEPTH, P, 2 * MT), chan(lru_lambda)], 2)
    params = np.ascontiguousarray(params.transpose(1, 0, 2))
    nm, nf = chan(norm_mix), chan(norm_ffn)
    norms = np.stack([nm[0], nf[0], nm[1], nf[1], chan(norm_final)], 1)
    slru = chan(state_lru).transpose(0, 2, 3, 1)
    sconv = chan(state_conv).transpose(0, 3, 4, 2, 1)
    trig, dec, kdt, ident = constants(np, 4096)
    ins = dict(
        wstream=weight_units(np, *(arr(a) for a in (w_in, w_ret_out, lru_wa, lru_wx, w_lru_out, w_o,
                                                    w_gate_up, w_down))),
        xt=xt, params=params, norms=norms, tables=trig, dec=dec, kdt=kdt, slru=slru, sconv=sconv,
        sret=arr(state_ret), ident=ident)
    outs = dict(yt=(P, MT, TOK), ret_p=(DEPTH, HEADS, DK, DV), ret_s=(DEPTH, NS, HEADS, DK, DV),
                lru_o=(DEPTH, P, LT, NS + 1), conv_p=(DEPTH, P, LT, CW - 1),
                conv_s=(DEPTH, P, LT, CW - 1, NS))

    nc = bacc.Bacc("TRN2", target_bir_lowering=False, num_devices=1)
    arrays, aps = {}, {}
    for name, a in ins.items():
        a = np.ascontiguousarray(a)
        arrays["in_" + name] = a
        aps[name] = nc.dram_tensor("in_" + name, a.shape, F32, kind="ExternalInput").ap()
    for name, shape in outs.items():
        aps[name] = nc.dram_tensor("out_" + name, shape, F32, kind="ExternalOutput").ap()
    aps["vscr"] = nc.dram_tensor("v_rows", (NS, DV), F32, kind="Internal").ap()
    build(nc, **aps)
    got = run_bass_kernel_spmd(nc, [arrays], core_ids=[0]).results[0]
    got = {name: got["out_" + name] for name in outs}

    y = got["yt"].transpose(1, 0, 2).reshape(DM, TOK).T
    lru = got["lru_o"].transpose(0, 3, 2, 1).reshape(DEPTH, NS + 1, LW)
    return (
        np.ascontiguousarray(y[:SEQ])[None], np.ascontiguousarray(y[SEQ:])[:, None],
        got["ret_p"][:, None], np.ascontiguousarray(lru[:, :1]),
        np.ascontiguousarray(got["conv_p"].transpose(0, 3, 2, 1).reshape(DEPTH, 1, CW - 1, LW)),
        got["ret_s"], np.ascontiguousarray(lru[:, 1:]),
        np.ascontiguousarray(got["conv_s"].transpose(0, 4, 3, 2, 1).reshape(DEPTH, NS, CW - 1, LW)),
    )
```

```python
from contextlib import ExitStack

import concourse.bass as bass
from concourse import mybir

F32 = mybir.dt.float32
F32R = mybir.dt.float32r
ACT = mybir.ActivationFunctionType
ALU = mybir.AluOpType
AX = mybir.AxisListType

P = 128
DEPTH, DM, SEQ, NS = 2, 1024, 512, 8
TOK = SEQ + NS
HALF = TOK // 2
MT = DM // P
HEADS, DK, DV = 4, 256, 512
KT, VT = DK // P, DV // P
TT = SEQ // P
LW, CW, NBLK = 1280, 4, 16
LT = LW // P
GROUPS = 2
GT = LT // GROUPS
DFF = 2816
FH = 2
FT = DFF // P // FH
EPS = 1e-6
UW = 8 * P

BLK = LW // NBLK
BAND = [sorted({(b * BLK + e) // P for b in range(t * P // BLK, (t * P + P - 1) // BLK + 1)
                for e in (0, BLK - 1)}) for t in range(GT)]

QK, GATES = 2 * KT, VT
YG_UNIT = [(MT + 2 * len(BAND[t])) // 2 for t in range(GT)]
MG_UNIT = (2 * MT + GT) // 3
LRU_GATES = [n for t in range(GT) for n in (YG_UNIT[t],) * 2]
assert MG_UNIT * 3 == 2 * MT + GT
K_DOWN = (6, FT - 6)
U_HEAD = QK + VT + GATES + MT // 2
RUNS = ([(HEADS * U_HEAD, (MT,))]
        + [(1, (MT,) * GT + tuple(LRU_GATES) + (MT,) * GT), (MT, (GT,)), (1, tuple(LRU_GATES)),
           (MT, (MG_UNIT,) * 3), (MT, (MT,))] + [(2 * FT, (MT,)), (MT, K_DOWN)] * FH)
B_LRU = HEADS * U_HEAD
X_EARLY = 2
B_X = [[B_LRU + t - (MT // 2 if t < X_EARLY else 0) for t in range(GT)],
       [B_LRU + 3 * GT + t for t in range(GT)]]
B_Y = [B_LRU + GT, B_LRU + 4 * GT + MT]
B_OUT = B_LRU + 4 * GT
B_MERGE = B_LRU + 6 * GT + MT
B_WO = B_MERGE + 3 * MT
B_FFN = B_WO + MT
U_FFN = 2 * FT + 2 * MT
UNITS = B_FFN + FH * U_FFN
assert UNITS == sum(n * len(w) for n, w in RUNS)

T_HEAD = QK + VT + GATES + 2 + MT
C_LRU = HEADS * T_HEAD
C_X = [[C_LRU + t - (MT if t < X_EARLY else 0) for t in range(GT)],
       [C_LRU + 4 * GT + t for t in range(GT)]]
C_Y = [C_LRU + GT, C_LRU + 5 * GT + MT]
C_OUT = C_LRU + 5 * GT
C_MERGE = C_LRU + 8 * GT + MT
C_WO = C_MERGE + 3 * MT
C_FFN = C_WO + MT
T_FFN = 2 * FT + MT
TILES = C_FFN + FH * T_FFN
TILE0 = 2
TG = [0, 1, 4, 2]
T_MEAN, T_VAR = 3, 5
UG = [0, 1, 3, 2]
assert UNITS % 2 == TILES % 2 == U_HEAD % 2 == T_HEAD % 2 == C_MERGE % 2 == B_MERGE % 2 == MT // 2 % 2 == 0

N_SC, N_TK, N_VS, N_TV, N_AT, N_ST = 0, 4, 6, 7, 11, 15
AUX_USES = 17
BANK = [0, 1, 2, 3, 0, 1, 2, 3, 0, 1, 2, 0, 1, 2, 0, 1, 2]
BANK_SO = 3
PREV = [max([m for m in range(n) if BANK[m] == BANK[n]], default=None) for n in range(AUX_USES)]

ST_OFF = [sum(SEQ - P * i for i in range(j)) for j in range(TT + 1)]
SRING, VRING = 4, 2
SUSES = [len(range(r, NS, SRING)) for r in range(SRING)]

PC_GN, PC_CW, PC_CB, PC_BA, PC_BX, PC_BG, PC_SP = 0, 16, 56, 66, 76, 86, 102
PCOLS = 112


def build(nc, wstream, xt, params, norms, tables, dec, kdt, slru, sconv, sret, ident,
          yt, ret_p, ret_s, lru_o, conv_p, conv_s, vscr):
    ctx = ExitStack()
    with ctx:
        def sb(name, shape, dt=F32):
            return ctx.enter_context(nc.sbuf_tensor(name, shape, dt))

        def sem(name):
            return ctx.enter_context(nc.semaphore(name))

        X = sb("residual", [P, MT, TOK])
        XH = sb("x_high", [P, MT, TOK], F32R)
        XL = sb("x_low", [P, MT, TOK], F32R)
        WR = sb("w_raw", [P, 2, UW])
        WH = sb("w_high", [P, 2, UW], F32R)
        WL = sb("w_low", [P, 2, UW], F32R)
        ACC = sb("ret_acc", [P, MT, TOK])
        COS = sb("cos_r", [P, TOK])
        SIN = sb("sin_r", [P, TOK])
        DEC = sb("decay", [P, SEQ])
        RINV = sb("rinv", [P, TOK])
        ONES = sb("ones", [P, P])
        ID = sb("ident_sb", [P, P])
        PAR = sb("params_all", [P, DEPTH, PCOLS])
        CUR = sb("params_cur", [P, PCOLS])
        NRM = sb("norms_all", [P, 2 * DEPTH + 1, MT])
        GAIN = sb("gain_cur", [P, MT])
        GAIN2 = GAIN[:, :].rearrange("p (n two) -> p two n", two=2)
        KDT = sb("kd_all", [P, HEADS, TT + 1])
        KDC = sb("kd_cur", [P, TT + 1])
        GNC = sb("gn_cur", [P, VT])
        SLR = sb("state_lru_sb", [P, LT, NS])
        SCV = sb("state_conv_sb", [P, LT, CW - 1, NS])
        LRO = sb("lru_out_sb", [P, LT, NS + 1])
        CVP = sb("conv_p_sb", [P, LT, CW - 1])
        CVS = sb("conv_s_sb", [P, LT, CW - 1, NS])
        EPST2 = sb("eps", [P, 2])
        EPST, TOUCH = EPST2[:, 0:1], EPST2[:, 1:2]
        KSC = sb("k_sample", [P, KT, NS])

        R_HEAD = 4 * KT * TOK + 2 * TT * DV + 2 * TT * DK + 2 * ST_OFF[TT]
        R = sb("split_scratch", [P, max(R_HEAD, 2 * FT * TOK, (2 * MT - 1) * TOK + 2 * GT * TOK)], F32R)

        def rview(off, a, b):
            return R[:, off:off + a * b].rearrange("p (a b) -> p a b", a=a)

        QH, QL, KH, KL = (rview(i * KT * TOK, KT, TOK) for i in range(4))
        o = 4 * KT * TOK
        VH, VL = rview(o, TT, DV), rview(o + TT * DV, TT, DV)
        OGH, OGL = rview(o, VT, TOK), rview(o + VT * TOK, VT, TOK)
        o += 2 * VT * TOK
        KDH, KDL = rview(o, TT, DK), rview(o + TT * DK, TT, DK)
        o += 2 * TT * DK
        STH, STL = R[:, o:o + ST_OFF[TT]], R[:, o + ST_OFF[TT]:o + 2 * ST_OFF[TT]]
        XCH, XCL = (rview(i * GT * TOK, GT, TOK) for i in range(2))
        GLH, GLL = (rview((2 * MT - 1 + i * GT) * TOK, GT, TOK) for i in range(2))
        MH, ML = rview(0, MT, TOK), rview(MT * TOK, MT, TOK)
        AH, AL = rview(0, FT, TOK), rview(FT * TOK, FT, TOK)

        sizes = [("qk", 2 * KT * TOK), ("vo", VT * TOK), ("sg", VT * TOK), ("rt", 2 * TOK),
                 ("s", 3 * KT * DV), ("t", KT * DV), ("vb", VRING * DV), ("s3", KT * DV), ("sum", TOK)]
        FA = sb("scratch", [P, sum(n for _, n in sizes)])
        at, pos = {}, 0
        for name, n in sizes:
            at[name] = pos
            pos += n

        def fview(off, a, b):
            return FA[:, off:off + a * b].rearrange("p (a b) -> p a b", a=a)

        QF, KF = fview(at["qk"], KT, TOK), fview(at["qk"] + KT * TOK, KT, TOK)
        SQ4 = fview(at["t"], VT, TOK)
        VF = OF = fview(at["vo"], VT, TOK)
        SG = fview(at["sg"], VT, TOK)
        STF = FA[:, at["sg"]:at["sg"] + ST_OFF[TT]]
        RT = fview(at["rt"], 2, TOK)
        SF = fview(at["rt"], KT, DV)
        SS = [fview(at["s"] + r * KT * DV, KT, DV) for r in range(3)] + [fview(at["s3"], KT, DV)]
        TS = [fview(at["t"], KT, DV), fview(at["rt"], KT, DV)]
        VB = fview(at["vb"], VRING, DV)
        VS = FA[0:NS, at["t"]:at["t"] + DV]
        SUM = RSTD = FA[:, at["sum"]:at["sum"] + TOK]
        SSQ = FA[:, at["s3"]:at["s3"] + TOK]
        SQT = fview(at["rt"], 2, TOK)
        e_, z_, z2, acc = (DEC[:, LT * i:LT * (i + 1)] for i in range(4))
        ACCL = fview(0, MT, TOK)
        o = MT * TOK
        XCF = fview(o, GT, TOK)
        o += GT * TOK
        LA, IX, YF, AF = (fview(o + 2 * i * TOK, 2, TOK) for i in range(4))
        o += 8 * TOK
        DF, HF, XR = (FA[:, o + i * TOK:o + (i + 1) * TOK] for i in range(3))
        assert o + 3 * TOK <= pos
        ZM = fview(MT * TOK, 4, TOK)
        MG = FA[:, (MT + 4) * TOK:(MT + 5) * TOK]
        BG = CUR[:, PC_BG:PC_BG + 2 * MT].rearrange("p (w n two) -> p w two n", w=2, two=2)
        FG = fview(0, 2, TOK)
        FF = FA[:, 2 * TOK:3 * TOK]

        PP = ctx.enter_context(nc.psum_tensor("proj", [P, 2, 2, 512], F32))
        AUX = ctx.enter_context(nc.psum_tensor("aux", [P, 4, 512], F32))

        names = ("go_pool go_pe setup_ld boot w_split w_used p_done t_free "
                 "rope_done qk_high qk_low st_high st_low aux_mm aux_free kv_high kv_low "
                 "vs_st dec_ld trig_ld silu_g t_mul s_new so_done gn_sum centred gn_sq gn_sd var_rd og_full og_high "
                 "og_low sfin_st sq_mm state_ld xc_full xc_high xc_low lam_exp gate_r gate_i th_full d_full "
                 "w_sqrt y_gelu gl_full gl_high gl_low small_rd small_st sg_m mg_full mg_high mg_low "
                 "x_full x_high_s x_low_s x_sd f_silu f_full f_high f_low ones_ok y_full y_st").split()
        s = {n: sem(n) for n in names}
        w_ld = [sem(f"w_loaded{j}") for j in range(2)]
        s_ld = [sem(f"s_loaded{j}") for j in range(SRING)]
        s_st = [sem(f"s_stored{j}") for j in range(SRING)]
        x_ld = [sem(f"x_loaded{m}") for m in range(MT)]
        v_ld = [sem(f"vb_loaded{j}") for j in range(VRING)]

        def halves(ap):
            return ap.rearrange("p (t b) -> p t b", t=2)

        def pair_row(t, i, j):
            return t[:, :, :].rearrange("p (n two) t -> p two n t", two=2)[:, j, bass.ds(i, 1), :].rearrange(
                "p a t -> p (a t)")

        def slot(idx):
            return (TILE0 + idx) % 2

        def pp(idx):
            return PP[:, slot(idx), :, 0:HALF]

        def runs():
            base = 0
            for times, blocks in RUNS:
                if len(blocks) % 2 and times > 1:
                    times, blocks = times // 2, blocks * 2
                yield base, times, blocks
                base += times * len(blocks)

        block = ctx.enter_context(nc.Block())

        @block.sync
        def _(sp):
            with sp.Fori(0, DEPTH) as layer:
                for base, times, blocks in runs():
                    units = wstream[:, base:base + times * len(blocks)].rearrange(
                        "l (n k) p c -> l k n p c", k=len(blocks))
                    with sp.Fori(0, times) as i:
                        for k, n in enumerate(blocks):
                            u = base + k
                            sp.wait_ge(s["w_split"], layer * UNITS + (u + 1) + i * len(blocks))
                            sp.dma_start(WR[:, u % 2, 0:n * P],
                                         units[bass.ds(layer, 1), k, bass.ds(i, 1), :, 0:n * P].rearrange(
                                             "l a p c -> p (l a) c").rearrange("p a c -> p (a c)")
                                         ).then_inc(w_ld[u % 2], 16)

        @block.gpsimd
        def _(pool):
            pool.memset(ONES[:], 1.0).then_inc(s["ones_ok"], 1)

            pool.sem_inc(s["w_split"], 2)
            with pool.Fori(0, DEPTH) as layer:
                for base, times, blocks in runs():
                    with pool.Fori(0, times) as i:
                        for k, n in enumerate(blocks):
                            j, w = (base + k) % 2, slice(0, n * P)
                            u = layer * UNITS + base + k + i * len(blocks)
                            pool.wait_ge(s["w_used"], u + 2)
                            pool.wait_ge(w_ld[j], (layer * (UNITS // 2) + i * (len(blocks) // 2)) * 16
                                         + 16 * ((base + k) // 2 + 1))
                            pool.sem_inc(s["go_pool"], 1)
                            pool.tensor_scalar(WH[:, j, w], WR[:, j, w], 1.0, 0.0, ALU.mult, ALU.add)
                            pool.drain()
                            pool.tensor_tensor(WL[:, j, w], WR[:, j, w], WH[:, j, w].bitcast(F32),
                                               ALU.subtract).then_inc(s["w_split"], 1)

        @block.tensor
        def _(pe):
            def product(outs, w, blk, xs, first, last):
                started = blk
                for n, (wt, xi) in enumerate(((WH, 0), (WH, 1), (WL, 0))):
                    for out, x in zip(outs, xs):
                        m = pe.matmul(out, wt[:, w, blk * P:(blk + 1) * P], x[xi],
                                      start=first and n == 0, stop=last and n == 2)
                        if not started:
                            m.then_inc(s["w_used"], 1)
                            started = True
                return m

            def tile_begin(tb, idx):
                pe.wait_ge(s["t_free"], tb + (idx - 1))

            def unit_begin(ub, u):
                pe.wait_ge(s["w_split"], ub + (u + 3))

            def pairs(hi, lo, k):
                return [(hi[:, k, c * HALF:(c + 1) * HALF], lo[:, k, c * HALF:(c + 1) * HALF])
                        for c in range(2)]

            def whole(ub, u, tb, idx, hi, lo, made=None, count=0, midway=None, variances=None):
                unit_begin(ub, u)
                if variances is not None:
                    pe.wait_ge(s["var_rd"], variances)
                else:
                    tile_begin(tb, idx)
                outs = [PP[:, slot(idx), c, 0:HALF] for c in range(2)]
                for k in range(MT):
                    if made is not None:
                        pe.wait_ge(made, count + (k + 1))
                    if midway and k == MT // 2:
                        midway()
                    m = product(outs, u % 2, k, pairs(hi, lo, k), k == 0, k == MT - 1)
                m.then_inc(s["p_done"], 1)

            def spread(ub, u, size, tb, idx, hi, lo, ks, q):
                tile_begin(tb, idx)
                outs = [PP[:, slot(idx), c, 0:HALF] for c in range(2)]
                for k in ks:
                    if q % size == 0:
                        unit_begin(ub, u + q // size)
                    m = product(outs, (u + q // size) % 2, q % size, pairs(hi, lo, k),
                                k == ks[0], k == ks[-1])
                    q += 1
                m.then_inc(s["p_done"], 1)
                return q

            def column_sums(tb, idx, src):
                tile_begin(tb, idx)
                for c in range(2):
                    m = pe.matmul(PP[:, slot(idx), c, 0:HALF], ONES[:], src[:, c * HALF:(c + 1) * HALF],
                                  start=True, stop=True)
                m.then_inc(s["p_done"], 1)

            def norm_sums():
                for c in range(2):
                    m = pe.matmul(AUX[:, c, 0:HALF], ONES[:], SSQ[:, c * HALF:(c + 1) * HALF],
                                  start=True, stop=True)
                m.then_inc(s["sq_mm"], 1)

            pe.sem_inc(s["p_done"], TILE0)
            pe.sem_inc(s["w_used"], 2)
            pe.wait_ge(s["ones_ok"], 1)
            pe.wait_ge(s["setup_ld"], 16 * 4)

            with pe.Fori(0, DEPTH) as layer:
                ub0, tb0 = layer * UNITS, layer * TILES + TILE0

                def ret_out(hh, ub, u0, tb, i0):
                    for m_ in range(MT):
                        if m_ % 2 == 0:
                            unit_begin(ub, u0 + m_ // 2)
                        tile_begin(tb, i0 + m_)
                        outs = [PP[:, slot(i0 + m_), c, 0:HALF] for c in range(2)]
                        for k in range(VT):
                            if m_ == 0:
                                pe.wait_ge(s["og_low"], hh * VT + (k + 1 - VT))
                            m = product(outs, (u0 + m_ // 2) % 2, (m_ % 2) * VT + k, pairs(OGH, OGL, k),
                                        k == 0, k == VT - 1)
                        m.then_inc(s["p_done"], 1)

                def x_tile(g, t):
                    whole(ub0, B_X[g][t], tb0, C_X[g][t], XH, XL,
                          variances=(layer + 1) * HEADS if g == 0 and t == 1 else None)

                def one_head(head, first):
                    hh = layer * HEADS + head
                    if first:
                        ub, tb, uv, v0 = ub0, tb0, QK, QK
                    else:
                        ub, tb = ub0 - MT // 2 + head * U_HEAD, tb0 - MT + head * T_HEAD
                        uv, v0 = QK + MT // 2, QK + MT
                    for i in range(QK):
                        if first and i == 0:
                            whole(ub, i, tb, i, XH, XL, s["x_low_s"], layer * (2 * MT))
                            norm_sums()
                        else:
                            whole(ub, i, tb, i, XH, XL, variances=hh if i == 1 and not first else None)
                    if not first:
                        ret_out(hh, ub, QK, tb, QK)
                    for i in range(VT):
                        whole(ub, uv + i, tb, v0 + i, XH, XL)
                    pe.wait_ge(s["qk_low"], hh * 2 + 2)

                    def aux_begin(n):
                        if PREV[n] is not None:
                            pe.wait_ge(s["aux_free"], hh * AUX_USES + (PREV[n] + 1))

                    for j in range(TT):
                        aux_begin(N_SC + j)
                        for d in range(KT):
                            for n, (a, b) in enumerate(((KH, QH), (KH, QL), (KL, QH))):
                                m = pe.matmul(AUX[:, BANK[N_SC + j], 0:SEQ - j * P],
                                              a[:, d, j * P:(j + 1) * P], b[:, d, j * P:SEQ],
                                              start=d == n == 0, stop=d == KT - 1 and n == 2)
                        m.then_inc(s["aux_mm"], 1)
                    for i in range(TT // 2):
                        aux_begin(N_TK + i)
                        for j in range(2):
                            for d in range(KT):
                                m = pe.transpose(
                                    AUX[:, BANK[N_TK + i], (j * KT + d) * P:(j * KT + d + 1) * P],
                                    KF[:, d, (2 * i + j) * P:(2 * i + j + 1) * P], ID[:])
                        m.then_inc(s["aux_mm"], 1)
                    pe.wait_ge(s["t_free"], tb + (v0 + VT))
                    aux_begin(N_VS)
                    for e in range(VT):
                        m = pe.transpose(AUX[0:NS, BANK[N_VS], e * P:(e + 1) * P],
                                         VF[:, e, SEQ:TOK], ID[:])
                    m.then_inc(s["aux_mm"], 1)

                    def v_by_token(j):
                        aux_begin(N_TV + j)
                        for e in range(VT):
                            m = pe.transpose(AUX[:, BANK[N_TV + j], e * P:(e + 1) * P],
                                             VF[:, e, j * P:(j + 1) * P], ID[:])
                        m.then_inc(s["aux_mm"], 1)

                    def gate(e, midway=None):
                        whole(ub, uv + VT + UG[e], tb, v0 + VT + TG[e], XH, XL, midway=midway)

                    def attend(e):
                        aux_begin(N_AT + e)
                        for j in range(TT):
                            for n, (a, b) in enumerate(((VH, STH), (VH, STL), (VL, STH))):
                                m = pe.matmul(AUX[:, BANK[N_AT + e], j * P:SEQ],
                                              a[:, j, e * P:(e + 1) * P],
                                              b[:, ST_OFF[j]:ST_OFF[j + 1]],
                                              start=j == n == 0, stop=j == TT - 1 and n == 2)
                        m.then_inc(s["aux_mm"], 1)

                    def final_state(d):
                        aux_begin(N_ST + d)
                        for j in range(TT):
                            for n, (a, b) in enumerate(((KDH, VH), (KDH, VL), (KDL, VH))):
                                m = pe.matmul(AUX[:, BANK[N_ST + d], :], a[:, j, d * P:(d + 1) * P],
                                              b[:, j, :], start=j == n == 0,
                                              stop=j == TT - 1 and n == 2)
                        m.then_inc(s["aux_mm"], 1)

                    def sample_out(b):
                        pe.wait_ge(s["s_new"], hh * NS + (b + 1))
                        for e in range(VT):
                            for d in range(KT):
                                m = pe.matmul(AUX[:, BANK_SO, e * NS + b:e * NS + b + 1],
                                              SS[b % SRING][:, d, e * P:(e + 1) * P],
                                              QF[:, d, SEQ + b:SEQ + b + 1],
                                              start=b == e == d == 0, stop=d == KT - 1,
                                              skip_group_check=True)
                        m.then_inc(s["so_done"], 1)

                    v_by_token(0)
                    gate(0)
                    for j in range(1, TT):
                        v_by_token(j)
                    gate(1)
                    sample_out(0)
                    gate(3, midway=lambda: sample_out(1))
                    sample_out(2)
                    pe.wait_ge(s["kv_low"], hh * (2 * TT) + 2 * TT)
                    pe.wait_ge(s["st_low"], hh * TT + TT)
                    for e in range(VT):
                        attend(e)
                        sample_out(3 + e)
                    final_state(0)
                    sample_out(NS - 1)
                    final_state(1)
                    pe.wait_ge(s["gn_sum"], hh * 2 + 1)
                    column_sums(tb, v0 + VT + T_MEAN, SUM)
                    gate(2)
                    pe.wait_ge(s["gn_sum"], hh * 2 + 2)
                    column_sums(tb, v0 + VT + T_VAR, SUM)

                one_head(0, True)
                with pe.Fori(1, HEADS) as head:
                    one_head(head, False)
                for t in range(X_EARLY):
                    x_tile(0, t)
                ret_out((layer + 1) * HEADS, ub0, B_LRU - MT // 2 + X_EARLY, tb0, C_LRU - MT + X_EARLY)

                def y_gates(g):
                    for t in range(GT):
                        u, idx = B_Y[g] + 2 * t, C_Y[g] + 3 * t
                        q = spread(ub0, u, YG_UNIT[t], tb0, idx, XH, XL, range(MT), 0)
                        pe.wait_ge(s["xc_low"], layer * LT + (g * GT + BAND[t][-1] + 1))
                        for w in range(2):
                            q = spread(ub0, u, YG_UNIT[t], tb0, idx + 1 + w, XCH, XCL, BAND[t], q)

                def lru_out(u, units, idx, tiles):
                    pe.wait_ge(s["w_split"], ub0 + (u + 3) + units)
                    pe.wait_ge(s["t_free"], tb0 + (idx - 1) + tiles)
                    outs = [PP[:, slot(idx), c, 0:HALF] for c in range(2)]
                    for k in range(GT):
                        m = product(outs, u % 2, k, pairs(GLH, GLL, k), k == 0, k == GT - 1)
                    m.then_inc(s["p_done"], 1)

                for t in range(X_EARLY, GT):
                    x_tile(0, t)
                y_gates(0)
                for t in range(GT):
                    x_tile(1, t)
                pe.wait_ge(s["gl_low"], layer * LT + GT)
                pe.sem_inc(s["go_pe"], 1)
                with pe.Fori(0, MT // 2) as i:
                    for j in range(2):
                        lru_out(B_OUT + j, 2 * i, C_OUT + j, 2 * i)
                y_gates(1)

                with pe.Fori(0, MT // 2) as i:
                    for j in range(2):
                        place = (ub0 + 6 * i, B_MERGE + 3 * j, MG_UNIT, tb0 + 6 * i)
                        q = 0
                        for w in range(2):
                            q = spread(*place, C_MERGE + 3 * j + w, XH, XL, range(MT), q)
                        pe.wait_ge(s["gl_low"], layer * LT + LT)
                        spread(*place, C_MERGE + 3 * j + 2, GLH, GLL, range(GT), q)

                whole(ub0, B_WO, tb0, C_WO, MH, ML, s["mg_low"], layer * MT)
                whole(ub0, B_WO + 1, tb0, C_WO + 1, MH, ML)
                with pe.Fori(1, MT // 2) as i:
                    for j in range(2):
                        whole(ub0 + 2 * i, B_WO + j, tb0 + 2 * i, C_WO + j, MH, ML)

                for f in range(FH):
                    bu, bt = B_FFN + f * U_FFN, C_FFN + f * T_FFN
                    if f == 0:
                        whole(ub0, bu, tb0, bt, XH, XL, s["x_low_s"], layer * (2 * MT) + MT)
                        norm_sums()
                        whole(ub0, bu + 1, tb0, bt + 1, XH, XL)
                    with pe.Fori(1 - f, FT) as i:
                        for j in range(2):
                            whole(ub0 + 2 * i, bu + j, tb0 + 2 * i, bt + j, XH, XL)

                    def down(i, j, meet=False):
                        idx = bt + 2 * FT + j
                        pe.wait_ge(s["t_free"], tb0 + (idx - 1) + 2 * i)
                        outs = [PP[:, slot(idx), c, 0:HALF] for c in range(2)]
                        k = 0
                        for v in range(2):
                            u = bu + 2 * FT + 2 * j + v
                            pe.wait_ge(s["w_split"], ub0 + (u + 3) + 4 * i)
                            for b in range(K_DOWN[v]):
                                if meet:
                                    pe.wait_ge(s["f_low"], layer * (FH * FT) + (f * FT + k + 1))
                                m = product(outs, u % 2, b, pairs(AH, AL, k), k == 0, k == FT - 1)
                                k += 1
                        m.then_inc(s["p_done"], 1)

                    for j in range(2):
                        down(0, j, j == 0)
                    with pe.Fori(1, MT // 2) as i:
                        for j in range(2):
                            down(i, j)

            pe.wait_ge(s["x_low_s"], (2 * DEPTH + 1) * MT)
            norm_sums()

        @block.vector
        def _(dve):
            tt, ts, stt = dve.tensor_tensor, dve.tensor_scalar, dve.scalar_tensor_tensor

            def done(tb, idx):
                dve.wait_ge(s["p_done"], tb + (idx + 1))

            def norm_low(x, xh, xl, gain, j, first):
                if first:
                    ts(SSQ, SQT[:, j, :], 1.0, None, ALU.mult)
                else:
                    tt(SSQ, SSQ, SQT[:, j, :], ALU.add)
                return stt(xl, x, gain, xh.bitcast(F32), ALU.mult, ALU.subtract)

            def root_inverse(dst):
                return dve.reciprocal(dst, dst)

            dve.sem_inc(s["t_free"], TILE0)
            dve.memset(EPST, EPS).then_inc(s["boot"], 1)
            dve.memset(ACC[:], 0.0)
            dve.wait_ge(s["setup_ld"], 16 * 4)
            dve.tensor_copy(GAIN[:], NRM[:, 0, :])
            dve.drain().then_inc(s["boot"], 1)
            for m in range(MT):
                dve.wait_ge(s["x_high_s"], m + 1)
                norm_low(X[:, m, :], XH[:, m, :], XL[:, m, :], GAIN[:, m:m + 1], m % 2, m == 0
                         ).then_inc(s["x_low_s"], 1)
                dve.drain()
            with dve.Fori(0, DEPTH) as layer:
                tb0 = layer * TILES + TILE0
                nb = layer * (2 * MT)
                dve.drain()
                dve.tensor_copy(CUR[:], PAR[:, bass.ds(layer, 1), :].rearrange("p a n -> p (a n)"))
                dve.wait_ge(s["x_sd"], layer * 2 + 1)
                root_inverse(RINV[:])
                dve.drain()
                dve.wait_ge(s["trig_ld"], layer * 32 + 32)
                tt(COS[:], COS[:], RINV[:], ALU.mult)
                tt(SIN[:], SIN[:], RINV[:], ALU.mult)

                def ret_tail(hh):
                    dve.wait_ge(s["gn_sd"], hh)
                    root_inverse(RSTD).then_inc(s["t_free"], 1)
                    dve.drain()
                    for e in range(VT):
                        tt(SG[:, e, :], SG[:, e, :], RSTD, ALU.mult).then_inc(s["og_full"], 1)
                    dve.drain()

                def og_split(hh):
                    for e in range(VT):
                        dve.wait_ge(s["og_high"], hh * VT + (e + 1 - VT))
                        stt(OGL[:, e, :], SG[:, e, :], GNC[:, e:e + 1], OGH[:, e, :].bitcast(F32),
                            ALU.mult, ALU.subtract).then_inc(s["og_low"], 1)

                def ret_add(tb, i0, m_):
                    done(tb, i0 + m_)
                    tt(halves(ACC[:, m_, :]), pp(i0 + m_), halves(ACC[:, m_, :]), ALU.add
                       ).then_inc(s["t_free"], 1)

                def one_head(head, first):
                    hh = layer * HEADS + head
                    tb, v0 = (tb0, QK) if first else (tb0 - MT + head * T_HEAD, QK + MT)
                    g0 = v0 + VT
                    dve.drain()
                    dve.tensor_copy(KDC[:], KDT[:, bass.ds(head, 1), :].rearrange("p a n -> p (a n)"))
                    if not first:
                        ret_tail(hh)
                    dve.wait_ge(s["sfin_st"], hh * 16 + 16)

                    def low(dst, src, hi, scale, n):
                        dve.wait_ge(s["qk_high"], hh * 2 + n)
                        stt(dst, src, scale, hi.bitcast(F32), ALU.mult, ALU.subtract
                            ).then_inc(s["qk_low"], 1)

                    def rotate(n, dst, meanwhile):
                        done(tb, n)
                        tt(halves(dst[:, 0, :]), pp(n), halves(COS[:]), ALU.mult)
                        tt(halves(dst[:, 1, :]), pp(n), halves(SIN[:]), ALU.mult).then_inc(s["t_free"], 1)
                        meanwhile()
                        done(tb, n + 1)
                        tt(halves(RT[:, 0, :]), pp(n + 1), halves(SIN[:]), ALU.mult)
                        tt(halves(RT[:, 1, :]), pp(n + 1), halves(COS[:]), ALU.mult).then_inc(s["t_free"], 1)
                        dve.drain()
                        tt(dst[:, 0, :], dst[:, 0, :], RT[:, 0, :], ALU.subtract)
                        tt(dst[:, 1, :], dst[:, 1, :], RT[:, 1, :], ALU.add).then_inc(s["rope_done"], 1)
                        dve.drain()

                    def new_gain():
                        if not first:
                            og_split(hh)
                            dve.drain()
                        dve.tensor_copy(GNC[:], CUR[:, bass.ds(head * VT + PC_GN, VT)])

                    rotate(0, QF, new_gain)
                    rotate(KT, KF, lambda: low(QL, QF, QH, 1.0, 1))
                    ts(KSC[:], KF[:, :, SEQ:TOK], DK ** -0.5, None, ALU.mult)
                    if not first:
                        for m_ in range(MT):
                            ret_add(tb, QK, m_)
                            if m_ == 0:
                                low(KL, KF, KH, DK ** -0.5, 2)
                    for e in range(VT):
                        done(tb, v0 + e)
                        tt(halves(VF[:, e, :]), pp(v0 + e), halves(RINV[:]), ALU.mult
                           ).then_inc(s["t_free"], 1)
                        if first and e == 0:
                            low(KL, KF, KH, DK ** -0.5, 2)

                    def aux(n):
                        dve.wait_ge(s["aux_mm"], hh * AUX_USES + (n + 1))

                    dve.wait_ge(s["dec_ld"], hh * 16 + 16)
                    for j in range(TT):
                        aux(N_SC + j)
                        tt(STF[:, ST_OFF[j]:ST_OFF[j + 1]], AUX[:, BANK[N_SC + j], 0:SEQ - j * P],
                           DEC[:, 0:SEQ - j * P], ALU.mult).then_inc(s["aux_free"], 1)
                    for i in range(TT // 2):
                        dve.wait_ge(s["kv_high"], hh * 2 * TT + 2 * (i + 1))
                        for j in range(2 * i, 2 * i + 2):
                            stt(KDL[:, j, :], AUX[:, BANK[N_TK + i], (j % 2) * DK:(j % 2 + 1) * DK],
                                KDC[:, j:j + 1], KDH[:, j, :].bitcast(F32), ALU.mult, ALU.subtract
                                ).then_inc(s["kv_low"], 1)
                        dve.drain().then_inc(s["aux_free"], 1)
                    aux(N_VS)
                    ts(VS, AUX[0:NS, BANK[N_VS], :], 1.0, None, ALU.mult).then_inc(s["aux_free"], 1)

                    def v_low(j):
                        dve.wait_ge(s["kv_high"], hh * 2 * TT + (TT + j + 1))
                        tt(VL[:, j, :], AUX[:, BANK[N_TV + j], :], VH[:, j, :].bitcast(F32), ALU.subtract
                           ).then_inc(s["kv_low"], 1)
                        dve.drain().then_inc(s["aux_free"], 1)

                    v_low(0)
                    for j in range(TT):
                        dve.wait_ge(s["st_high"], hh * TT + (j + 1))
                        w = slice(ST_OFF[j], ST_OFF[j + 1])
                        tt(STL[:, w], STF[:, w], STH[:, w].bitcast(F32), ALU.subtract
                           ).then_inc(s["st_low"], 1)
                    for j in range(1, TT):
                        v_low(j)

                    def gate(e):
                        done(tb, g0 + TG[e])
                        tt(halves(SG[:, e, :]), pp(g0 + TG[e]), halves(RINV[:]), ALU.mult
                           ).then_inc(s["t_free"], 1)

                    def new_state(b):
                        r = b % SRING
                        dve.wait_ge(s_ld[r], hh * (16 * SUSES[r]) + 16 * (b // SRING + 1))
                        dve.wait_ge(s["t_mul"], hh * NS + (b + 1))
                        stt(SS[r], SS[r], KDC[:, TT:TT + 1], TS[b % 2], ALU.mult, ALU.add
                            ).then_inc(s["s_new"], 1)

                    def attended(e):
                        aux(N_AT + e)
                        ts(OF[:, e, 0:SEQ], AUX[:, BANK[N_AT + e], :], 1.0, None, ALU.mult
                           ).then_inc(s["aux_free"], 1)

                    def final_state(d):
                        aux(N_ST + d)
                        ts(SF[:, d, :], AUX[:, BANK[N_ST + d], :], 1.0, None, ALU.mult
                           ).then_inc(s["aux_free"], 1)

                    gate(0)
                    new_state(0)
                    gate(1)
                    new_state(1)
                    new_state(2)
                    gate(3)
                    new_state(3)
                    for e in range(VT):
                        attended(e)
                        new_state(VT + e)
                    dve.wait_ge(s["so_done"], hh * NS + NS)
                    ts(OF[:, :, SEQ:TOK], AUX[:, BANK_SO, 0:VT * NS].rearrange("p (e b) -> p e b", e=VT),
                       1.0, None, ALU.mult)
                    dve.drain()
                    dve.tensor_reduce(SUM, OF.rearrange("p e t -> p t e"), AX.X, ALU.add
                                      ).then_inc(s["gn_sum"], 1)
                    final_state(0)
                    done(tb, g0 + T_MEAN)
                    for e in range(VT):
                        m = stt(halves(OF[:, e, :]), pp(g0 + T_MEAN), -1.0 / DV, halves(OF[:, e, :]),
                                ALU.mult, ALU.add)
                        if e == VT // 2 - 1:
                            m.then_inc(s["centred"], 1)
                    m.then_inc(s["t_free"], 1)
                    dve.wait_ge(s["gn_sq"], hh * 2 + 2)
                    dve.tensor_reduce(SUM, SQ4.rearrange("p e t -> p t e"), AX.X, ALU.add
                                      ).then_inc(s["gn_sum"], 1)
                    gate(2)
                    final_state(1)
                    dve.wait_ge(s["silu_g"], hh * VT + VT)
                    tt(SG, SG, OF, ALU.mult)

                one_head(0, True)
                with dve.Fori(1, HEADS) as head:
                    one_head(head, False)
                dve.drain()
                ret_tail((layer + 1) * HEADS)

                def read_x(g, t, dst):
                    done(tb0, C_X[g][t])
                    tt(halves(dst), pp(C_X[g][t]), halves(RINV[:]), ALU.mult).then_inc(s["t_free"], 1)

                XR_EARLY = [XR, HF]

                def conv(g, t, then=None):
                    early = g == 0 and t < X_EARLY
                    xr = XR_EARLY[t] if early else XR
                    c = g * GT + t

                    def cw(j):
                        return CUR[:, PC_CW + c * CW + j:PC_CW + c * CW + j + 1]

                    dve.drain()
                    if not early:
                        read_x(g, t, XR)
                        dve.drain()
                        if then:
                            then()
                    ts(XCF[:, t, :], xr, cw(CW - 1), CUR[:, PC_CB + c:PC_CB + c + 1],
                       ALU.mult, ALU.add)
                    dve.tensor_copy(CVP[:, c, :], xr[:, SEQ - CW + 1:SEQ])
                    dve.tensor_copy(CVS[:, c, 0:CW - 2, :], SCV[:, c, 1:CW - 1, :])
                    dve.tensor_copy(CVS[:, c, CW - 2, :], xr[:, SEQ:TOK])
                    for j in range(CW - 1):
                        d = CW - 1 - j
                        dve.drain()
                        stt(XCF[:, t, d:SEQ], xr[:, 0:SEQ - d], cw(j), XCF[:, t, d:SEQ],
                            ALU.mult, ALU.add)
                        m = stt(XCF[:, t, SEQ:TOK], SCV[:, c, j, :], cw(j), XCF[:, t, SEQ:TOK],
                                ALU.mult, ALU.add)
                    m.then_inc(s["xc_full"], 1)

                def conv_low(g, t):
                    dve.drain()
                    dve.wait_ge(s["xc_high"], layer * LT + (g * GT + t + 1))
                    tt(XCL[:, t, :], XCF[:, t, :], XCH[:, t, :].bitcast(F32), ALU.subtract
                       ).then_inc(s["xc_low"], 1)

                lam = CUR[:, PC_SP:PC_SP + LT]

                def series(n):
                    tt(acc, acc, z2, ALU.mult)
                    dve.drain()
                    ts(acc, acc, 1.0 / n, None, ALU.add)
                    dve.drain()

                for r in range(SRING):
                    dve.wait_ge(s_st[r], (layer + 1) * (16 * SUSES[r] * HEADS) + 16)
                read_x(0, 0, XR_EARLY[0])
                og_split((layer + 1) * HEADS)
                read_x(0, 1, XR_EARLY[1])
                dve.wait_ge(s["sfin_st"], (layer + 1) * (16 * HEADS) + 16)
                dve.wait_ge(s["state_ld"], layer * 32 + 32)
                dve.wait_ge(s["small_st"], layer * 48 + 16)
                for m_ in range(MT):
                    ret_add(tb0, C_LRU - MT + X_EARLY, m_)
                    if m_ == 2:
                        conv(0, 0)
                    elif m_ == 5:
                        conv(0, 1)
                        conv_low(0, 0)
                    elif m_ == 0:
                        dve.wait_ge(s["lam_exp"], layer + 1)
                        ts(z_, e_, 2.0, None, ALU.add)
                        dve.memset(acc, 1.0 / 19)
                        dve.drain()
                        dve.reciprocal(z_, z_)
                        dve.drain()
                        tt(z_, z_, e_, ALU.mult)
                        dve.drain()
                        tt(z2, z_, z_, ALU.mult)
                        dve.drain()
                    else:
                        for n in {1: (17, 15, 13), 3: (11, 9), 4: (7,), 6: (5, 3), 7: (1,)}[m_]:
                            series(n)
                tt(acc, acc, z_, ALU.mult)
                ts(e_, lam, -8.0, 0.0, ALU.mult, ALU.max)
                dve.drain()
                stt(lam, acc, 16.0, e_, ALU.mult, ALU.add)

                def read_y(g, t):
                    dve.drain()
                    done(tb0, C_Y[g] + 3 * t)
                    tt(halves(YF[:, t % 2, :]), pp(C_Y[g] + 3 * t), halves(RINV[:]), ALU.mult
                       ).then_inc(s["t_free"], 1)

                def use_gates(g, t):
                    b, c = t % 2, g * GT + t
                    dve.wait_ge(s["gate_r"], layer * LT + (c + 1))
                    ts(LA[:, b, :], LA[:, b, :], CUR[:, PC_SP + c:PC_SP + c + 1], None, ALU.mult
                       ).then_inc(s["t_free"], 1)
                    dve.wait_ge(s["gate_i"], layer * LT + (c + 1))
                    tt(IX[:, b, :], IX[:, b, :], XCF[:, t, :], ALU.mult).then_inc(s["t_free"], 1)

                def one_less_a2(g, t):
                    b = t % 2
                    dve.drain()
                    dve.wait_ge(s["th_full"], layer * LT + (g * GT + t + 1))
                    tt(DF, AF[:, b, :], AF[:, b, :], ALU.mult)
                    dve.drain()
                    stt(DF, DF, 1.0, LA[:, b, :], ALU.add, ALU.mult).then_inc(s["d_full"], 1)

                def scan(g, t):
                    b, c = t % 2, g * GT + t
                    dve.drain()
                    tt(HF[:, SEQ:TOK], AF[:, b, SEQ:TOK], SLR[:, c, :], ALU.mult)
                    dve.wait_ge(s["w_sqrt"], layer * LT + (c + 1))
                    tt(IX[:, b, :], IX[:, b, :], DF, ALU.mult)
                    dve.drain()
                    dve.tensor_tensor_scan(HF[:, 0:SEQ], AF[:, b, 0:SEQ], IX[:, b, 0:SEQ], 0.0,
                                           ALU.mult, ALU.add)
                    tt(HF[:, SEQ:TOK], HF[:, SEQ:TOK], IX[:, b, SEQ:TOK], ALU.add)
                    dve.drain()
                    dve.tensor_copy(LRO[:, c, :], HF[:, SEQ - 1:TOK])
                    dve.wait_ge(s["y_gelu"], layer * LT + (c + 1))
                    tt(YF[:, b, :], YF[:, b, :], HF, ALU.mult).then_inc(s["gl_full"], 1)

                def gated_low(g, t):
                    dve.drain()
                    dve.wait_ge(s["gl_high"], layer * LT + (g * GT + t + 1))
                    tt(GLL[:, t, :], YF[:, t % 2, :], GLH[:, t, :].bitcast(F32), ALU.subtract
                       ).then_inc(s["gl_low"], 1)

                def y_gates(g, first=None):
                    for t in range(GT):
                        read_y(g, t)
                        if t:
                            scan(g, t - 1)
                        elif first:
                            first()
                        use_gates(g, t)
                        if t:
                            gated_low(g, t - 1)
                        one_less_a2(g, t)

                for t in range(X_EARLY, GT):
                    conv(0, t)
                    if t < GT - 1:
                        conv_low(0, t - 1)
                y_gates(0, lambda: (conv_low(0, GT - 2), conv_low(0, GT - 1)))
                conv(1, 0)
                scan(0, GT - 1)
                conv_low(1, 0)
                conv(1, 1)
                gated_low(0, GT - 1)
                for t in range(2, GT - 1):
                    conv(1, t)
                    conv_low(1, t - 1)

                def read_out(m_):
                    done(tb0, C_OUT + m_)
                    ts(halves(ACCL[:, m_, :]), pp(C_OUT + m_), 1.0, None, ALU.mult).then_inc(s["t_free"], 1)

                conv(1, GT - 1, lambda: read_out(0))
                read_out(1)
                conv_low(1, GT - 2)
                conv_low(1, GT - 1)
                for m_ in range(2, MT):
                    read_out(m_)
                y_gates(1)
                scan(1, GT - 1)
                gated_low(1, GT - 1)
                dve.drain().then_inc(s["small_rd"], 1)

                with dve.Fori(0, MT // 2) as i:
                    for j in range(2):
                        idx = C_MERGE + 3 * j
                        dve.drain()
                        for w in range(2):
                            dve.wait_ge(s["p_done"], tb0 + (idx + w + 1) + 6 * i)
                            tt(halves(ZM[:, 2 * j + w, :]), pp(idx + w), halves(RINV[:]), ALU.mult
                               ).then_inc(s["t_free"], 1)
                        lru = pair_row(ACCL, i, j)
                        dve.wait_ge(s["sg_m"], layer * (2 * MT) + (2 * j + 2) + 4 * i)
                        tt(ZM[:, 2 * j, :], ZM[:, 2 * j, :], pair_row(ACC, i, j), ALU.mult)
                        dve.wait_ge(s["p_done"], tb0 + (idx + 3) + 6 * i)
                        tt(halves(lru), pp(idx + 2), halves(lru), ALU.add).then_inc(s["t_free"], 1)
                        dve.drain()
                        tt(ZM[:, 2 * j + 1, :], ZM[:, 2 * j + 1, :], lru, ALU.mult)
                        dve.drain()
                        tt(MG, ZM[:, 2 * j, :], ZM[:, 2 * j + 1, :], ALU.add).then_inc(s["mg_full"], 1)
                        dve.wait_ge(s["mg_high"], layer * MT + (j + 1) + 2 * i)
                        tt(pair_row(ML, i, j), MG, pair_row(MH, i, j).bitcast(F32),
                           ALU.subtract).then_inc(s["mg_low"], 1)

                dve.drain()
                dve.memset(ACC[:], 0.0)

                def residual(tbi, idx, i, j, count, normed):
                    dve.wait_ge(s["p_done"], tbi + (idx + 1) + 2 * i)
                    xr = halves(pair_row(X, i, j))
                    m = tt(xr, pp(idx), xr, ALU.add)
                    m.then_inc(s["t_free"], 1)
                    if normed:
                        dve.drain().then_inc(s["x_full"], 1)
                        dve.wait_ge(s["x_high_s"], count + 2 * i)
                        x1, h1, l1 = (pair_row(v, i, j) for v in (X, XH, XL))
                        tt(SSQ, SSQ, SQT[:, j, :], ALU.add)
                        stt(l1, x1, GAIN2[:, j, bass.ds(i, 1)], h1.bitcast(F32), ALU.mult,
                            ALU.subtract).then_inc(s["x_low_s"], 1)
                        dve.drain()

                def next_norm(idx, n):
                    dve.drain()
                    dve.memset(SSQ, 0.0)
                    dve.tensor_copy(GAIN[:], NRM[:, bass.ds(layer * 2 + n, 1), :].rearrange("p a n -> p (a n)"))
                    dve.drain()

                next_norm(0, 1)
                with dve.Fori(0, MT // 2) as i:
                    for j in range(2):
                        residual(tb0, C_WO + j, i, j, nb + MT + j + 1, True)
                dve.wait_ge(s["x_sd"], layer * 2 + 2)
                root_inverse(RINV[:])

                for f in range(FH):
                    bt = C_FFN + f * T_FFN
                    fb = layer * (FH * FT) + f * FT
                    dve.drain()
                    with dve.Fori(0, FT) as i:
                        for j in range(2):
                            idx = bt + j
                            dve.wait_ge(s["p_done"], tb0 + (idx + 1) + 2 * i)
                            tt(halves(FG[:, j, :]), pp(idx), halves(RINV[:]), ALU.mult
                               ).then_inc(s["t_free"], 1)
                        dve.drain()
                        dve.wait_ge(s["f_silu"], fb + 1 + i)
                        tt(FF, FG[:, 0, :], FG[:, 1, :], ALU.mult).then_inc(s["f_full"], 1)
                        dve.wait_ge(s["f_high"], fb + 1 + i)
                        tt(AL[:, bass.ds(i, 1), :].rearrange("p a t -> p (a t)"), FF,
                           AH[:, bass.ds(i, 1), :].rearrange("p a t -> p (a t)").bitcast(F32),
                           ALU.subtract).then_inc(s["f_low"], 1)
                    if f == FH - 1:
                        next_norm(1, 2)
                    with dve.Fori(0, MT // 2) as i:
                        for j in range(2):
                            residual(tb0, bt + 2 * FT + j, i, j, nb + 2 * MT + j + 1, f == FH - 1)

            dve.wait_ge(s["x_sd"], 2 * DEPTH + 1)
            root_inverse(RINV[:])
            dve.drain()
            for m in range(MT):
                stt(ACC[:, m, :], X[:, m, :], GAIN[:, m:m + 1], RINV[:], ALU.mult, ALU.mult
                    ).then_inc(s["y_full"], 1)

        @block.scalar
        def _(act):
            copy, A = ACT.Copy, act.activation

            def apart():
                act.wait_ge(s["boot"], 1)

            for st in (*s_st, s["sfin_st"], s["small_st"]):
                act.sem_inc(st, 16)
            act.dma_start(PAR[:], params).then_inc(s["setup_ld"], 16)
            act.dma_start(NRM[:], norms).then_inc(s["setup_ld"], 16)
            act.dma_start(KDT[:], kdt).then_inc(s["setup_ld"], 16)
            act.dma_start(ID[:], ident).then_inc(s["setup_ld"], 16)
            for m in range(MT):
                act.dma_start(X[:, m, :], xt[:, m, :]).then_inc(x_ld[m], 16)
            act.wait_ge(s["boot"], 2)
            for m in range(MT):
                act.wait_ge(x_ld[m], 16)
                if m >= 2:
                    act.wait_ge(s["x_low_s"], m - 1)
                A(SQT[:, m % 2, :], X[:, m, :], ACT.Square)
                A(XH[:, m, :], X[:, m, :], copy, scale=GAIN[:, m:m + 1]).then_inc(s["x_high_s"], 1)
                act.drain()

            def norm_root(n):
                act.wait_ge(s["sq_mm"], n)
                A(halves(RINV[:]), AUX[:, 0:2, 0:HALF], ACT.Sqrt, bias=EPST, scale=1.0 / DM
                  ).then_inc(s["x_sd"], 1)

            with act.Fori(0, DEPTH) as layer:
                tb0 = layer * TILES + TILE0
                nb = layer * (2 * MT)
                act.dma_start(COS[:], tables[0]).then_inc(s["trig_ld"], 16)
                act.dma_start(SIN[:], tables[1]).then_inc(s["trig_ld"], 16)
                act.dma_start(SLR[:], slru[bass.ds(layer, 1)].rearrange("a p c b -> (a p) c b")
                              ).then_inc(s["state_ld"], 16)
                act.dma_start(SCV[:], sconv[bass.ds(layer, 1)].rearrange("a p c j b -> (a p) c j b")
                              ).then_inc(s["state_ld"], 16)

                norm_root(layer * 2 + 1)

                def ret_tail(hh, tb, var):
                    act.wait_ge(s["p_done"], tb + (var + 1))
                    A(halves(RSTD), pp(var), ACT.Sqrt, bias=EPST, scale=1.0 / DV
                      ).then_inc(s["gn_sd"], 1)
                    act.drain().then_inc(s["var_rd"], 1)
                    for e in range(VT):
                        act.wait_ge(s["og_full"], hh * VT + (e + 1 - VT))
                        A(OGH[:, e, :], SG[:, e, :], copy, scale=GNC[:, e:e + 1]).then_inc(s["og_high"], 1)

                def one_head(head, first):
                    hh = layer * HEADS + head
                    tb, v0 = (tb0, QK) if first else (tb0 - MT + head * T_HEAD, QK + MT)
                    g0 = v0 + VT

                    def state(dram, b):
                        return dram[bass.ds(layer, 1), b, bass.ds(head, 1)].rearrange(
                            "l h (d p) e -> p (l h d) e", p=P)

                    def load_state(b):
                        act.dma_start(SS[b % SRING], state(sret, b)).then_inc(s_ld[b % SRING], 16)

                    def load_vb(b):
                        act.dma_start(VB[:, b % VRING, :],
                                      vscr[b:b + 1, :].broadcast_to([P, DV])
                                      ).then_inc(v_ld[b % VRING], 16)

                    act.dma_start(DEC[:], dec[bass.ds(head, 1)].rearrange("a p n -> (a p) n")
                                  ).then_inc(s["dec_ld"], 16)
                    if not first:
                        ret_tail(hh, tb, -1)
                    for r in range(SRING):
                        act.wait_ge(s_st[r], hh * (16 * SUSES[r]) + 16)
                        load_state(r)
                    for n, (hi, full, scale) in enumerate(((QH, QF, 1.0), (KH, KF, DK ** -0.5))):
                        act.wait_ge(s["rope_done"], hh * 2 + (n + 1))
                        A(hi, full, copy, scale=scale).then_inc(s["qk_high"], 1)
                    for i in range(TT // 2):
                        act.wait_ge(s["aux_mm"], hh * AUX_USES + (N_TK + i + 1))
                        for j in range(2 * i, 2 * i + 2):
                            A(KDH[:, j, :], AUX[:, BANK[N_TK + i], (j % 2) * DK:(j % 2 + 1) * DK], copy,
                              scale=KDC[:, j:j + 1]).then_inc(s["kv_high"], 1)
                    act.wait_ge(s["aux_free"], hh * AUX_USES + (N_VS + 1))
                    act.dma_start(vscr[:, :], VS).then_inc(s["vs_st"], 16)

                    def v_high(j):
                        act.wait_ge(s["aux_mm"], hh * AUX_USES + (N_TV + j + 1))
                        A(VH[:, j, :], AUX[:, BANK[N_TV + j], :], copy).then_inc(s["kv_high"], 1)

                    v_high(0)
                    for j in range(TT):
                        w = slice(ST_OFF[j], ST_OFF[j + 1])
                        A(STH[:, w], STF[:, w], copy).then_inc(s["st_high"], 1)
                    act.wait_ge(s["vs_st"], hh * 16 + 16)
                    for b in range(VRING):
                        load_vb(b)
                    for j in range(1, TT):
                        v_high(j)

                    def silu(e):
                        act.wait_ge(s["t_free"], tb + (g0 + TG[e] + 1))
                        A(SG[:, e, :], SG[:, e, :], ACT.Silu).then_inc(s["silu_g"], 1)

                    for b in range(NS):
                        act.wait_ge(v_ld[b % VRING], hh * (16 * NS // VRING) + 16 * (b // VRING + 1))
                        if b >= 2:
                            act.wait_ge(s["s_new"], hh * NS + (b - 1))
                        A(TS[b % 2][:, 0, :], VB[:, b % VRING, :], copy, scale=KSC[:, 0, b:b + 1])
                        A(TS[b % 2][:, 1, :], VB[:, b % VRING, :], copy, scale=KSC[:, 1, b:b + 1]
                          ).then_inc(s["t_mul"], 1)
                        if b + VRING < NS:
                            act.wait_ge(s["t_mul"], hh * NS + (b + 1))
                            load_vb(b + VRING)
                        if SRING - 1 <= b < NS - 1:
                            n = b + 1 - SRING
                            act.wait_ge(s_st[n % SRING], hh * (16 * SUSES[n % SRING]) + 16 * (n // SRING + 2))
                            act.wait_ge(s["so_done"], hh * NS + (n + 1))
                            load_state(b + 1)
                        if b:
                            act.wait_ge(s["s_new"], hh * NS + b)
                            act.dma_start(state(ret_s, b - 1), SS[(b - 1) % SRING]
                                          ).then_inc(s_st[(b - 1) % SRING], 16)
                        if b in (1, 2, 3):
                            silu((0, 1, 3)[b - 1])
                    act.wait_ge(s["s_new"], hh * NS + NS)
                    act.dma_start(state(ret_s, NS - 1), SS[(NS - 1) % SRING]
                                  ).then_inc(s_st[(NS - 1) % SRING], 16)
                    half = VT // 2
                    act.wait_ge(s_st[SRING - 1], (hh + 1) * (16 * SUSES[SRING - 1]) + 16)
                    act.wait_ge(s["centred"], hh + 1)
                    A(SQ4[:, 0:half, :], OF[:, 0:half, :], ACT.Square).then_inc(s["gn_sq"], 1)
                    act.wait_ge(s["t_free"], tb + (g0 + T_MEAN + 1))
                    A(SQ4[:, half:VT, :], OF[:, half:VT, :], ACT.Square).then_inc(s["gn_sq"], 1)
                    silu(2)
                    act.wait_ge(s["aux_free"], hh * AUX_USES + (N_ST + KT))
                    act.dma_start(ret_p[bass.ds(layer, 1), bass.ds(head, 1)].rearrange(
                        "l h (d p) e -> p (l h d) e", p=P), SF).then_inc(s["sfin_st"], 16)

                one_head(0, True)
                with act.Fori(1, HEADS) as head:
                    one_head(head, False)
                ret_tail((layer + 1) * HEADS, tb0, C_LRU - MT - 1)
                A(e_, CUR[:, PC_SP:PC_SP + LT], ACT.Abs)
                act.drain()
                A(e_, e_, ACT.Exp, scale=-1.0).then_inc(s["lam_exp"], 1)

                def conv_high(g, t):
                    act.wait_ge(s["xc_full"], layer * LT + (g * GT + t + 1))
                    A(XCH[:, t, :], XCF[:, t, :], copy).then_inc(s["xc_high"], 1)

                def gated_high(g, t):
                    act.wait_ge(s["gl_full"], layer * LT + (g * GT + t + 1))
                    A(GLH[:, t, :], YF[:, t % 2, :], copy).then_inc(s["gl_high"], 1)

                def y_gates(g):
                    for t in range(GT):
                        b, c, idx = t % 2, g * GT + t, C_Y[g] + 3 * t
                        act.wait_ge(s["p_done"], tb0 + (idx + 2))
                        A(halves(LA[:, b, :]), pp(idx + 1), ACT.Sigmoid,
                          bias=CUR[:, PC_BA + c:PC_BA + c + 1]).then_inc(s["gate_r"], 1)
                        act.wait_ge(s["p_done"], tb0 + (idx + 3))
                        A(halves(IX[:, b, :]), pp(idx + 2), ACT.Sigmoid,
                          bias=CUR[:, PC_BX + c:PC_BX + c + 1]).then_inc(s["gate_i"], 1)
                        if t:
                            gated_high(g, t - 1)
                        act.wait_ge(s["t_free"], tb0 + (idx + 2))
                        A(AF[:, b, :], LA[:, b, :], ACT.Exp, scale=-1.0)
                        act.drain()
                        A(LA[:, b, :], LA[:, b, :], ACT.Tanh).then_inc(s["th_full"], 1)
                        A(YF[:, b, :], YF[:, b, :], ACT.Gelu_apprx_tanh).then_inc(s["y_gelu"], 1)
                        act.wait_ge(s["d_full"], layer * LT + (c + 1))
                        A(DF, DF, ACT.Sqrt).then_inc(s["w_sqrt"], 1)

                for t in range(GT):
                    conv_high(0, t)
                y_gates(0)
                conv_high(1, 0)
                gated_high(0, GT - 1)
                for t in range(1, GT):
                    conv_high(1, t)
                y_gates(1)
                gated_high(1, GT - 1)
                act.wait_ge(s["small_rd"], layer + 1)
                for dram, src in ((lru_o, LRO), (conv_p, CVP)):
                    act.dma_start(dram[bass.ds(layer, 1)].rearrange("a p c b -> (a p) c b"), src[:]
                                  ).then_inc(s["small_st"], 16)
                act.dma_start(conv_s[bass.ds(layer, 1)].rearrange("a p c j b -> (a p) c j b"), CVS[:]
                              ).then_inc(s["small_st"], 16)

                A(TOUCH, EPST, ACT.Sigmoid)
                with act.Fori(0, MT // 2) as i:
                    for j in range(2):
                        for w in range(2):
                            act.wait_ge(s["t_free"], tb0 + (C_MERGE + 3 * j + w + 1) + 6 * i)
                            apart()
                            A(ZM[:, 2 * j + w, :], ZM[:, 2 * j + w, :], ACT.Sigmoid,
                              bias=BG[:, w, j, bass.ds(i, 1)]).then_inc(s["sg_m"], 1)
                        act.wait_ge(s["mg_full"], layer * MT + (j + 1) + 2 * i)
                        apart()
                        A(pair_row(MH, i, j), MG, copy).then_inc(s["mg_high"], 1)

                def normed(full, high, i, j):
                    act.wait_ge(s["x_full"], full + 2 * i)
                    act.wait_ge(s["x_low_s"], high - 2 + 2 * i)
                    apart()
                    x1, h1 = pair_row(X, i, j), pair_row(XH, i, j)
                    A(SQT[:, j, :], x1, ACT.Square)
                    A(h1, x1, copy, scale=GAIN2[:, j, bass.ds(i, 1)]).then_inc(s["x_high_s"], 1)
                    act.drain()

                with act.Fori(0, MT // 2) as i:
                    for j in range(2):
                        normed(nb + j + 1, nb + MT + j + 1, i, j)
                norm_root(layer * 2 + 2)

                A(TOUCH, EPST, ACT.Silu)
                for f in range(FH):
                    bt = C_FFN + f * T_FFN
                    fb = layer * (FH * FT) + f * FT
                    with act.Fori(0, FT) as i:
                        act.wait_ge(s["t_free"], tb0 + (bt + 1) + 2 * i)
                        A(FG[:, 0, :], FG[:, 0, :], ACT.Silu).then_inc(s["f_silu"], 1)
                        act.wait_ge(s["f_full"], fb + 1 + i)
                        apart()
                        A(AH[:, bass.ds(i, 1), :].rearrange("p a t -> p (a t)"), FF, copy
                          ).then_inc(s["f_high"], 1)
                with act.Fori(0, MT // 2) as i:
                    for j in range(2):
                        normed(nb + MT + j + 1, nb + 2 * MT + j + 1, i, j)
            norm_root(2 * DEPTH + 1)

            for m in range(MT):
                act.wait_ge(s["y_full"], m + 1)
                act.dma_start(yt[:, m, :], ACC[:, m, :]).then_inc(s["y_st"], 16)
            act.wait_ge(s["y_st"], 16 * MT)
            act.wait_ge(s["small_st"], 48 * DEPTH + 16)
            act.wait_ge(s["sfin_st"], 16 * DEPTH * HEADS + 16)
            act.wait_ge(s["vs_st"], 16 * DEPTH * HEADS)
            for r in range(SRING):
                act.wait_ge(s_st[r], 16 * SUSES[r] * DEPTH * HEADS + 16)


def weight_units(np, w_in, w_ret_out, wa, wx, w_lru_out, w_o, w_gate_up, w_down):
    off = np.cumsum([0, HEADS * DK, HEADS * DK, HEADS * DV, HEADS * DV, LW, LW, DM])
    out = np.zeros((DEPTH * UNITS, P, UW), np.float32)
    n = 0

    def tile(w, col, rows, put=0):
        for i, r in enumerate(rows):
            out[n, :, (put + i) * P:(put + i + 1) * P] = w[r * P:(r + 1) * P, col:col + P]

    def spread(size, tiles):
        nonlocal n
        blocks = [(w, col, r) for w, col, rows in tiles for r in rows]
        for q, (w, col, r) in enumerate(blocks):
            tile(w, col, [r], q % size)
            if q % size == size - 1:
                n += 1
        assert len(blocks) % size == 0

    for l in range(DEPTH):
        def ret_out(h):
            nonlocal n
            for m in range(0, MT, 2):
                for j in range(2):
                    tile(w_ret_out[l], (m + j) * P, range(h * VT, (h + 1) * VT), j * VT)
                n += 1

        for h in range(HEADS):
            for part in range(3):
                if part == 0:
                    cols = [off[i] + h * DK + j * P for i in range(2) for j in range(KT)]
                elif part == 1:
                    cols = [off[2] + h * DV + j * P for j in range(VT)]
                    if h:
                        ret_out(h - 1)
                else:
                    cols = [off[3] + h * DV + UG.index(j) * P for j in range(VT)]
                for c in cols:
                    tile(w_in[l], c, range(MT))
                    n += 1
        wide = GT * P

        def x_branch(g, t0, t1):
            nonlocal n
            for t in range(t0, t1):
                tile(w_in[l], off[4] + g * wide + t * P, range(MT))
                n += 1

        def y_gates(g):
            gates = []
            for w in (wa, wx):
                full = np.zeros((wide, wide), np.float32)
                for b in range(NBLK // GROUPS):
                    full[b * BLK:(b + 1) * BLK, b * BLK:(b + 1) * BLK] = w[l, g * (NBLK // GROUPS) + b]
                gates.append(full)
            for t in range(GT):
                spread(YG_UNIT[t], [(w_in[l], off[5] + g * wide + t * P, range(MT))]
                       + [(full, t * P, BAND[t]) for full in gates])

        x_branch(0, 0, X_EARLY)
        ret_out(HEADS - 1)
        x_branch(0, X_EARLY, GT)
        y_gates(0)
        x_branch(1, 0, GT)
        for m in range(MT):
            tile(w_lru_out[l], m * P, range(GT))
            n += 1
        y_gates(1)
        for m in range(MT):
            spread(MG_UNIT, [(w_in[l], off[6 + j] + m * P, range(MT)) for j in range(2)]
                   + [(w_lru_out[l], m * P, range(GT, 2 * GT))])
        for m in range(MT):
            tile(w_o[l], m * P, range(MT))
            n += 1
        for f in range(FH):
            for t in range(FT):
                for j in range(2):
                    tile(w_gate_up[l], j * DFF + (f * FT + t) * P, range(MT))
                    n += 1
            for m in range(MT):
                tile(w_down[l], m * P, range(f * FT, f * FT + K_DOWN[0]))
                n += 1
                tile(w_down[l], m * P, range(f * FT + K_DOWN[0], (f + 1) * FT))
                n += 1
    assert n == DEPTH * UNITS
    return out.reshape(DEPTH, UNITS, P, UW)


def constants(np, past):
    f4 = np.float32
    half = DK // 2
    freqs = np.power(10000.0, -(np.arange(half, dtype=f4) / f4(half)).astype(np.float64)).astype(f4)
    pos = np.concatenate([np.arange(SEQ, dtype=f4), np.full(NS, past, f4)])
    ang = (freqs[:, None] * pos[None, :]).astype(f4).astype(np.float64)
    trig = np.stack([np.cos(ang), np.sin(ang)]).astype(f4)
    lg = np.log(1.0 - 2.0 ** (-5.0 - np.arange(HEADS)))
    diff = np.arange(SEQ)[None, :] - np.arange(P)[:, None]
    dec = np.where(diff >= 0, np.exp(lg[:, None, None] * np.maximum(diff, 0)), 0.0).astype(f4)
    kd = np.zeros((P, HEADS, TT + 1), f4)
    for h in range(HEADS):
        for j in range(TT):
            kd[:, h, j] = np.exp(lg[h] * (SEQ - 1 - j * P - np.arange(P))) * DK ** -0.5
        kd[:, h, TT] = np.exp(lg[h])
    return trig, dec, kd, np.eye(P, dtype=f4)


def kernel(x_prompt, x_sample, state_ret, state_lru, state_conv, w_in, norm_mix, gn_gain, w_ret_out,
           conv_w, conv_b, lru_wa, lru_ba, lru_wx, lru_bx, lru_lambda, w_lru_out, b_gate, w_o,
           norm_ffn, w_gate_up, w_down, norm_final):
    import numpy as np
    import concourse.bacc as bacc
    from concourse.bass_utils import run_bass_kernel_spmd

    arr = lambda a: np.asarray(a)
    x = np.concatenate([arr(x_prompt)[0], arr(x_sample)[:, 0]], 0)
    xt = np.ascontiguousarray(x.T.reshape(MT, P, TOK).transpose(1, 0, 2))

    def chan(a):
        a = arr(a)
        return np.moveaxis(a.reshape(a.shape[:-1] + (-1, P)), -1, -2)

    cw = chan(conv_w)
    params = np.concatenate([
        chan(gn_gain), cw.transpose(0, 2, 3, 1).reshape(DEPTH, P, LT * CW), chan(conv_b), chan(lru_ba),
        chan(lru_bx), chan(b_gate).transpose(0, 2, 1, 3).reshape(DEPTH, P, 2 * MT), chan(lru_lambda)], 2)
    params = np.ascontiguousarray(params.transpose(1, 0, 2))
    nm, nf = chan(norm_mix), chan(norm_ffn)
    norms = np.stack([nm[0], nf[0], nm[1], nf[1], chan(norm_final)], 1)
    slru = chan(state_lru).transpose(0, 2, 3, 1)
    sconv = chan(state_conv).transpose(0, 3, 4, 2, 1)
    trig, dec, kdt, ident = constants(np, 4096)
    ins = dict(
        wstream=weight_units(np, *(arr(a) for a in (w_in, w_ret_out, lru_wa, lru_wx, w_lru_out, w_o,
                                                    w_gate_up, w_down))),
        xt=xt, params=params, norms=norms, tables=trig, dec=dec, kdt=kdt, slru=slru, sconv=sconv,
        sret=arr(state_ret), ident=ident)
    outs = dict(yt=(P, MT, TOK), ret_p=(DEPTH, HEADS, DK, DV), ret_s=(DEPTH, NS, HEADS, DK, DV),
                lru_o=(DEPTH, P, LT, NS + 1), conv_p=(DEPTH, P, LT, CW - 1),
                conv_s=(DEPTH, P, LT, CW - 1, NS))

    nc = bacc.Bacc("TRN2", target_bir_lowering=False, num_devices=1)
    arrays, aps = {}, {}
    for name, a in ins.items():
        a = np.ascontiguousarray(a)
        arrays["in_" + name] = a
        aps[name] = nc.dram_tensor("in_" + name, a.shape, F32, kind="ExternalInput").ap()
    for name, shape in outs.items():
        aps[name] = nc.dram_tensor("out_" + name, shape, F32, kind="ExternalOutput").ap()
    aps["vscr"] = nc.dram_tensor("v_rows", (NS, DV), F32, kind="Internal").ap()
    build(nc, **aps)
    got = run_bass_kernel_spmd(nc, [arrays], core_ids=[0]).results[0]
    got = {name: got["out_" + name] for name in outs}

    y = got["yt"].transpose(1, 0, 2).reshape(DM, TOK).T
    lru = got["lru_o"].transpose(0, 3, 2, 1).reshape(DEPTH, NS + 1, LW)
    return (
        np.ascontiguousarray(y[:SEQ])[None], np.ascontiguousarray(y[SEQ:])[:, None],
        got["ret_p"][:, None], np.ascontiguousarray(lru[:, :1]),
        np.ascontiguousarray(got["conv_p"].transpose(0, 3, 2, 1).reshape(DEPTH, 1, CW - 1, LW)),
        got["ret_s"], np.ascontiguousarray(lru[:, 1:]),
        np.ascontiguousarray(got["conv_s"].transpose(0, 4, 3, 2, 1).reshape(DEPTH, NS, CW - 1, LW)),
    )
```
